# Optimizing a Trainium2 kernel written in Bass

```python
import math
import jax, jax.numpy as jnp
from jax import lax
import numpy as np

D_MODEL = 1024
BATCH = 1
SEQ = 256
DEPTH = 2

HEAD_DIM = 64
SB_HEADS = 4
NSA_HEADS = 8
NSA_GROUPS = 2
NSA_HPG = NSA_HEADS // NSA_GROUPS
NSA_BRANCHES = 3
MLA_HEADS = 4
MLA_NOPE = 64
MLA_ROPE = 32
MLA_V = 64
MLA_QK = MLA_NOPE + MLA_ROPE
MLA_Q_LORA = 256
MLA_KV_LORA = 128
ROPE_THETA = 10000.0
Q_BLOCK = 128
CMP_LEN = 32
CMP_STRIDE = 16
CMP_HIDDEN = 256
SEL_BLOCK = 64
SEL_TOPK = 16
N_LOCAL_BLOCKS = 2
WINDOW = 512
NUM_BUCKETS = 32
MAX_DISTANCE = 1024
N_MIXERS = 3
D_FF = 2816
N_EXPERTS = 8
TOP_K = 2
EXPERT_FF = 3584
N_DENSE_LAYERS = (DEPTH + 1) // 2
N_MOE_LAYERS = DEPTH // 2
EPS = 1e-6
NEG_INF = -1e30
FORCE = 1e30

SB_W = SB_HEADS * HEAD_DIM
NSA_QW = NSA_HEADS * HEAD_DIM
NSA_KVW = NSA_GROUPS * HEAD_DIM
IN_SPLITS = (SB_W, SB_W, SB_W,
             NSA_QW, NSA_KVW, NSA_KVW, NSA_KVW, NSA_KVW, NSA_KVW, NSA_KVW, NSA_HEADS * NSA_BRANCHES,
             MLA_Q_LORA, MLA_KV_LORA, MLA_ROPE,
             N_MIXERS * D_MODEL)
IN_COLS = sum(IN_SPLITS)

kernel_name = 'hybrid_stickbreak_nsa_mla_moe'

def rmsnorm(x, g):
    xf = x.astype(jnp.float32)
    y = xf * lax.rsqrt(jnp.mean(xf * xf, axis=-1, keepdims=True) + EPS)
    return (y * g.astype(jnp.float32)).astype(x.dtype)

def masked_softmax(s, mask):
    p = jax.nn.softmax(jnp.where(mask, s, NEG_INF), axis=-1)
    return jnp.where(mask, p, 0.0)

def t5_bucket(rel):
    n = jnp.maximum(rel, 0)
    max_exact = NUM_BUCKETS // 2
    nf = jnp.maximum(n, 1).astype(jnp.float32)
    large = max_exact + (jnp.log(nf / max_exact) / math.log(MAX_DISTANCE / max_exact)
                         * (NUM_BUCKETS - max_exact)).astype(jnp.int32)
    large = jnp.minimum(large, NUM_BUCKETS - 1)
    return jnp.where(n < max_exact, n, large)

def apply_rope(x, pos):
    half = x.shape[-1] // 2
    inv = ROPE_THETA ** (-jnp.arange(half, dtype=jnp.float32) / half)
    ang = pos.astype(jnp.float32)[:, None] * inv[None, :]
    cos = jnp.cos(ang)[None, :, None, :]
    sin = jnp.sin(ang)[None, :, None, :]
    xf = x.astype(jnp.float32)
    x1, x2 = xf[..., :half], xf[..., half:]
    return jnp.concatenate([x1 * cos - x2 * sin, x2 * cos + x1 * sin], axis=-1).astype(x.dtype)

def stick_breaking_attention(q, k, v):
    B, S, H, D = q.shape
    scale = D ** -0.5
    kpos = jnp.arange(S)

    def block(i):
        start = i * Q_BLOCK
        qb = lax.dynamic_slice_in_dim(q, start, Q_BLOCK, axis=1)
        z = jnp.einsum('bqhd,bkhd->bhqk', qb, k).astype(jnp.float32) * scale
        qpos = start + jnp.arange(Q_BLOCK)
        causal = kpos[None, :] < qpos[:, None]
        log_stay = jnp.where(causal, jax.nn.log_sigmoid(-z), 0.0)
        after = lax.cumsum(log_stay, axis=3, reverse=True) - log_stay
        w = jnp.where(causal, jnp.exp(jax.nn.log_sigmoid(z) + after), 0.0)
        return jnp.einsum('bhqk,bkhd->bqhd', w.astype(v.dtype), v)

    out = lax.map(block, jnp.arange(S // Q_BLOCK))
    return out.transpose(1, 0, 2, 3, 4).reshape(B, S, H * D)

def causal_softmax_attention(q, k, v, scale):
    B, S, H, _ = q.shape
    Dv = v.shape[-1]
    kpos = jnp.arange(S)

    def block(i):
        start = i * Q_BLOCK
        qb = lax.dynamic_slice_in_dim(q, start, Q_BLOCK, axis=1)
        s = jnp.einsum('bqhd,bkhd->bhqk', qb, k).astype(jnp.float32) * scale
        qpos = start + jnp.arange(Q_BLOCK)
        mask = kpos[None, :] <= qpos[:, None]
        p = jax.nn.softmax(jnp.where(mask, s, NEG_INF), axis=-1)
        return jnp.einsum('bhqk,bkhd->bqhd', p.astype(v.dtype), v)

    out = lax.map(block, jnp.arange(S // Q_BLOCK))
    return out.transpose(1, 0, 2, 3, 4).reshape(B, S, H * Dv)

def compress_blocks(x, pos_emb, w1, w2):
    B, S, G, Dh = x.shape
    n_chunk = S // CMP_STRIDE
    r = CMP_LEN // CMP_STRIDE
    n_cmp = n_chunk - r + 1
    chunks = x.reshape(B, n_chunk, CMP_STRIDE, G, Dh)
    blocks = jnp.concatenate([chunks[:, j:j + n_cmp] for j in range(r)], axis=2)
    blocks = blocks + pos_emb[:, None, :]
    flat = blocks.transpose(0, 1, 3, 2, 4).reshape(B, n_cmp, G, CMP_LEN * Dh)
    return jax.nn.silu(flat @ w1) @ w2

def native_sparse_attention(q, k_cmp_in, v_cmp_in, k_sel, v_sel, k_win, v_win, gate_logits,
                            q_norm, k_norms, cmp_pos, cmp_w1, cmp_w2, bias_table):
    B, S, H, Dh = q.shape
    G, R = NSA_GROUPS, NSA_HPG
    scale = Dh ** -0.5
    q = rmsnorm(q, q_norm)
    k_cmp = rmsnorm(compress_blocks(k_cmp_in, cmp_pos[0], cmp_w1[0], cmp_w2[0]), k_norms[0])
    v_cmp = compress_blocks(v_cmp_in, cmp_pos[1], cmp_w1[1], cmp_w2[1])
    k_sel = rmsnorm(k_sel, k_norms[1])
    k_win = rmsnorm(k_win, k_norms[2])
    gates = jax.nn.sigmoid(gate_logits.astype(jnp.float32)).astype(q.dtype).reshape(B, S, G, R, NSA_BRANCHES)

    n_chunk = S // CMP_STRIDE
    r_c = CMP_LEN // CMP_STRIDE
    r_s = SEL_BLOCK // CMP_STRIDE
    n_cmp = n_chunk - r_c + 1
    cmp_end = jnp.arange(n_cmp) * CMP_STRIDE + CMP_LEN - 1
    n_blk = S // SEL_BLOCK
    n_sel = min(SEL_TOPK, n_blk)
    n_keys_sel = n_sel * SEL_BLOCK
    blk_ids = jnp.arange(n_blk)
    ks_blocks = k_sel.reshape(B, n_blk, SEL_BLOCK, G, Dh).transpose(0, 3, 1, 2, 4)
    vs_blocks = v_sel.reshape(B, n_blk, SEL_BLOCK, G, Dh).transpose(0, 3, 1, 2, 4)
    pad = ((0, 0), (WINDOW, 0), (0, 0), (0, 0))
    kw_pad = jnp.pad(k_win, pad)
    vw_pad = jnp.pad(v_win, pad)
    table = bias_table.reshape(NUM_BUCKETS, G, R)
    table_g = table.transpose(1, 0, 2)
    b_ix = jnp.arange(B)[:, None, None, None]
    g_ix = jnp.arange(G)[None, :, None, None]

    def block(i):
        start = i * Q_BLOCK
        qpos = start + jnp.arange(Q_BLOCK)
        qb = lax.dynamic_slice_in_dim(q, start, Q_BLOCK, axis=1).reshape(B, Q_BLOCK, G, R, Dh)
        rel_c = qpos[:, None] - cmp_end[None, :]
        bias_c = table[t5_bucket(rel_c)].transpose(2, 3, 0, 1)
        s_c = jnp.einsum('bqgrd,bngd->bgrqn', qb, k_cmp).astype(jnp.float32) * scale + bias_c
        p_c = masked_softmax(s_c, rel_c >= 0)
        o_c = jnp.einsum('bgrqn,bngd->bqgrd', p_c.astype(v_cmp.dtype), v_cmp)
        imp = jnp.pad(p_c.sum(axis=2), ((0, 0), (0, 0), (0, 0), (r_c - 1, r_c - 1)))
        imp_blk = imp[..., 0:r_s * n_blk:r_s]
        for m in range(1, r_s + r_c - 1):
            imp_blk = imp_blk + imp[..., m:m + r_s * n_blk:r_s]
        qblk = qpos // SEL_BLOCK
        causal_b = blk_ids[None, :] * SEL_BLOCK <= qpos[:, None]
        dist_b = qblk[:, None] - blk_ids[None, :]
        forced = (blk_ids[None, :] == 0) | ((dist_b >= 0) & (dist_b < N_LOCAL_BLOCKS))
        score = jnp.where(causal_b, jnp.where(forced, FORCE, imp_blk), NEG_INF)
        top_val, top_idx = lax.top_k(score, n_sel)
        sel_ok = top_val > 0.5 * NEG_INF
        kg = ks_blocks[b_ix, g_ix, top_idx]
        vg = vs_blocks[b_ix, g_ix, top_idx]
        tok = top_idx[..., None] * SEL_BLOCK + jnp.arange(SEL_BLOCK)
        rel_s = qpos[None, None, :, None, None] - tok
        mask_s = (sel_ok[..., None] & (rel_s >= 0)).reshape(B, G, 1, Q_BLOCK, n_keys_sel)
        bias_s = table_g[g_ix[..., None], t5_bucket(rel_s)]
        s_s = (jnp.einsum('bqgrd,bgqnld->bgrqnl', qb, kg).astype(jnp.float32) * scale
               + bias_s.transpose(0, 1, 5, 2, 3, 4)).reshape(B, G, R, Q_BLOCK, n_keys_sel)
        p_s = masked_softmax(s_s, mask_s)
        o_s = jnp.einsum('bgrqk,bgqkd->bqgrd', p_s.astype(vg.dtype),
                         vg.reshape(B, G, Q_BLOCK, n_keys_sel, Dh))
        kwb = lax.dynamic_slice_in_dim(kw_pad, start, WINDOW + Q_BLOCK, axis=1)
        vwb = lax.dynamic_slice_in_dim(vw_pad, start, WINDOW + Q_BLOCK, axis=1)
        kpos_w = start - WINDOW + jnp.arange(WINDOW + Q_BLOCK)
        rel_w = qpos[:, None] - kpos_w[None, :]
        mask_w = (rel_w >= 0) & (rel_w < WINDOW) & (kpos_w[None, :] >= 0)
        bias_w = table[t5_bucket(rel_w)].transpose(2, 3, 0, 1)
        s_w = jnp.einsum('bqgrd,bkgd->bgrqk', qb, kwb).astype(jnp.float32) * scale + bias_w
        p_w = masked_softmax(s_w, mask_w)
        o_w = jnp.einsum('bgrqk,bkgd->bqgrd', p_w.astype(vwb.dtype), vwb)
        gb = lax.dynamic_slice_in_dim(gates, start, Q_BLOCK, axis=1)
        o = gb[..., 0:1] * o_c + gb[..., 1:2] * o_s + gb[..., 2:3] * o_w
        return o.reshape(B, Q_BLOCK, H * Dh)

    out = lax.map(block, jnp.arange(S // Q_BLOCK))
    return out.transpose(1, 0, 2, 3).reshape(B, S, H * Dh)

def multi_head_latent_attention(c_q, c_kv, k_rope, q_a_norm, kv_a_norm, w_uq, w_ukv, q_norm, k_norm):
    B, S, _ = c_q.shape
    H = MLA_HEADS
    q = (rmsnorm(c_q, q_a_norm) @ w_uq).reshape(B, S, H, MLA_QK)
    kv = (rmsnorm(c_kv, kv_a_norm) @ w_ukv).reshape(B, S, H, MLA_NOPE + MLA_V)
    k = jnp.concatenate([kv[..., :MLA_NOPE],
                         jnp.broadcast_to(k_rope[:, :, None, :], (B, S, H, MLA_ROPE))], axis=-1)
    v = kv[..., MLA_NOPE:]
    q = rmsnorm(q, q_norm)
    k = rmsnorm(k, k_norm)
    pos = jnp.arange(S)
    q = jnp.concatenate([q[..., :MLA_NOPE], apply_rope(q[..., MLA_NOPE:], pos)], axis=-1)
    k = jnp.concatenate([k[..., :MLA_NOPE], apply_rope(k[..., MLA_NOPE:], pos)], axis=-1)
    return causal_softmax_attention(q, k, v, MLA_QK ** -0.5)

def swiglu(h, w_gate, w_up, w_down):
    return (jax.nn.silu(h @ w_gate) * (h @ w_up)) @ w_down

def moe_swiglu(h, w_router, w_gate, w_up, w_down):
    logits = (h @ w_router).astype(jnp.float32)
    top_val, top_idx = lax.top_k(logits, TOP_K)
    weights = jax.nn.softmax(top_val, axis=-1)
    combine = jnp.sum(jax.nn.one_hot(top_idx, N_EXPERTS, dtype=jnp.float32) * weights[..., None],
                      axis=-2).astype(h.dtype)
    y = jnp.zeros_like(h)
    for e in range(N_EXPERTS):
        y = y + combine[..., e:e + 1] * swiglu(h, w_gate[e], w_up[e], w_down[e])
    return y

def setup_inputs(seed: int = 0) -> dict:
    key = jax.random.key(seed)
    keys = iter(jax.random.split(key, 48))

    def w(shape, fan_in):
        return jax.random.normal(next(keys), shape, jnp.float32) * (fan_in ** -0.5)

    def gain(shape):
        return 1.0 + 0.02 * jax.random.normal(next(keys), shape, jnp.float32)

    def small(shape, scale):
        return scale * jax.random.normal(next(keys), shape, jnp.float32)

    L, ND, NM = DEPTH, N_DENSE_LAYERS, N_MOE_LAYERS
    return {
        'x': small((BATCH, SEQ, D_MODEL), 1.0),
        'rel_bias_table': small((NUM_BUCKETS, NSA_HEADS), 0.5),
        'mix_norm': gain((L, D_MODEL)),
        'w_in': w((L, D_MODEL, IN_COLS), D_MODEL),
        'b_gate': small((L, N_MIXERS * D_MODEL), 0.01),
        'sb_w_o': w((L, SB_W, D_MODEL), SB_W),
        'nsa_q_norm': gain((L, HEAD_DIM)),
        'nsa_k_norm': gain((L, NSA_BRANCHES, HEAD_DIM)),
        'nsa_cmp_pos': small((L, 2, CMP_LEN, HEAD_DIM), 0.1),
        'nsa_cmp_w1': w((L, 2, CMP_LEN * HEAD_DIM, CMP_HIDDEN), CMP_LEN * HEAD_DIM),
        'nsa_cmp_w2': w((L, 2, CMP_HIDDEN, HEAD_DIM), CMP_HIDDEN),
        'nsa_w_o': w((L, NSA_QW, D_MODEL), NSA_QW),
        'mla_q_a_norm': gain((L, MLA_Q_LORA)),
        'mla_kv_a_norm': gain((L, MLA_KV_LORA)),
        'mla_w_uq': w((L, MLA_Q_LORA, MLA_HEADS * MLA_QK), MLA_Q_LORA),
        'mla_w_ukv': w((L, MLA_KV_LORA, MLA_HEADS * (MLA_NOPE + MLA_V)), MLA_KV_LORA),
        'mla_q_norm': gain((L, MLA_QK)),
        'mla_k_norm': gain((L, MLA_QK)),
        'mla_w_o': w((L, MLA_HEADS * MLA_V, D_MODEL), MLA_HEADS * MLA_V),
        'w_out': w((L, D_MODEL, D_MODEL), D_MODEL),
        'ffn_norm': gain((L, D_MODEL)),
        'dense_w_gate': w((ND, D_MODEL, D_FF), D_MODEL),
        'dense_w_up': w((ND, D_MODEL, D_FF), D_MODEL),
        'dense_w_down': w((ND, D_FF, D_MODEL), D_FF),
        'moe_router': w((NM, D_MODEL, N_EXPERTS), D_MODEL),
        'moe_w_gate': w((NM, N_EXPERTS, D_MODEL, EXPERT_FF), D_MODEL),
        'moe_w_up': w((NM, N_EXPERTS, D_MODEL, EXPERT_FF), D_MODEL),
        'moe_w_down': w((NM, N_EXPERTS, EXPERT_FF, D_MODEL), EXPERT_FF),
    }

def reference(x, rel_bias_table, mix_norm, w_in, b_gate, sb_w_o, nsa_q_norm, nsa_k_norm,
              nsa_cmp_pos, nsa_cmp_w1, nsa_cmp_w2, nsa_w_o, mla_q_a_norm, mla_kv_a_norm,
              mla_w_uq, mla_w_ukv, mla_q_norm, mla_k_norm, mla_w_o, w_out, ffn_norm,
              dense_w_gate, dense_w_up, dense_w_down, moe_router, moe_w_gate, moe_w_up, moe_w_down):
    B, S, D = x.shape
    split_points = [int(p) for p in np.cumsum(IN_SPLITS)[:-1]]
    for layer in range(DEPTH):
        h = rmsnorm(x, mix_norm[layer])
        proj = h @ w_in[layer]
        (sb_q, sb_k, sb_v, n_q, n_kc, n_vc, n_ks, n_vs, n_kw, n_vw, n_g,
         m_cq, m_ckv, m_kr, gate_logits) = jnp.split(proj, split_points, axis=-1)
        y_sb = stick_breaking_attention(sb_q.reshape(B, S, SB_HEADS, HEAD_DIM),
                                        sb_k.reshape(B, S, SB_HEADS, HEAD_DIM),
                                        sb_v.reshape(B, S, SB_HEADS, HEAD_DIM)) @ sb_w_o[layer]
        kv_shape = (B, S, NSA_GROUPS, HEAD_DIM)
        y_nsa = native_sparse_attention(
            n_q.reshape(B, S, NSA_HEADS, HEAD_DIM),
            n_kc.reshape(kv_shape), n_vc.reshape(kv_shape),
            n_ks.reshape(kv_shape), n_vs.reshape(kv_shape),
            n_kw.reshape(kv_shape), n_vw.reshape(kv_shape), n_g,
            nsa_q_norm[layer], nsa_k_norm[layer], nsa_cmp_pos[layer],
            nsa_cmp_w1[layer], nsa_cmp_w2[layer], rel_bias_table) @ nsa_w_o[layer]
        y_mla = multi_head_latent_attention(
            m_cq, m_ckv, m_kr, mla_q_a_norm[layer], mla_kv_a_norm[layer],
            mla_w_uq[layer], mla_w_ukv[layer], mla_q_norm[layer], mla_k_norm[layer]) @ mla_w_o[layer]
        g = jax.nn.sigmoid((gate_logits + b_gate[layer]).astype(jnp.float32)).astype(x.dtype)
        g = g.reshape(B, S, N_MIXERS, D)
        merged = g[:, :, 0] * y_sb + g[:, :, 1] * y_nsa + g[:, :, 2] * y_mla
        x = x + merged @ w_out[layer]
        h = rmsnorm(x, ffn_norm[layer])
        if layer % 2 == 0:
            j = layer // 2
            x = x + swiglu(h, dense_w_gate[j], dense_w_up[j], dense_w_down[j])
        else:
            j = layer // 2
            x = x + moe_swiglu(h, moe_router[j], moe_w_gate[j], moe_w_up[j], moe_w_down[j])
    return x


_drawn_inputs = setup_inputs


def setup_inputs(seed=0):
    import zlib

    import numpy as np

    out = dict(_drawn_inputs(seed))
    spreads = {}
    factors = {'b_gate': 8.0,
     'nsa_q_norm': 3.544,
     'nsa_k_norm': 8.0,
     'mla_q_a_norm': 8.0,
     'mla_kv_a_norm': 8.0,
     'mla_q_norm': 8.0,
     'mla_k_norm': 8.0}
    for name, (base, spread) in spreads.items():
        noise = np.random.default_rng([zlib.crc32(name.encode()), seed]).standard_normal(out[name].shape)
        drawn = base * np.exp(spread * noise) if base else spread * noise
        out[name] = __import__('jax').numpy.asarray(drawn.astype(out[name].dtype))
    for name, factor in factors.items():
        out[name] = (out[name] * factor).astype(out[name].dtype)
    return out
```

```python
from contextlib import ExitStack

import concourse.bass as bass
from concourse import mybir

ALU = mybir.AluOpType
ACT = mybir.ActivationFunctionType
F32 = mybir.dt.float32
U32 = mybir.dt.uint32
I32 = mybir.dt.int32
AX = mybir.AxisListType

P = 128
SEQ, D = 256, 1024
NT = SEQ // P
KD = D // P
DEPTH = 2
HD = 64
EPS = 1e-6
NEG = -1e30

SBQ, SBK, SBV = 0, 256, 512
NQ, KC, VC, KS, VS, KW, VW, NG = 768, 1280, 1408, 1536, 1664, 1792, 1920, 2048
CQ, CKV, KR, GATES = 2072, 2328, 2456, 2488
IN_COLS = 5560
CHUNKS = [(c, min(512, GATES - c)) for c in range(0, GATES, 512)] + [(c, 512) for c in range(GATES, IN_COLS, 512)]
N_MIX_CHUNKS = 5

N_CMP = 15
MQ = 96
FF_DENSE, FF_EXPERT, N_EXPERTS = 2816, 3584, 8
EXPERT_UNITS = FF_EXPERT // 512
DENSE_GROUPS = [(f, min(512, FF_DENSE - f)) for f in range(0, FF_DENSE, 512)]
DENSE_UNITS = NT * len(DENSE_GROUPS)

SLOT = 4096
RING = 4
MOE_RING = 7

JOBS = ([("mla", i, hp) for i in range(NT) for hp in range(2)]
        + [(kind, i, r) for i in range(NT) for r in range(4) for kind in ("sel", "win")])
FIRST_SPARSE = {i: JOBS.index(("sel", i, 0)) for i in range(NT)}
LAG_TURN, LAG_PV = 2, 3
STEPS = len(JOBS) + LAG_PV
LATE_GATES = {2 + 3 * n: (8 + n // 2, n % 2) for n in range(6)}


def pool_plan(order, banks):
    assert len(set(order)) == len(order)
    return {key: (banks[k % len(banks)], k // len(banks)) for k, key in enumerate(order)}


def bank_uses():
    turn, proj, score, outp = [], [], [], []
    for L in range(DEPTH):
        turn += [(L, "norm1", t, h) for t in range(NT) for h in range(2)]
        turn += [(L, "xt", t, b) for t in range(NT) for b in range(4)]
        turn += [(L, "kct")]
        turn += [(L, "mt", t, b) for t in range(NT) for b in range(2)]
        for j, (kind, i, r) in enumerate(JOBS):
            if j == FIRST_SPARSE[i]:
                turn += [(L, "pc", i, h) for h in range(2)]
            turn += [(L, "p", j)]
        turn += [(L, "merge", t, h) for t in range(NT) for h in range(2)]
        turn += [(L, "norm2", t, h) for t in range(NT) for h in range(2)]
        proj += [(L, "proj", c, t) for c in range(7) for t in range(NT)]
        proj += [(L, w, t) for t in range(NT) for w in ("uq", "ukv")]
        proj += [(L, "c1"), (L, "c2")]
        proj += [(L, "proj", 7, t) for t in range(NT)]
        proj += [(L, "proj", *LATE_GATES[s]) for s in sorted(LATE_GATES)]
        proj += [(L, "y", t, h, m) for t in range(NT) for h in range(2) for m in range(3)]
        proj += [(L, "out", t, h) for t in range(NT) for h in range(2)]
        score += [(L, "z", h) for h in range(4)] + [(L, "S", h) for h in range(4)]
        score += [(L, "sc", i) for i in range(NT)] + [(L, "s", j) for j in range(len(JOBS))]
        if L == 0:
            outp += [(L, "flip", h) for h in range(8)]
        outp += [(L, "sbo", hp) for hp in range(2)] + [(L, "mlao", i, hp) for i in range(NT) for hp in range(2)]
        outp += [(L, "nsao", i, r) for i in range(NT) for r in range(4)]
    plan = {}
    for order, banks in ((turn, (0, 1)), (proj, (2, 3)), (score, (4, 5)), (outp, (6, 7))):
        plan.update(pool_plan(order, banks))
    return plan


def weight_chunks():
    seq = []
    for L in range(DEPTH):
        seq += [(L, "in", c) for c in range(7)] + [(L, "small"), (L, "w1", 0), (L, "w1", 1)]
        seq += [(L, "in", c) for c in range(7, 11)] + [(L, "wo", 0), (L, "wo", 1), (L, "wout", 0), (L, "wout", 1)]
        if L == 0:
            for g in range(len(DENSE_GROUPS)):
                seq += [(L, "gate", g), (L, "up", g), (L, "down", g)]
    return seq


EXPERT_CHUNKS = [("gate", 0), ("up", 0)]
for _u in range(1, EXPERT_UNITS):
    EXPERT_CHUNKS += [("gate", _u), ("up", _u), ("down", _u - 1)]
EXPERT_CHUNKS += [("down", EXPERT_UNITS - 1)]
assert len(EXPERT_CHUNKS) % MOE_RING == 0

G_MIX, G_FFN, G_LAYER = 0, DEPTH * KD, 2 * DEPTH * KD
G_Q, G_KCMP, G_KSEL, G_KWIN, G_QA, G_KVA, G_PER_LAYER = 0, 1, 2, 3, 4, 6, 7
G_ROWS = G_LAYER + DEPTH * G_PER_LAYER
SMALL_IN = 16 * (9 + 8 * DEPTH)


def trunk(nc, a, out):
    uses = bank_uses()
    chunk_seq = weight_chunks()
    chunk_no = {key: n for n, key in enumerate(chunk_seq)}

    with ExitStack() as ctx:
        def sb(name, shape, dt=F32):
            return ctx.enter_context(nc.sbuf_tensor(name, shape, dt))

        def sem(name):
            return ctx.enter_context(nc.semaphore(name))

        ps = ctx.enter_context(nc.psum_tensor("ps", [P, 8, 512], F32))

        arena = sb("arena", [P, MOE_RING * SLOT + 1904])
        PROJ0 = RING * SLOT
        proj = arena[:, PROJ0:PROJ0 + NT * IN_COLS].rearrange("p (t n) -> p t n", t=NT)
        bias = arena[:, PROJ0 + NT * IN_COLS:PROJ0 + NT * IN_COLS + 8 * 384].rearrange("p (h k) -> p h k", h=8)
        x = sb("x", [P, NT, D])
        xn = sb("xn", [P, NT, D])
        hT = sb("hT", [P, KD, SEQ])
        xT = sb("xT", [P, 13, SEQ])
        cmp_x = sb("cmp_x", [P, 2, 3, P])
        mqk = sb("mqk", [P, NT, 8, MQ])
        probs = mqk[:, :, :, :].rearrange("p t h d -> p (t h d)").rearrange("p (b n) -> p b n", b=3)
        mv = sb("mv", [P, NT, 4, HD])
        mT = sb("mT", [P, 8, SEQ])
        tmp = sb("tmp", [P, 1536])
        probsT = sb("probsT", [P, 2, 512])
        pcs = cmp_x[:, 0, 0:2, :].rearrange("p g (h n) -> p g h n", h=8)
        pcT = sb("pcT", [P, 8, P])
        yT = sb("yT", [P, 8, SEQ])
        ident = sb("ident", [P, P])
        tri_ge = sb("tri_ge", [P, P])
        ones = sb("ones", [P, P])
        stick_mask = sb("stick_mask", [P, 384])
        causal = sb("causal", [P, SEQ])
        gain_rows = pcT[:, 0, :]
        pos_rows = pcT[0:64, 1, :]
        rope_tmp = pcT[:, 0:4, :]
        flip = pcT[:, 4, :]
        gains = sb("gains", [P, 64])
        posT = sb("posT", [P, 4, 16])
        mla_gain = sb("mla_gain", [P, DEPTH, 2, MQ])
        trig = sb("trig", [P, 2, NT, 16])
        bgate = sb("bgate", [12, 512])
        router = sb("router", [P, KD, N_EXPERTS])
        table = sb("table", [64, 8])
        sums = sb("sums", [P, NT, 20])
        inv_n = sb("inv_n", [P, 20])
        mhalf = sb("mhalf", [P, 20])
        ssum = sb("ssum", [P, NT])
        msum = sb("msum", [P, NT, 8])
        ksum = sb("ksum", [P, 2])
        nmax = sb("nmax", [P, 3, 2])
        prob_sum = sb("prob_sum", [P, 3, 2])
        prec = sb("prob_scale", [P, 3, 2])
        ngate = sb("ngate", [P, NT, 24])
        cmax = sb("cmax", [P, 8])
        csum = sb("csum", [P, 8])
        valid = sb("valid", [P, NT])
        early = yT[:, :, :].rearrange("p a b -> p (a b)")
        ch_raw, ch, ce = (early[:, o:o + 4 * n].rearrange("p (f n) -> p f n", f=4) for o, n in ((0, 45), (180, 30), (300, 30)))
        ckv_c = cmp_x[0:16, 1, 0:2, :].rearrange("p g (f d) -> p (g f) d", f=2)
        csq = early[0:16, 512:640].rearrange("p (g d) -> p g d", g=2)
        kcT = sb("kcT", [P, 2, 16])
        NS = 2 * N_EXPERTS + 1
        slots, comb = (early[:, o:o + NT * NS].rearrange("p (t e) -> p t e", t=NT) for o in (0, 64))
        route = early[:, 128:320].rearrange("p (v t e) -> p v t e", v=12, t=NT)
        top_i = sb("top_i", [P, NT, 8], U32)
        flag = sb("flag", [P, 2])
        flag_i = sb("flag_i", [P, 1], I32)
        now = sb("now", [P, 4])
        xTf = xT[:, :, :].rearrange("p a b -> p (a b)")
        hTe = xTf[:, 0:1024].rearrange("p (k s) -> p k s", k=KD)
        ye = xTf[:, 1024:2048]
        pick = xTf[:, 2048:2304].rearrange("p (t s) -> p t s", t=NT)
        put = xTf[:, 2304:2560].rearrange("p (t s) -> p t s", t=NT)
        putT = xTf[:, 2560:2816]
        iota = xTf[:, 2816:2944]
        tri_lt = xTf[:, 2944:3072]
        iota8 = xTf[:, 3072:3080]
        act_g = probs[:, 0, :]
        act = probs[:, 1, :]
        actT = probsT[:, 0, :]
        stick = xn[:, :, :].rearrange("p a b -> p (a b)")[:, 0:1536].rearrange("p (h k) -> p h k", h=4)
        stick_tmp = tmp[:, :].rearrange("p (h k) -> p h k", h=4)
        rvec = tmp[0:8, 0:512]
        onehot = tmp[0:33, 512:1024]
        bias_dram = nc.dram_tensor("bias_by_distance", (8, 512), F32, kind="Internal").ap()

        bank_full = [sem(f"bank{b}_full") for b in range(8)]
        bank_free = [sem(f"bank{b}_free") for b in range(8)]
        slot_full = [sem(f"slot{s}_full") for s in range(MOE_RING)]
        small_in = sem("small_in")
        consts_ready = sem("consts_ready")
        bias_out, bias_in = sem("bias_out"), sem("bias_in")
        v_done, a_done, g_done = sem("vector_done"), sem("scalar_done"), sem("gpsimd_done")
        setup_pe, setup_dve = sem("setup_pe"), sem("setup_dve")
        sq_ready, sums_ready, rstd_ready, xn_ready = sem("sq_ready"), sem("sums_ready"), sem("rstd_ready"), sem("xn_ready")
        head_sq, head_sums, head_rstd, heads_normed = sem("head_sq"), sem("head_sums"), sem("head_rstd"), sem("heads_normed")
        cmp_x_ready = sem("cmp_x_ready")
        mla_in, mla_rope_in, mla_sq, mla_sums, mla_rstd, mla_ready = (
            sem("mla_in"), sem("mla_rope_in"), sem("mla_sq"), sem("mla_sums"), sem("mla_rstd"), sem("mla_ready"))
        ng_exp = sem("ng_exp")
        stick_out = sem("stick_out")
        keys_split = sem("keys_split")
        ch_ready, ch_exp, ch_act = sem("ch_ready"), sem("ch_exp"), sem("ch_act")
        ck_sums, ck_rstd, ck_ready = sem("ck_sums"), sem("ck_rstd"), sem("ck_ready")
        stick_z, stick_ln, stick_sp, stick_t, stick_w = (
            sem("stick_z"), sem("stick_ln"), sem("stick_sp"), sem("stick_t"), sem("stick_w"))
        cmp_s, cmp_e, cmp_p = sem("cmp_s"), sem("cmp_e"), sem("cmp_p")
        max_ready, exp_ready, probs_ready, pv_done = sem("max_ready"), sem("exp_ready"), sem("probs_ready"), sem("pv_done")
        gates_ready, merged, x_mixed = sem("gates_ready"), sem("merged"), sem("x_mixed")
        gate_done, up_done, silu_done, act_ready = sem("gate_done"), sem("up_done"), sem("silu_done"), sem("act_ready")
        act_turned, actT_ready, down_done = sem("act_turned"), sem("actT_ready"), sem("down_done")
        x_dense = sem("x_dense")
        route_pe, route_dve, route_exp, routed = sem("route_pe"), sem("route_dve"), sem("route_exp"), sem("routed")
        now_ready, pick_ready = sem("now_ready"), sem("pick_ready")
        gathered, hTe_ready, put_turned, putT_ready = sem("gathered"), sem("hTe_ready"), sem("put_turned"), sem("putT_ready")
        ye_ready, spread, added = sem("ye_ready"), sem("spread"), sem("added")
        x_final, out_done = sem("x_final"), sem("out_done")

        def bank(key):
            return uses[key][0]

        def bank_taken_over(pe, key):
            b, n = uses[key]
            if n > 0:
                pe.wait_ge(bank_free[b], n)

        def bank_written(eng, key):
            b, n = uses[key]
            eng.wait_ge(bank_full[b], n + 1)

        def bank_read(eng, key):
            b, n = uses[key]
            eng.wait_ge(bank_free[b], n + 1)

        def slot_of(key):
            return chunk_no[key] % RING

        landed_value, slot_total = [], [0] * MOE_RING
        for n, key in enumerate(chunk_seq):
            slot_total[n % RING] += 16 * {"small": 4, "wo": 3}.get(key[1], 1)
            landed_value.append(slot_total[n % RING])

        def weights_landed(pe, key):
            n = chunk_no[key]
            pe.wait_ge(slot_full[n % RING], landed_value[n])

        def slot_view(s, k, w):
            return arena[:, s * SLOT:s * SLOT + k * w].rearrange("p (k w) -> p k w", k=k)

        block = ctx.enter_context(nc.Block())

        @block.sync
        def _(sp):
            def rows(ap):
                return ap.rearrange("(k p) n -> p k n", p=P)

            def chunk_free(key):
                L, kind = key[0], key[1]
                if kind == "in":
                    bank_written(sp, (L, "proj", key[2], NT - 1))
                elif kind in ("small", "w1"):
                    bank_written(sp, (L, "c2"))
                elif kind == "wo":
                    bank_written(sp, (L, "y", NT - 1, 1, 2))
                elif kind == "wout":
                    bank_written(sp, (L, "out", NT - 1, 1))
                else:
                    done = {"gate": gate_done, "up": up_done, "down": down_done}[kind]
                    sp.wait_ge(done, NT * (key[2] + 1))

            for n, key in enumerate(chunk_seq):
                L, kind = key[0], key[1]
                if n >= RING:
                    chunk_free(chunk_seq[n - RING])
                s = n % RING
                full = slot_full[s]
                if kind == "in":
                    c0, w = CHUNKS[key[2]]
                    parts = [(slot_view(s, KD, w), rows(a["w_in"][L, :, c0:c0 + w]))]
                elif kind == "small":
                    v = slot_view(s, 1, 1536)[:, 0, :]
                    parts = [(v[:, 0:768].rearrange("p (k w) -> p k w", k=2), rows(a["mla_w_uq"][L])),
                             (v[:, 768:1280], a["mla_w_ukv"][L]),
                             (v[:, 1280:1408].rearrange("p (k w) -> p k w", k=2), rows(a["nsa_cmp_w2"][L, 0])),
                             (v[:, 1408:1536].rearrange("p (k w) -> p k w", k=2), rows(a["nsa_cmp_w2"][L, 1]))]
                elif kind == "w1":
                    parts = [(slot_view(s, 16, 256), rows(a["nsa_cmp_w1"][L, key[2]]))]
                elif kind == "wo":
                    v = slot_view(s, 4, D)
                    nsa = a["nsa_w_o"][L].rearrange("(g r d) n -> g d r n", g=2, r=4)
                    plain, pv, q0, qv = ((a["sb_w_o"][L], 0, 0, 2), (a["mla_w_o"][L], 2, 2, 0))[key[2]]
                    parts = [(v[:, pv:pv + 2, :], rows(plain))]
                    parts += [(v[64 * g:64 * g + 64, qv:qv + 2, :], nsa[g, :, q0:q0 + 2, :]) for g in range(2)]
                elif kind == "wout":
                    parts = [(slot_view(s, 4, D), rows(a["w_out"][L, 512 * key[2]:512 * key[2] + 512, :]))]
                elif kind in ("gate", "up"):
                    f, w = DENSE_GROUPS[key[2]]
                    parts = [(slot_view(s, KD, w), rows(a["dense_w_" + kind][0, :, f:f + w]))]
                else:
                    f, w = DENSE_GROUPS[key[2]]
                    parts = [(slot_view(s, w // P, D), rows(a["dense_w_down"][0, f:f + w, :]))]
                for dst, src in parts:
                    sp.dma_start(dst, src).then_inc(full, 16)

            bank_read(sp, (DEPTH - 1, "out", NT - 1, 1))

            def expert_loads(it, e):
                for m, (kind, u) in enumerate(EXPERT_CHUNKS):
                    before_kind, before_u = EXPERT_CHUNKS[m - MOE_RING]
                    done = {"gate": gate_done, "up": up_done, "down": down_done}[before_kind]
                    back = EXPERT_UNITS if m < MOE_RING else 0
                    sp.wait_ge(done, it * EXPERT_UNITS + (DENSE_UNITS - back + before_u + 1))
                    s = m % MOE_RING
                    if kind == "down":
                        dst = slot_view(s, 4, D)
                        src = a["moe_w_down"][0, bass.ds(e, 1), 512 * u:512 * u + 512, :]
                    else:
                        dst = slot_view(s, KD, 512)
                        src = a["moe_w_" + kind][0, bass.ds(e, 1), :, 512 * u:512 * u + 512]
                    src = src.rearrange("e (k p) n -> p (e k) n", p=P)
                    sp.dma_start(dst, src).then_inc(slot_full[s], 16)

            with sp.Fori(0, N_EXPERTS) as e:
                expert_loads(e, e)
            sp.wait_ge(routed, 2)
            crowded = sp.value_load(flag_i[0:1, 0:1], min_val=0, max_val=1)
            with sp.If(crowded > 0):
                with sp.Fori(N_EXPERTS, 2 * N_EXPERTS) as it:
                    expert_loads(it, it - N_EXPERTS)
            sp.wait_ge(x_final, 1)
            sp.dma_start(out[0].rearrange("(t p) d -> p t d", p=P), x[:, :, :]).then_inc(out_done, 16)
            sp.wait_ge(out_done, 16)

        @block.gpsimd
        def _(pool):
            g = [0]

            def link(ins):
                g[0] += 1
                ins.then_inc(g_done, 1)
                pool.wait_ge(g_done, g[0])

            link(nc.gpsimd.memset(gain_rows, 0.0))
            link(nc.gpsimd.memset(table[32:64, :], NEG))
            link(nc.gpsimd.memset(ident[:, :], 0.0))
            link(nc.gpsimd.affine_select(out=ident[:, :], in_=ident[:, :], compare_op=ALU.not_equal, fill=1.0,
                                         base=0, pattern=[[-1, P]], channel_multiplier=1))
            link(nc.gpsimd.memset(flip, 0.0))
            link(nc.gpsimd.affine_select(out=flip, in_=flip, compare_op=ALU.not_equal, fill=1.0,
                                         base=-(P - 1), pattern=[[1, P]], channel_multiplier=1))
            link(nc.gpsimd.memset(ones[:, :], 1.0))
            link(nc.gpsimd.affine_select(out=tri_ge[:, :], in_=ones[:, :], compare_op=ALU.is_ge, fill=0.0,
                                         base=0, pattern=[[-1, P]], channel_multiplier=1))
            link(nc.gpsimd.memset(stick_mask[:, :], 0.0))
            for c in (0, 256):
                link(nc.gpsimd.affine_select(out=stick_mask[:, c:c + P], in_=stick_mask[:, c:c + P],
                                             compare_op=ALU.is_ge, fill=NEG, base=-1, pattern=[[1, P]],
                                             channel_multiplier=-1))
            link(nc.gpsimd.memset(causal[:, :], 0.0))
            link(nc.gpsimd.affine_select(out=causal[:, :], in_=causal[:, :], compare_op=ALU.is_ge, fill=NEG,
                                         base=P, pattern=[[-1, SEQ]], channel_multiplier=1))
            link(nc.gpsimd.memset(valid[:, :], 1.0))
            link(nc.gpsimd.affine_select(out=valid[:, 0:1], in_=valid[:, 0:1], compare_op=ALU.is_ge, fill=0.0,
                                         base=-31, pattern=[[0, 1]], channel_multiplier=1))
            link(nc.gpsimd.memset(inv_n[:, 0:18], 1.0 / HD))
            link(nc.gpsimd.memset(inv_n[:, 18:19], 1.0 / 256))
            link(nc.gpsimd.memset(inv_n[:, 19:20], 1.0 / 128))
            link(nc.gpsimd.memset(mhalf[:, :], -0.5))
            link(nc.gpsimd.memset(kcT[:, :, :], 0.0))
            nc.gpsimd.memset(cmp_x[:, :, 2, :], 0.0).then_inc(consts_ready, 1)

            def inverse_norm(s, n, done):
                link(nc.gpsimd.tensor_scalar(s, s, 1.0 / n, EPS, ALU.mult, ALU.add))
                w = s.shape[-1]
                nc.gpsimd.tensor_tensor(s, s, mhalf[0:s.shape[0], 0:w], ALU.pow).then_inc(done, 1)

            def residual_norm(N):
                for t in range(NT):
                    pool.wait_ge(sq_ready, NT * N + t + 1)
                    inverse_norm(ssum[:, t:t + 1], D, rstd_ready)

            for L in range(DEPTH):
                residual_norm(2 * L)
                for t in range(NT):
                    pool.wait_ge(head_sums, NT * L + t + 1)
                    link(nc.gpsimd.tensor_tensor(sums[:, t, :], sums[:, t, :], inv_n[:, :], ALU.mult))
                    link(nc.gpsimd.tensor_scalar(sums[:, t, :], sums[:, t, :], 1.0, EPS, ALU.mult, ALU.add))
                    nc.gpsimd.tensor_tensor(sums[:, t, :], sums[:, t, :], mhalf[:, :], ALU.pow).then_inc(head_rstd, 1)
                for t in range(NT):
                    pool.wait_ge(mla_sums, NT * L + t + 1)
                    inverse_norm(msum[:, t, :], MQ, mla_rstd)
                pool.wait_ge(ck_sums, L + 1)
                inverse_norm(ksum[0:N_CMP, :], HD, ck_rstd)
                residual_norm(2 * L + 1)

            bank_read(pool, (DEPTH - 1, "out", NT - 1, 1))
            link(nc.gpsimd.affine_select(out=tri_lt, in_=ones[:, :], compare_op=ALU.is_ge, fill=0.0,
                                         base=-1, pattern=[[1, P]], channel_multiplier=-1))
            link(nc.gpsimd.iota(iota, [[1, P]], base=0, channel_multiplier=0, allow_small_or_imprecise_dtypes=True))
            nc.gpsimd.iota(iota8, [[1, 8]], base=0, channel_multiplier=0,
                           allow_small_or_imprecise_dtypes=True).then_inc(consts_ready, 1)

        @block.scalar
        def _(act_e):
            c = [0]

            def link(ins):
                c[0] += 1
                ins.then_inc(a_done, 1)
                act_e.wait_ge(a_done, c[0])

            act = nc.scalar.activation

            def read_out(key, dst, src):
                bank_written(act_e, key)
                nc.scalar.copy(dst, src).then_inc(bank_free[bank(key)], 1)

            act_e.dma_start(x[:, :, :], a["x"][0].rearrange("(t p) d -> p t d", p=P)).then_inc(small_in, 16)
            act_e.dma_start(table[0:32, :], a["rel_bias_table"]).then_inc(small_in, 16)
            act_e.dma_start(onehot, a["bucket_onehot"]).then_inc(small_in, 16)
            act_e.dma_start(pos_rows, a["nsa_cmp_pos"].rearrange("l k (m j) d -> (l k m) (j d)", j=2)).then_inc(small_in, 16)
            act_e.dma_start(trig[:, :, :, :], a["rope_tables"]).then_inc(small_in, 16)
            act_e.dma_start(bgate[:, :], a["b_gate"].rearrange("l (c n) -> (l c) n", n=512)).then_inc(small_in, 16)
            act_e.dma_start(router[:, :, :], a["moe_router"][0].rearrange("(k p) e -> p k e", p=P)).then_inc(small_in, 16)
            act_e.wait_ge(g_done, 1)
            act_e.dma_start(gain_rows[G_MIX:G_MIX + 16, :], a["mix_norm"].rearrange("l (r c) -> (l r) c", c=P)).then_inc(small_in, 16)
            act_e.dma_start(gain_rows[G_FFN:G_FFN + 16, :], a["ffn_norm"].rearrange("l (r c) -> (l r) c", c=P)).then_inc(small_in, 16)
            for L in range(DEPTH):
                r = G_LAYER + L * G_PER_LAYER
                for half in (0, HD):
                    act_e.dma_start(gain_rows[r + G_Q:r + G_Q + 1, half:half + HD], a["nsa_q_norm"][L:L + 1, :]).then_inc(small_in, 16)
                    act_e.dma_start(gain_rows[r + G_KCMP:r + G_KCMP + 3, half:half + HD], a["nsa_k_norm"][L]).then_inc(small_in, 16)
                act_e.dma_start(gain_rows[r + G_QA:r + G_QA + 2, :], a["mla_q_a_norm"][L].rearrange("(r c) -> r c", c=P)).then_inc(small_in, 16)
                act_e.dma_start(gain_rows[r + G_KVA:r + G_KVA + 1, :], a["mla_kv_a_norm"][L:L + 1, :]).then_inc(small_in, 16)
                act_e.dma_start(mla_gain[:, L, 0, :], a["mla_q_norm"][L].partition_broadcast(P)).then_inc(small_in, 16)
                act_e.dma_start(mla_gain[:, L, 1, :], a["mla_k_norm"][L].partition_broadcast(P)).then_inc(small_in, 16)
            act_e.wait_ge(setup_dve, 1)
            act_e.dma_start(bias_dram, rvec).then_inc(bias_out, 16)
            act_e.wait_ge(bias_out, 16)
            toeplitz = bass.AP(bias_dram.tensor, 0, [[1, P], [512, 8], [1, 384]])
            act_e.dma_start(bias, toeplitz).then_inc(bias_in, 16)

            def residual_squares(N):
                for t in range(NT):
                    if N == 0:
                        act_e.wait_ge(small_in, SMALL_IN)
                    elif N % 2:
                        bank_read(act_e, (N // 2, "out", t, 0))
                        bank_read(act_e, (N // 2, "out", t, 1))
                    else:
                        act_e.wait_ge(x_dense, t + 1)
                    act(xn[:, t, :], x[:, t, :], ACT.Square, accum_out=ssum[:, t:t + 1]).then_inc(sq_ready, 1)

            def projection_out(L, c, t):
                c0, w = CHUNKS[c]
                key = (L, "proj", c, t)
                read_out(key, proj[:, t, c0:c0 + w], ps[:, bank(key), 0:w])

            def mixers(L):
                residual_squares(2 * L)
                for c_ in range(N_MIX_CHUNKS):
                    projection_out(L, c_, 0)
                for t in range(NT):
                    for c_ in range(1, N_MIX_CHUNKS):
                        bank_read(act_e, (L, "proj", c_, t))
                    if t == 1:
                        act_e.wait_ge(head_sums, NT * L + 1)
                    act(tmp[:, 0:1152], proj[:, t, NQ:NQ + 1152], ACT.Square).then_inc(head_sq, 1)
                    act(tmp[:, 1152:1536], proj[:, t, CQ:CQ + 384], ACT.Square).then_inc(head_sq, 1)
                for t in range(NT):
                    act(ngate[:, t, :], proj[:, t, NG:NG + 24], ACT.Exp, scale=-1.0).then_inc(ng_exp, 1)
                projection_out(L, 5, 0)
                for t in range(NT):
                    key = (L, "xt", t, 0)
                    read_out(key, xT[:, 0:4, P * t:P * t + P], ps[:, bank(key), :].rearrange("p (j q) -> p j q", j=4))
                projection_out(L, 6, 0)
                for t in range(NT):
                    key = (L, "uq", t)
                    read_out(key, mqk[:, t, 0:4, :], ps[:, bank(key), 0:384].rearrange("p (h d) -> p h d", h=4))
                    key = (L, "ukv", t)
                    both = ps[:, bank(key), :].rearrange("p (h d) -> p h d", h=4)
                    bank_written(act_e, key)
                    nc.scalar.copy(mqk[:, t, 4:8, 0:HD], both[:, :, 0:HD]).then_inc(mla_in, 1)
                    nc.scalar.copy(mv[:, t, :, :], both[:, :, HD:P]).then_inc(bank_free[bank(key)], 1)
                for t in range(NT):
                    act_e.wait_ge(mla_in, NT * L + t + 1)
                    bank_read(act_e, (L, "uq", t))
                    act_e.wait_ge(mla_rope_in, L + 1)
                    act_e.wait_ge(*((head_sums, NT * L + NT) if t == 0 else (mla_sums, NT * L + 1)))
                    act(tmp[:, 0:768], mqk[:, t, :, :].rearrange("p h d -> p (h d)"), ACT.Square).then_inc(mla_sq, 1)
                key = (L, "c1")
                read_out(key, ch_raw[:, :, :], ps[:, bank(key), 0:180].rearrange("p (f n) -> p f n", f=4))
                act_e.wait_ge(ch_ready, L + 1)
                act(ce[:, :, :], ch[:, :, :], ACT.Exp, scale=-1.0).then_inc(ch_exp, 1)
                projection_out(L, 7, 0)
                act_e.wait_ge(stick_z, L + 1)
                act_e.wait_ge(mla_sums, NT * L + NT)
                link(act(stick_tmp[:, :, :], stick, ACT.Abs))
                link(act(tmp[:, :], tmp[:, :], ACT.Exp, scale=-1.0))
                act(tmp[:, :], tmp[:, :], ACT.Ln, bias=1.0).then_inc(stick_ln, 1)
                for t in range(NT):
                    for b in range(2):
                        key = (L, "mt", t, b)
                        read_out(key, mT[0:MQ, 4 * b:4 * b + 4, P * t:P * t + P],
                                 ps[0:MQ, bank(key), :].rearrange("p (j q) -> p j q", j=4))
                act_e.wait_ge(stick_t, L + 1)
                act(stick, stick, ACT.Exp).then_inc(stick_w, 1)
                for i in range(NT):
                    act_e.wait_ge(cmp_s, NT * L + i + 1)
                    act(pcs[:, i, :, 0:N_CMP], pcs[:, i, :, 0:N_CMP], ACT.Exp).then_inc(cmp_e, 1)
                for hp in range(2):
                    key = (L, "sbo", hp)
                    act_e.wait_ge(stick_out, 2 * L + hp + 1)
                    nc.scalar.copy(yT[:, hp, :], ps[:, bank(key), 0:SEQ]).then_inc(bank_free[bank(key)], 1)
                for s in range(STEPS):
                    if s < len(JOBS):
                        job_exp(L, s)
                    if 0 <= s - LAG_TURN < len(JOBS):
                        job_turned(L, s - LAG_TURN)
                    if 0 <= s - LAG_PV < len(JOBS):
                        job_out(L, s - LAG_PV)
                    if s in LATE_GATES and LATE_GATES[s][1] == 0:
                        projection_out(L, *LATE_GATES[s])
                for t in range(NT):
                    for c_ in range(N_MIX_CHUNKS, len(CHUNKS)):
                        bank_read(act_e, (L, "proj", c_, t))
                    act(proj[:, t, GATES:], proj[:, t, GATES:], ACT.Sigmoid).then_inc(gates_ready, 1)
                for t in range(NT):
                    for h in range(2):
                        key = (L, "merge", t, h)
                        read_out(key, hT[:, 4 * h:4 * h + 4, P * t:P * t + P],
                                 ps[:, bank(key), :].rearrange("p (j q) -> p j q", j=4))
                residual_squares(2 * L + 1)

            def job_exp(L, j):
                kind, i, r = JOBS[j]
                nk = P * (i + 1)
                n = len(JOBS) * L + j
                b = n % 3
                act_e.wait_ge(max_ready, n + 1)
                v = probs[:, b, 0:2 * nk].rearrange("p (a k) -> p a k", a=2)
                for h in range(2):
                    act(v[:, h, :], v[:, h, :], ACT.Exp, bias=nmax[:, b, h:h + 1],
                        accum_out=prob_sum[:, b, h:h + 1]).then_inc(exp_ready, 1)

            def job_turned(L, j):
                kind, i, r = JOBS[j]
                n = len(JOBS) * L + j
                if n >= 2:
                    act_e.wait_ge(pv_done, n - 1)
                key = (L, "p", j)
                w = 2 * (i + 1) * P
                read_out(key, probsT[:, n % 2, 0:w], ps[:, bank(key), 0:w])

            def job_out(L, j):
                kind, i, r = JOBS[j]
                if kind == "sel":
                    return
                act_e.wait_ge(pv_done, len(JOBS) * L + j + 1)
                key = (L, "mlao", i, r) if kind == "mla" else (L, "nsao", i, r)
                to = 6 + r if kind == "mla" else 2 + r
                nc.scalar.copy(yT[:, to, P * i:P * i + P], ps[:, bank(key), 0:P]).then_inc(bank_free[bank(key)], 1)

            def ffn_silu(n, w, first=False):
                act_e.wait_ge(gate_done, n + 1)
                if not first:
                    act_e.wait_ge(act_ready, n)
                act(act_g[:, 0:w], ps[:, 2, 0:w], ACT.Silu).then_inc(silu_done, 1)

            def ffn_turned(n, w, first=False):
                act_e.wait_ge(act_turned, n + 1)
                if not first:
                    act_e.wait_ge(down_done, n)
                nc.scalar.copy(actT[:, 0:w], ps[:, 0, 0:w]).then_inc(actT_ready, 1)

            mixers(0)
            widths = [w for _, w in DENSE_GROUPS for _ in range(NT)]
            for u in range(DENSE_UNITS):
                ffn_silu(u, widths[u], u == 0)
                if u:
                    ffn_turned(u - 1, widths[u - 1], u == 1)
            ffn_turned(DENSE_UNITS - 1, widths[-1])
            mixers(1)

            act_e.wait_ge(route_dve, 1)
            act(route[:, 2, :, 1:2], route[:, 2, :, 0:1], ACT.Exp).then_inc(route_exp, 1)

            def put_out(it):
                act_e.wait_ge(put_turned, it + 1)
                nc.scalar.copy(putT, ps[:, 1, 0:SEQ]).then_inc(putT_ready, 1)

            put_out(0)
            act_e.sem_inc(ye_ready, 1)

            def expert(it):
                base = it * EXPERT_UNITS
                for u in range(EXPERT_UNITS):
                    ffn_silu(base + (DENSE_UNITS + u), 512)
                    if u:
                        ffn_turned(base + (DENSE_UNITS + u - 1), 512)
                ffn_turned(base + (DENSE_UNITS + EXPERT_UNITS - 1), 512)
                act_e.wait_ge(down_done, base + (DENSE_UNITS + EXPERT_UNITS))
                act_e.wait_ge(spread, it * 4 + 1)
                nc.scalar.copy(ye, ps[:, 4:6, :].rearrange("p h n -> p (h n)")).then_inc(ye_ready, 1)
                act_e.wait_ge(spread, it * 4 + 5)
                put_out(it + 1)

            with act_e.Fori(0, N_EXPERTS) as it:
                expert(it)
            act_e.wait_ge(routed, 2)
            crowded = act_e.value_load(flag_i[0:1, 0:1], min_val=0, max_val=1)
            with act_e.If(crowded > 0):
                with act_e.Fori(N_EXPERTS, 2 * N_EXPERTS) as it:
                    expert(it)

        @block.vector
        def _(dve):
            c = [0]
            V = nc.vector

            def link(ins):
                c[0] += 1
                ins.then_inc(v_done, 1)
                dve.wait_ge(v_done, c[0])

            def bc(ap, n):
                return ap.unsqueeze(len(ap.shape)).to_broadcast(list(ap.shape) + [n])

            def turned_with_gains(key, dst, col):
                bank_written(dve, key)
                k = dst.shape[1]
                V.tensor_tensor(dst, ps[:, bank(key), 0:k * P].rearrange("p (j q) -> p j q", j=k),
                                bc(gains[:, col:col + k], P), ALU.mult).then_inc(bank_free[bank(key)], 1)

            def residual_norm(L, which, col):
                N = 2 * L + (which == "norm2")
                for t in range(NT):
                    dve.wait_ge(rstd_ready, NT * N + t + 1)
                    V.tensor_scalar(xn[:, t, :], x[:, t, :], ssum[:, t:t + 1], None, ALU.mult).then_inc(xn_ready, 1)
                for t in range(NT):
                    for h in range(2):
                        turned_with_gains((L, which, t, h), hT[:, 4 * h:4 * h + 4, P * t:P * t + P], col + 4 * h)

            def projection_out(L, c_, t):
                c0, w = CHUNKS[c_]
                key = (L, "proj", c_, t)
                bank_written(dve, key)
                V.tensor_copy(proj[:, t, c0:c0 + w], ps[:, bank(key), 0:w]).then_inc(bank_free[bank(key)], 1)

            dve.wait_ge(setup_pe, 1)
            link(V.tensor_copy(gains[:, :], ps[:, 6, 0:64]))
            link(V.tensor_copy(posT[:, :, :].rearrange("p a b -> p (a b)"), ps[:, 6, P:P + 64]))
            V.tensor_copy(rvec, ps[0:8, 7, :]).then_inc(setup_dve, 1)

            def head_norms(L, t):
                dve.wait_ge(head_sq, 2 * (NT * L + t) + 2)
                V.tensor_reduce(sums[:, t, 0:18], tmp[:, 0:1152].rearrange("p (h d) -> p h d", d=HD), AX.X, ALU.add)
                V.tensor_reduce(sums[:, t, 18:19], tmp[:, 1152:1408], AX.X, ALU.add)
                V.tensor_reduce(sums[:, t, 19:20], tmp[:, 1408:1536], AX.X, ALU.add).then_inc(head_sums, 1)
                dve.wait_ge(head_rstd, NT * L + t + 1)
                q = proj[:, t, NQ:NQ + 512].rearrange("p (g r d) -> p g r d", g=2, r=4)
                pairs = xn[:, t, 0:512].rearrange("p (r g d) -> p g r d", r=4, g=2)
                for g in range(2):
                    V.tensor_tensor(pairs[:, g], q[:, g], bc(sums[:, t, 4 * g:4 * g + 4], HD), ALU.mult)
                for c0, n, s0 in ((KS, 2, 12), (KW, 2, 16)):
                    v = proj[:, t, c0:c0 + n * HD].rearrange("p (h d) -> p h d", d=HD)
                    V.tensor_tensor(v, v, bc(sums[:, t, s0:s0 + n], HD), ALU.mult)
                V.tensor_scalar(proj[:, t, CQ:CQ + 256], proj[:, t, CQ:CQ + 256], sums[:, t, 18:19], None, ALU.mult)
                V.tensor_scalar(proj[:, t, CKV:CKV + P], proj[:, t, CKV:CKV + P], sums[:, t, 19:20], None,
                                ALU.mult).then_inc(heads_normed, 1)

            def turned_mixer_inputs(L, t):
                g0 = G_LAYER + L * G_PER_LAYER
                q = slice(P * t, P * t + P)
                key = (L, "xt", t, 1)
                bank_written(dve, key)
                V.tensor_scalar(xT[:, 4:8, q], ps[:, bank(key), :].rearrange("p (j q) -> p j q", j=4),
                                gains[:, g0 + G_Q:g0 + G_Q + 1], None, ALU.mult).then_inc(bank_free[bank(key)], 1)
                key = (L, "xt", t, 2)
                bank_written(dve, key)
                b = ps[:, bank(key), :]
                for kv in range(2):
                    for g in range(2):
                        for par in range(2):
                            src = b[64 * g:64 * g + 64, (2 + kv) * P:(3 + kv) * P].rearrange("p (m j) -> p m j", j=2)
                            V.tensor_copy(cmp_x[64 * par:64 * par + 64, kv, g, 64 * t:64 * t + 64], src[:, :, par])
                if t == 0:
                    V.tensor_copy(cmp_x[:, :, 2, 0:16], posT[:, 2 * L:2 * L + 2, :])
                V.tensor_tensor(xT[:, 8:10, q], b[:, 0:2 * P].rearrange("p (j q) -> p j q", j=2),
                                bc(gains[:, g0 + G_KSEL:g0 + G_KSEL + 2], P), ALU.mult).then_inc(bank_free[bank(key)], 1)
                turned_with_gains((L, "xt", t, 3), xT[:, 10:13, q], g0 + G_QA)

            def latent_heads(L, t):
                m = mqk[:, t, :, :]
                dve.wait_ge(mla_sq, NT * L + t + 1)
                V.tensor_reduce(msum[:, t, :], tmp[:, 0:768].rearrange("p (h d) -> p h d", d=MQ), AX.X,
                                ALU.add).then_inc(mla_sums, 1)
                dve.wait_ge(mla_rstd, NT * L + t + 1)
                link(V.tensor_tensor(m, m, bc(msum[:, t, :], MQ), ALU.mult))
                for w in range(2):
                    v = m[:, 4 * w:4 * w + 4, :]
                    gain = mla_gain[:, L, w, :].unsqueeze(1).to_broadcast([P, 4, MQ])
                    ins = V.tensor_tensor(v, v, gain, ALU.mult)
                link(ins)
                x1, x2 = m[:, :, 64:80], m[:, :, 80:96]
                cos, sin = (trig[:, f, t, :].unsqueeze(1).to_broadcast([P, 8, 16]) for f in range(2))
                r = rope_tmp.rearrange("p f (h d) -> p f h d", h=8)
                V.tensor_tensor(r[:, 0], x1, cos, ALU.mult)
                V.tensor_tensor(r[:, 1], x2, sin, ALU.mult)
                V.tensor_tensor(r[:, 2], x2, cos, ALU.mult)
                link(V.tensor_tensor(r[:, 3], x1, sin, ALU.mult))
                V.tensor_tensor(x1, r[:, 0], r[:, 1], ALU.subtract)
                V.tensor_tensor(x2, r[:, 2], r[:, 3], ALU.add).then_inc(mla_ready, 1)

            def mixers(L):
                residual_norm(L, "norm1", G_MIX + KD * L)
                g0 = G_LAYER + L * G_PER_LAYER
                for c_ in range(N_MIX_CHUNKS):
                    projection_out(L, c_, 1)
                for t in range(NT):
                    bank_read(dve, (L, "proj", 4, t))
                    ins = V.tensor_copy(mqk[:, t, 4:8, HD:MQ], proj[:, t, KR:KR + 32].unsqueeze(1).to_broadcast([P, 4, 32]))
                ins.then_inc(mla_rope_in, 1)
                for t in range(NT):
                    head_norms(L, t)
                dve.wait_ge(ng_exp, NT * L + NT)
                flat = ngate[:, :, :].rearrange("p t n -> p (t n)")
                link(V.tensor_scalar(flat, flat, 1.0, None, ALU.add))
                link(V.reciprocal(flat, flat))
                projection_out(L, 5, 1)
                for t in range(NT):
                    turned_mixer_inputs(L, t)
                projection_out(L, 6, 1)
                for t in range(NT):
                    latent_heads(L, t)
                for t in range(NT):
                    bank_read(dve, (L, "uq", t))
                    bank_read(dve, (L, "ukv", t))
                link(V.tensor_copy(xT[64:P, 10:12, :], xT[64:P, 8:10, :]))
                V.memset(xT[64:P, 8:10, :], 0.0)
                V.memset(xT[0:64, 10:12, :], 0.0).then_inc(keys_split, 1)
                bank_read(dve, (L, "c1"))
                V.tensor_tensor(ch[:, :, :], ch_raw[:, :, 0:30], ch_raw[:, :, 30:31].to_broadcast([P, 4, 30]),
                                ALU.add).then_inc(ch_ready, 1)
                dve.wait_ge(ch_exp, L + 1)
                link(V.tensor_scalar(ce[:, :, :], ce[:, :, :], 1.0, None, ALU.add))
                link(V.reciprocal(ce[:, :, :], ce[:, :, :]))
                V.tensor_tensor(ch[:, :, :], ch[:, :, :], ce[:, :, :], ALU.mult).then_inc(ch_act, 1)
                for h in range(4):
                    key = (L, "z", h)
                    bank_written(dve, key)
                    V.scalar_tensor_tensor(out=stick[:, h, :], in0=ps[:, bank(key), 0:384], scalar=HD ** -0.5,
                                           in1=stick_mask[:, :], op0=ALU.mult, op1=ALU.add).then_inc(bank_free[bank(key)], 1)
                bank_read(dve, (L, "z", 2))
                bank_read(dve, (L, "z", 3))
                link(V.tensor_copy(cmax[0:1, 0:1], ones[0:1, 0:1]))
                dve.sem_inc(stick_z, 1)
                key = (L, "c2")
                bank_written(dve, key)
                V.tensor_copy(ckv_c[0:N_CMP, :, :], ps[0:N_CMP, bank(key), 0:4 * HD].rearrange("p (f d) -> p f d", f=4)).then_inc(bank_free[bank(key)], 1)
                bank_read(dve, key)
                link(V.tensor_tensor(csq[0:N_CMP, :, :], ckv_c[0:N_CMP, 0:2, :], ckv_c[0:N_CMP, 0:2, :], ALU.mult))
                V.tensor_reduce(ksum[0:N_CMP, :], csq[0:N_CMP, :, :], AX.X, ALU.add).then_inc(ck_sums, 1)
                dve.wait_ge(ck_rstd, L + 1)
                V.tensor_tensor(ckv_c[0:N_CMP, 0:2, :], ckv_c[0:N_CMP, 0:2, :], bc(ksum[0:N_CMP, :], HD),
                                ALU.mult).then_inc(ck_ready, 1)
                projection_out(L, 7, 1)
                key = (L, "kct")
                bank_written(dve, key)
                for g in range(2):
                    r = slice(64 * g, 64 * g + 64)
                    ins = V.tensor_scalar(kcT[r, g, 0:N_CMP], ps[r, bank(key), 0:N_CMP],
                                          gains[r, g0 + G_KCMP:g0 + G_KCMP + 1], None, ALU.mult)
                ins.then_inc(bank_free[bank(key)], 1)
                dve.wait_ge(stick_ln, L + 1)
                V.scalar_tensor_tensor(out=stick_tmp[:, :, :], in0=stick, scalar=0.0, in1=stick_tmp[:, :, :],
                                       op0=ALU.max, op1=ALU.add).then_inc(stick_sp, 1)
                for h in range(4):
                    key = (L, "S", h)
                    bank_written(dve, key)
                    V.tensor_tensor(stick[:, h, :], stick[:, h, :], ps[:, bank(key), 0:384],
                                    ALU.subtract).then_inc(bank_free[bank(key)], 1)
                bank_read(dve, (L, "S", 2))
                bank_read(dve, (L, "S", 3))
                dve.sem_inc(stick_t, 1)
                if L == 0:
                    for h in range(8):
                        key = (0, "flip", h)
                        bank_written(dve, key)
                        V.tensor_copy(bias[:, h, :], ps[:, bank(key), 0:384]).then_inc(bank_free[bank(key)], 1)
                    for h in (6, 7):
                        bank_read(dve, (0, "flip", h))
                for i in range(NT):
                    key = (L, "sc", i)
                    bank_written(dve, key)
                    s = pcs[:, i, :, 0:N_CMP]
                    k0 = 31 + P * (1 - i)
                    V.scalar_tensor_tensor(out=s, in0=ps[:, bank(key), 0:P].rearrange("p (h n) -> p h n", h=8)[:, :, 0:N_CMP],
                                           scalar=HD ** -0.5, in1=bias[:, :, k0:k0 + 16 * (N_CMP - 1) + 1:16],
                                           op0=ALU.mult, op1=ALU.add).then_inc(bank_free[bank(key)], 1)
                    bank_read(dve, key)
                    link(V.tensor_reduce(cmax[:, :], s, AX.X, ALU.max))
                    V.tensor_tensor(s, s, bc(cmax[:, :], N_CMP), ALU.subtract).then_inc(cmp_s, 1)
                    dve.wait_ge(cmp_e, NT * L + i + 1)
                    link(V.tensor_reduce(csum[:, :], s, AX.X, ALU.add))
                    link(V.reciprocal(csum[:, :], csum[:, :]))
                    link(V.scalar_tensor_tensor(out=csum[:, :], in0=csum[:, :], scalar=valid[:, i:i + 1],
                                                in1=ngate[:, i, 0:24:3], op0=ALU.mult, op1=ALU.mult))
                    V.tensor_tensor(s, s, bc(csum[:, :], N_CMP), ALU.mult).then_inc(cmp_p, 1)
                for s in range(STEPS):
                    if s < len(JOBS):
                        job_scores(L, s)
                    if 0 <= s - 1 < len(JOBS):
                        job_scale(L, s - 1)
                    for i in range(NT):
                        if s - LAG_TURN == FIRST_SPARSE[i]:
                            compressed_turned(L, i)
                    if s in LATE_GATES and LATE_GATES[s][1] == 1:
                        projection_out(L, *LATE_GATES[s])
                for t in range(NT):
                    dve.wait_ge(gates_ready, NT * L + t + 1)
                    for h in range(2):
                        to = xn[:, t, 512 * h:512 * h + 512]
                        for m in range(3):
                            key = (L, "y", t, h, m)
                            gate = proj[:, t, GATES + D * m + 512 * h:GATES + D * m + 512 * h + 512]
                            dst = to if m == 0 else tmp[:, 512 * (m - 1):512 * m]
                            bank_written(dve, key)
                            V.tensor_tensor(dst, ps[:, bank(key), :], gate, ALU.mult).then_inc(bank_free[bank(key)], 1)
                            bank_read(dve, key)
                            if m == 1:
                                link(V.tensor_tensor(to, to, dst, ALU.add))
                            if m == 2:
                                V.tensor_tensor(to, to, dst, ALU.add).then_inc(merged, 1)
                                dve.wait_ge(merged, 4 * L + 2 * t + h + 1)
                for t in range(NT):
                    for h in range(2):
                        key = (L, "out", t, h)
                        bank_written(dve, key)
                        V.tensor_tensor(x[:, t, 512 * h:512 * h + 512], x[:, t, 512 * h:512 * h + 512],
                                        ps[:, bank(key), :], ALU.add).then_inc(bank_free[bank(key)], 1)
                residual_norm(L, "norm2", G_FFN + KD * L)

            def job_scores(L, j):
                kind, i, r = JOBS[j]
                nk = P * (i + 1)
                n = len(JOBS) * L + j
                b = n % 3
                if j >= 3:
                    bank_written(dve, (L, "p", j - 3))
                v = probs[:, b, 0:2 * nk].rearrange("p (a k) -> p a k", a=2)
                k0 = P * (1 - i)
                if kind == "mla":
                    add = causal[:, k0:SEQ].unsqueeze(1).to_broadcast([P, 2, nk])
                    scale = MQ ** -0.5
                else:
                    add = bias[:, r:8:4, k0:SEQ]
                    scale = HD ** -0.5
                key = (L, "s", j)
                bank_written(dve, key)
                V.scalar_tensor_tensor(out=v, in0=ps[:, bank(key), 0:2 * nk].rearrange("p (a k) -> p a k", a=2),
                                       scalar=scale, in1=add, op0=ALU.mult, op1=ALU.add).then_inc(bank_free[bank(key)], 1)
                bank_read(dve, key)
                V.tensor_reduce(nmax[:, b, :], v, AX.X, ALU.max, negate=True).then_inc(max_ready, 1)

            def job_scale(L, j):
                kind, i, r = JOBS[j]
                nk = P * (i + 1)
                n = len(JOBS) * L + j
                b = n % 3
                dve.wait_ge(exp_ready, 2 * n + 2)
                link(V.reciprocal(prec[:, b, :], prob_sum[:, b, :]))
                if kind != "mla":
                    g = 3 * r + (1 if kind == "sel" else 2)
                    link(V.tensor_tensor(prec[:, b, :], prec[:, b, :], ngate[:, i, g:g + 13:12], ALU.mult))
                v = probs[:, b, 0:2 * nk].rearrange("p (a k) -> p a k", a=2)
                V.tensor_tensor(v, v, bc(prec[:, b, :], nk), ALU.mult).then_inc(probs_ready, 1)

            def compressed_turned(L, i):
                for h in range(2):
                    key = (L, "pc", i, h)
                    if i > 0 and h == 0:
                        dve.wait_ge(pv_done, len(JOBS) * L + FIRST_SPARSE[i])
                    bank_written(dve, key)
                    V.tensor_copy(pcT[0:N_CMP, 4 * h:4 * h + 4, :],
                                  ps[0:N_CMP, bank(key), :].rearrange("p (h q) -> p h q", h=4)).then_inc(bank_free[bank(key)], 1)

            def ffn_product(n, w):
                dve.wait_ge(up_done, n + 1)
                dve.wait_ge(silu_done, n + 1)
                if not isinstance(n, int) or n > 0:
                    dve.wait_ge(act_turned, n)
                V.tensor_tensor(act[:, 0:w], act_g[:, 0:w], ps[:, 3, 0:w], ALU.mult).then_inc(act_ready, 1)

            mixers(0)
            widths = [w for _, w in DENSE_GROUPS for _ in range(NT)]
            for u in range(DENSE_UNITS):
                ffn_product(u, widths[u])
            for t in range(NT):
                dve.wait_ge(down_done, DENSE_UNITS - NT + t + 1)
                for h in range(2):
                    v = x[:, t, 512 * h:512 * h + 512]
                    ins = V.tensor_tensor(v, v, ps[:, 4 + 2 * t + h, :], ALU.add)
                ins.then_inc(x_dense, 1)
            mixers(1)

            dve.wait_ge(route_pe, 1)
            dve.wait_ge(consts_ready, 2)
            logits, top, w_top, oh0, oh1, sel = (route[:, n] for n in range(6))
            slot1 = route[:, 6]
            link(V.tensor_copy(logits, ps[:, 1, 0:16].rearrange("p (t e) -> p t e", t=NT)))
            for t in range(NT):
                link(V.max(top[:, t, :], logits[:, t, :]))
                link(V.max_index(top_i[:, t, :], top[:, t, :], logits[:, t, :]))
            top_f = route[:, 7]
            link(V.tensor_copy(top_f, top_i[:, :, :]))
            V.tensor_tensor(w_top[:, :, 0:1], top[:, :, 1:2], top[:, :, 0:1], ALU.subtract).then_inc(route_dve, 1)
            dve.wait_ge(route_exp, 1)
            link(V.tensor_scalar(w_top[:, :, 2:3], w_top[:, :, 1:2], 1.0, None, ALU.add))
            link(V.reciprocal(w_top[:, :, 3:4], w_top[:, :, 2:3]))
            link(V.tensor_tensor(w_top[:, :, 4:5], w_top[:, :, 1:2], w_top[:, :, 3:4], ALU.mult))
            for t in range(NT):
                V.tensor_scalar(oh0[:, t, :], iota8, top_f[:, t, 0:1], None, ALU.is_equal)
                link(V.tensor_scalar(oh1[:, t, :], iota8, top_f[:, t, 1:2], None, ALU.is_equal))
                link(V.tensor_scalar(comb[:, t, 0:8], oh1[:, t, :], w_top[:, t, 4:5], None, ALU.mult))
                link(V.scalar_tensor_tensor(out=comb[:, t, 0:8], in0=oh0[:, t, :], scalar=w_top[:, t, 3:4],
                                            in1=comb[:, t, 0:8], op0=ALU.mult, op1=ALU.add))
            V.tensor_copy(comb[:, :, 8:16], comb[:, :, 0:8])
            V.memset(comb[:, :, 16:17], 0.0)
            V.tensor_tensor(sel, oh0, oh1, ALU.add).then_inc(route_dve, 1)
            dve.wait_ge(route_pe, 2)
            link(V.scalar_tensor_tensor(out=slot1, in0=ps[:, 1, 0:16].rearrange("p (t e) -> p t e", t=NT), scalar=1.0,
                                        in1=sel, op0=ALU.add, op1=ALU.mult))
            link(V.tensor_scalar(slots[:, :, 0:8], slot1, -1.0, None, ALU.add))
            V.tensor_scalar(slots[:, :, 8:16], slot1, -1.0 - P, None, ALU.add)
            V.memset(slots[:, :, 16:17], -1.0)
            link(V.tensor_reduce(flag[:, 0:1], ps[:, 1, 16:24], AX.X, ALU.max))
            link(V.tensor_scalar(flag[:, 1:2], flag[:, 0:1], P + 0.5, None, ALU.is_gt))
            V.tensor_copy(flag_i[:, :], flag[:, 1:2]).then_inc(routed, 1)
            dve.wait_ge(routed, 1)
            V.tensor_copy(now[:, 0:1], flag[:, 0:1]).then_inc(routed, 1)
            dve.wait_ge(routed, 2)

            def pick_tokens(it, first=False):
                if not first:
                    dve.wait_ge(gathered, it * 2)
                    dve.wait_ge(put_turned, it)
                V.tensor_copy(now[:, 0:2], slots[:, :, bass.ds(it, 1)].rearrange("p t o -> p (t o)"))
                V.tensor_copy(now[:, 2:4], comb[:, :, bass.ds(it, 1)].rearrange("p t o -> p (t o)")).then_inc(now_ready, 1)
                dve.wait_ge(now_ready, it + 1)
                for t in range(NT):
                    V.tensor_scalar(pick[:, t, :], iota, now[:, t:t + 1], None, ALU.is_equal)
                    ins = V.tensor_scalar(put[:, t, :], iota, now[:, t:t + 1], now[:, 2 + t:3 + t], ALU.is_equal, ALU.mult)
                ins.then_inc(pick_ready, 1)

            ffn_gain = G_FFN + KD * (DEPTH - 1)

            def gathered_out(it, first=False):
                for h in range(2):
                    dve.wait_ge(gathered, it * 2 + (h + 1))
                    if not first:
                        dve.wait_ge(up_done, it * EXPERT_UNITS + DENSE_UNITS)
                    V.tensor_tensor(hTe[:, 4 * h:4 * h + 4, :], ps[:, 6 + h, :].rearrange("p (j s) -> p j s", j=4),
                                    bc(gains[:, ffn_gain + 4 * h:ffn_gain + 4 * h + 4], P), ALU.mult).then_inc(hTe_ready, 1)

            pick_tokens(0, True)
            gathered_out(0, True)
            dve.sem_inc(added, 1)

            def expert(it):
                pick_tokens(it + 1)
                for u in range(EXPERT_UNITS):
                    ffn_product(it * EXPERT_UNITS + (DENSE_UNITS + u), 512)
                gathered_out(it + 1)
                for k in range(4):
                    t, h = k // 2, k % 2
                    dve.wait_ge(spread, it * 4 + (k + 2))
                    v = x[:, t, 512 * h:512 * h + 512]
                    V.tensor_tensor(v, v, ps[:, 6 + k % 2, :], ALU.add).then_inc(added, 1)
                dve.wait_ge(added, it * 4 + 5)

            with dve.Fori(0, N_EXPERTS) as it:
                expert(it)
            crowded = dve.value_load(flag_i[0:1, 0:1], min_val=0, max_val=1)
            with dve.If(crowded > 0):
                with dve.Fori(N_EXPERTS, 2 * N_EXPERTS) as it:
                    expert(it)
            V.tensor_copy(now[:, 0:1], flag[:, 0:1]).then_inc(x_final, 1)

        @block.tensor
        def _(pe):
            mm, turn = nc.tensor.matmul, nc.tensor.transpose

            def done(ins, key):
                ins.then_inc(bank_full[bank(key)], 1)

            pe.wait_ge(consts_ready, 1)
            pe.wait_ge(small_in, SMALL_IN)
            turn(ps[:, 6, 0:P], gain_rows, ident[:, :])
            turn(ps[:, 6, P:P + 64], pos_rows, ident[0:64, 0:64])
            mm(ps[0:8, 7, :], table[0:33, 0:8], onehot, start=True, stop=True).then_inc(setup_pe, 1)
            pe.wait_ge(setup_dve, 1)

            def turn_residual(key, t, h):
                bank_taken_over(pe, key)
                for j in range(4):
                    ins = turn(ps[:, bank(key), P * j:P * j + P], xn[:, t, P * (4 * h + j):P * (4 * h + j + 1)], ident[:, :])
                done(ins, key)

            def turned_norm(L, which):
                N = 2 * L + (which == "norm2")
                for t in range(NT):
                    pe.wait_ge(xn_ready, NT * N + t + 1)
                    for h in range(2):
                        turn_residual((L, which, t, h), t, h)

            def project(L, c, t):
                c0, w = CHUNKS[c]
                key = (L, "proj", c, t)
                bank_taken_over(pe, key)
                weights_landed(pe, (L, "in", c))
                if c == 0:
                    for h in range(2):
                        bank_read(pe, (L, "norm1", t, h))
                wv = slot_view(slot_of((L, "in", c)), KD, w)
                b = ps[:, bank(key), 0:w]
                gate = c >= N_MIX_CHUNKS
                for k in range(KD):
                    ins = mm(b, hT[:, k, P * t:P * t + P], wv[:, k, :], start=(k == 0), stop=(k == KD - 1 and not gate))
                if gate:
                    row = 6 * L + c - N_MIX_CHUNKS
                    ins = mm(b, ident[0:12, row:row + 1].to_broadcast([12, P]), bgate[0:12, :], start=False, stop=True)
                done(ins, key)

            def turn_mixer_inputs(L, t):
                pe.wait_ge(heads_normed, NT * L + t + 1)
                p = proj[:, t, :]
                pairs = [xn[:, t, P * r:P * r + P] for r in range(4)]
                sources = [[p[:, c0:c0 + P] for c0 in (SBQ, SBQ + P, SBK, SBK + P)], pairs,
                           [p[:, c0:c0 + P] for c0 in (KS, KW, KC, VC)],
                           [p[:, c0:c0 + P] for c0 in (CQ, CQ + P, CKV)]]
                for b, group in enumerate(sources):
                    key = (L, "xt", t, b)
                    bank_taken_over(pe, key)
                    for j, src in enumerate(group):
                        ins = turn(ps[:, bank(key), P * j:P * j + P], src, ident[:, :])
                    done(ins, key)

            def latent_up(L, t):
                small = slot_view(slot_of((L, "small")), 1, 1536)[:, 0, :]
                bank_read(pe, (L, "xt", t, 3))
                weights_landed(pe, (L, "small"))
                key = (L, "uq", t)
                bank_taken_over(pe, key)
                for k in range(2):
                    ins = mm(ps[:, bank(key), 0:384], xT[:, 10 + k, P * t:P * t + P], small[:, 384 * k:384 * k + 384],
                             start=(k == 0), stop=(k == 1))
                done(ins, key)
                key = (L, "ukv", t)
                bank_taken_over(pe, key)
                done(mm(ps[:, bank(key), :], xT[:, 12, P * t:P * t + P], small[:, 768:1280], start=True, stop=True), key)

            def compress_hidden(L):
                key = (L, "c1")
                bank_taken_over(pe, key)
                for t in range(NT):
                    bank_read(pe, (L, "xt", t, 2))
                for kv in range(2):
                    weights_landed(pe, (L, "w1", kv))
                    w1 = slot_view(slot_of((L, "w1", kv)), 16, 256)
                    for hc in range(2):
                        o = (2 * kv + hc) * 45
                        for c in range(16):
                            ins = mm(ps[:, bank(key), o:o + 45], w1[:, c, P * hc:P * hc + P],
                                     cmp_x[:, kv, :, c:c + 8 * (N_CMP - 1) + 1:8], start=(c == 0), stop=(c == 15))
                done(ins, key)

            def compress_out(L):
                key = (L, "c2")
                small = slot_view(slot_of((L, "small")), 1, 1536)[:, 0, :]
                bank_taken_over(pe, key)
                pe.wait_ge(ch_act, L + 1)
                for kv in range(2):
                    for g in range(2):
                        o = (2 * kv + g) * HD
                        for hc in range(2):
                            w = 1280 + P * kv + HD * hc
                            ins = mm(ps[0:N_CMP, bank(key), o:o + HD], ch[:, 2 * kv + hc, N_CMP * g:N_CMP * g + N_CMP],
                                     small[:, w:w + HD], start=(hc == 0), stop=(hc == 1))
                done(ins, key)

            def job_scores(L, j):
                kind, i, r = JOBS[j]
                nk = P * (i + 1)
                key = (L, "s", j)
                bank_taken_over(pe, key)
                for h in range(2):
                    o = ps[:, bank(key), h * nk:h * nk + nk]
                    if kind == "mla":
                        ins = mm(o, mT[0:MQ, 2 * r + h, P * i:P * i + P], mT[0:MQ, 4 + 2 * r + h, 0:nk], start=True, stop=True)
                    else:
                        row = (8 if kind == "sel" else 9) + 2 * h
                        ins = mm(o, xT[:, 4 + r, P * i:P * i + P], xT[:, row, 0:nk], start=True, stop=True)
                done(ins, key)

            def job_turn(L, j):
                kind, i, r = JOBS[j]
                nk = P * (i + 1)
                n = len(JOBS) * L + j
                key = (L, "p", j)
                bank_taken_over(pe, key)
                pe.wait_ge(probs_ready, n + 1)
                for c in range(2 * (i + 1)):
                    ins = turn(ps[:, bank(key), P * c:P * c + P], probs[:, n % 3, P * c:P * c + P], ident[:, :])
                done(ins, key)

            def compressed_turn(L, i):
                pe.wait_ge(cmp_p, NT * L + i + 1)
                for half in range(2):
                    key = (L, "pc", i, half)
                    bank_taken_over(pe, key)
                    for h in range(4):
                        ins = turn(ps[0:N_CMP, bank(key), P * h:P * h + P], pcs[:, i, 4 * half + h, 0:N_CMP], ident[:, :])
                    done(ins, key)

            def job_value(L, j):
                kind, i, r = JOBS[j]
                n = len(JOBS) * L + j
                key = (L, "mlao", i, r) if kind == "mla" else (L, "nsao", i, r)
                if kind != "win":
                    bank_taken_over(pe, key)
                bank_read(pe, (L, "p", j))
                if kind == "win" and r == 0:
                    for h in range(2):
                        bank_read(pe, (L, "pc", i, h))
                for h in range(2):
                    o = ps[64 * h:64 * h + 64, bank(key), 0:P]
                    for kc in range(i + 1):
                        if kind == "mla":
                            v = mv[:, kc, 2 * r + h, :]
                        else:
                            v0 = (VS if kind == "sel" else VW) + HD * h
                            v = proj[:, kc, v0:v0 + HD]
                        c = h * (i + 1) + kc
                        ins = mm(o, v, probsT[:, n % 2, P * c:P * c + P], start=(kind != "win" and kc == 0),
                                 stop=(kind == "mla" and kc == i))
                    if kind == "win":
                        ins = mm(o, ckv_c[0:N_CMP, 2 + h, :], pcT[0:N_CMP, 4 * h + r, :], start=False, stop=True)
                ins.then_inc(pv_done, 1)

            def mixers(L):
                turned_norm(L, "norm1")
                for c in range(6):
                    for t in range(NT):
                        project(L, c, t)
                for t in range(NT):
                    turn_mixer_inputs(L, t)
                for t in range(NT):
                    project(L, 6, t)
                for t in range(NT):
                    latent_up(L, t)
                compress_hidden(L)
                for t in range(NT):
                    bank_read(pe, (L, "xt", t, 0))
                for h in range(4):
                    key = (L, "z", h)
                    bank_taken_over(pe, key)
                    r = slice(64 * (h % 2), 64 * (h % 2) + 64)
                    mm(ps[:, bank(key), 0:SEQ], xT[r, 2 + h // 2, 0:P], xT[r, h // 2, :], start=True, stop=True)
                    done(mm(ps[:, bank(key), SEQ:SEQ + P], xT[r, 2 + h // 2, P:SEQ], xT[r, h // 2, P:SEQ],
                            start=True, stop=True), key)
                compress_out(L)
                for t in range(NT):
                    project(L, 7, t)
                key = (L, "kct")
                bank_taken_over(pe, key)
                pe.wait_ge(ck_ready, L + 1)
                done(turn(ps[:, bank(key), 0:N_CMP], ckv_c[0:N_CMP, 0:2, :].rearrange("p g d -> p (g d)"),
                          ident[0:N_CMP, 0:N_CMP]), key)
                for t in range(NT):
                    pe.wait_ge(mla_ready, NT * L + t + 1)
                    for b in range(2):
                        key = (L, "mt", t, b)
                        bank_taken_over(pe, key)
                        for j in range(4):
                            ins = turn(ps[0:MQ, bank(key), P * j:P * j + P], mqk[:, t, 4 * b + j, :], ident[:, :])
                        done(ins, key)
                pe.wait_ge(stick_sp, L + 1)
                for h in range(4):
                    key = (L, "S", h)
                    bank_taken_over(pe, key)
                    b = ps[:, bank(key), :]
                    mm(b[:, 0:SEQ], tri_ge[:, :], stick_tmp[:, h, 0:SEQ], start=True, stop=False)
                    mm(b[:, P:SEQ], ones[:, :], stick_tmp[:, h, SEQ:SEQ + P], start=False, stop=True)
                    done(mm(b[:, SEQ:SEQ + P], tri_ge[:, :], stick_tmp[:, h, SEQ:SEQ + P], start=True, stop=True), key)
                if L == 0:
                    pe.wait_ge(bias_in, 16)
                    for h in range(8):
                        key = (0, "flip", h)
                        bank_taken_over(pe, key)
                        done(mm(ps[:, bank(key), 0:384], flip, bias[:, h, :], start=True, stop=True), key)
                bank_read(pe, (L, "kct"))
                pe.wait_ge(keys_split, L + 1)
                for i in range(NT):
                    key = (L, "sc", i)
                    bank_taken_over(pe, key)
                    for h in range(8):
                        g, r = h // 4, h % 4
                        ins = mm(ps[:, bank(key), 16 * h:16 * h + N_CMP], xT[:, 4 + r, P * i:P * i + P],
                                 kcT[:, g, 0:N_CMP], start=True, stop=True)
                    done(ins, key)
                pe.wait_ge(stick_w, L + 1)
                for hp in range(2):
                    key = (L, "sbo", hp)
                    bank_taken_over(pe, key)
                    for a_ in range(2):
                        h = 2 * hp + a_
                        o = ps[64 * a_:64 * a_ + 64, bank(key), :]
                        v0 = SBV + HD * h
                        mm(o[:, 0:SEQ], proj[:, 0, v0:v0 + HD], stick[:, h, 0:SEQ], start=True, stop=False)
                        ins = mm(o[:, P:SEQ], proj[:, 1, v0:v0 + HD], stick[:, h, SEQ:SEQ + P], start=False, stop=True)
                    ins.then_inc(stick_out, 1)
                for t in range(NT):
                    for b in range(2):
                        bank_read(pe, (L, "mt", t, b))
                for s in range(STEPS):
                    if s < len(JOBS):
                        job_scores(L, s)
                    if 0 <= s - LAG_PV < len(JOBS):
                        job_value(L, s - LAG_PV)
                    j = s - LAG_TURN
                    if 0 <= j < len(JOBS):
                        for i in range(NT):
                            if j == FIRST_SPARSE[i]:
                                compressed_turn(L, i)
                        job_turn(L, j)
                    if s in LATE_GATES:
                        project(L, *LATE_GATES[s])
                for r in (2, 3):
                    bank_read(pe, (L, "nsao", NT - 1, r))
                for k in range(2):
                    weights_landed(pe, (L, "wo", k))
                wo = [slot_view(slot_of((L, "wo", k)), 4, D) for k in range(2)]
                for t in range(NT):
                    for h in range(2):
                        for m, ks in enumerate(((0, 1), (2, 3, 4, 5), (6, 7))):
                            key = (L, "y", t, h, m)
                            bank_taken_over(pe, key)
                            for k in ks:
                                ins = mm(ps[:, bank(key), :], yT[:, k, P * t:P * t + P],
                                         wo[k // 4][:, k % 4, 512 * h:512 * h + 512], start=(k == ks[0]), stop=(k == ks[-1]))
                            done(ins, key)
                for t in range(NT):
                    for h in range(2):
                        pe.wait_ge(merged, 4 * L + 2 * t + h + 1)
                        turn_residual((L, "merge", t, h), t, h)
                for k in range(2):
                    weights_landed(pe, (L, "wout", k))
                wout = [slot_view(slot_of((L, "wout", k)), 4, D) for k in range(2)]
                for t in range(NT):
                    for h in range(2):
                        bank_read(pe, (L, "merge", t, h))
                    for h in range(2):
                        key = (L, "out", t, h)
                        bank_taken_over(pe, key)
                        for k in range(KD):
                            ins = mm(ps[:, bank(key), :], hT[:, k, P * t:P * t + P],
                                     wout[k // 4][:, k % 4, 512 * h:512 * h + 512], start=(k == 0), stop=(k == KD - 1))
                        done(ins, key)
                turned_norm(L, "norm2")

            def ffn_in(n, lhs, wv, w, b, taken, landed, signal):
                if not isinstance(n, int) or n > 0:
                    pe.wait_ge(taken, n)
                landed()
                for k in range(KD):
                    ins = mm(ps[:, b, 0:w], lhs(k), wv[:, k, :], start=(k == 0), stop=(k == KD - 1))
                ins.then_inc(signal, 1)

            def ffn_turn(n, w):
                pe.wait_ge(act_ready, n + 1)
                if not isinstance(n, int) or n > 0:
                    pe.wait_ge(actT_ready, n)
                for j in range(w // P):
                    ins = turn(ps[:, 0, P * j:P * j + P], act[:, P * j:P * j + P], ident[:, :])
                ins.then_inc(act_turned, 1)

            def ffn_down(n, wv, w, b, first, last, landed):
                pe.wait_ge(actT_ready, n + 1)
                landed()
                for k in range(w // P):
                    for h in range(2):
                        ins = mm(ps[:, b + h, :], actT[:, P * k:P * k + P], wv[:, k, 512 * h:512 * h + 512],
                                 start=(first and k == 0), stop=(last and k == w // P - 1))
                ins.then_inc(down_done, 1)

            mixers(0)

            def dense_in(u, kind, b, taken, signal):
                g, t = u // NT, u % NT
                w = DENSE_GROUPS[g][1]
                key = (0, kind, g)
                if u < NT and kind == "gate":
                    for h in range(2):
                        bank_read(pe, (0, "norm2", t, h))
                ffn_in(u, lambda k: hT[:, k, P * t:P * t + P], slot_view(slot_of(key), KD, w), w, b, taken,
                       lambda: weights_landed(pe, key), signal)

            def dense_down(u):
                g, t = u // NT, u % NT
                w = DENSE_GROUPS[g][1]
                key = (0, "down", g)
                ffn_down(u, slot_view(slot_of(key), w // P, D), w, 4 + 2 * t, g == 0, g == len(DENSE_GROUPS) - 1,
                         lambda: weights_landed(pe, key))

            for u in range(DENSE_UNITS + 1):
                if u < DENSE_UNITS:
                    dense_in(u, "gate", 2, silu_done, gate_done)
                if u:
                    ffn_turn(u - 1, DENSE_GROUPS[(u - 1) // NT][1])
                if u < DENSE_UNITS:
                    dense_in(u, "up", 3, act_ready, up_done)
                if u:
                    dense_down(u - 1)
            mixers(1)

            for t in range(NT):
                for h in range(2):
                    bank_read(pe, (DEPTH - 1, "norm2", t, h))
            for t in range(NT):
                for k in range(KD):
                    ins = mm(ps[:, 1, 8 * t:8 * t + 8], hT[:, k, P * t:P * t + P], router[:, k, :],
                             start=(k == 0), stop=(k == KD - 1))
            ins.then_inc(route_pe, 1)
            pe.wait_ge(route_dve, 2)
            pe.wait_ge(consts_ready, 2)
            sel = route[:, 5]
            mm(ps[:, 1, 0:8], tri_lt, sel[:, 0, :], start=True, stop=True)
            mm(ps[:, 1, 8:16], ones[:, :], sel[:, 0, :], start=True, stop=False)
            mm(ps[:, 1, 8:16], tri_lt, sel[:, 1, :], start=False, stop=True)
            mm(ps[:, 1, 16:24], ones[:, :], sel[:, 0, :], start=True, stop=False)
            mm(ps[:, 1, 16:24], ones[:, :], sel[:, 1, :], start=False, stop=True).then_inc(route_pe, 1)

            def gather(it, h, first=False):
                if h == 0:
                    pe.wait_ge(pick_ready, it + 1)
                if not first:
                    pe.wait_ge(added, it * 4 - 3)
                for j in range(4):
                    k = 4 * h + j
                    for t in range(NT):
                        ins = mm(ps[:, 6 + h, P * j:P * j + P], xn[:, t, P * k:P * k + P], pick[:, t, :],
                                 start=(t == 0), stop=(t == NT - 1))
                ins.then_inc(gathered, 1)

            def turn_put(it, first=False):
                if not first:
                    pe.wait_ge(putT_ready, it)
                for t in range(NT):
                    ins = turn(ps[:, 1, P * t:P * t + P], put[:, t, :], ident[:, :])
                ins.then_inc(put_turned, 1)

            gather(0, 0, True)
            gather(0, 1, True)
            pe.wait_ge(routed, 2)
            turn_put(0, True)
            pe.sem_inc(spread, 1)

            def expert(it):
                n0 = it * EXPERT_UNITS + DENSE_UNITS
                place = {key: m for m, key in enumerate(EXPERT_CHUNKS)}

                def landed(key):
                    m = place[key]
                    s = m % MOE_RING
                    per = len(EXPERT_CHUNKS) // MOE_RING
                    pe.wait_ge(slot_full[s], it * (16 * per) + (slot_total[s] + 16 * (m // MOE_RING + 1)))

                def unit_in(u, kind, b, taken, signal):
                    key = (kind, u)
                    ffn_in(n0 + u, lambda k: hTe[:, k, :], slot_view(place[key] % MOE_RING, KD, 512), 512, b, taken,
                           lambda: landed(key), signal)

                def unit_down(u):
                    key = ("down", u)
                    if u == 0:
                        pe.wait_ge(ye_ready, it + 1)
                    ffn_down(n0 + u, slot_view(place[key] % MOE_RING, 4, D), 512, 4, u == 0, u == EXPERT_UNITS - 1,
                             lambda: landed(key))

                pe.wait_ge(hTe_ready, it * 2 + 2)
                unit_in(0, "gate", 2, silu_done, gate_done)
                unit_in(0, "up", 3, act_ready, up_done)
                for u in range(1, EXPERT_UNITS):
                    unit_in(u, "gate", 2, silu_done, gate_done)
                    ffn_turn(n0 + (u - 1), 512)
                    unit_in(u, "up", 3, act_ready, up_done)
                    unit_down(u - 1)
                gather(it + 1, 0)
                ffn_turn(n0 + (EXPERT_UNITS - 1), 512)
                gather(it + 1, 1)
                unit_down(EXPERT_UNITS - 1)
                pe.wait_ge(ye_ready, it + 2)
                pe.wait_ge(putT_ready, it + 1)
                for k in range(4):
                    t, h = k // 2, k % 2
                    if k < 2:
                        pe.wait_ge(hTe_ready, it * 2 + (3 + k))
                    else:
                        pe.wait_ge(added, it * 4 + k)
                    mm(ps[:, 6 + k % 2, :], putT[:, P * t:P * t + P], ye[:, 512 * h:512 * h + 512],
                       start=True, stop=True).then_inc(spread, 1)
                turn_put(it + 1)

            with pe.Fori(0, N_EXPERTS) as it:
                expert(it)
            crowded = pe.value_load(flag_i[0:1, 0:1], min_val=0, max_val=1)
            with pe.If(crowded > 0):
                with pe.Fori(N_EXPERTS, 2 * N_EXPERTS) as it:
                    expert(it)


_INS = ['x', 'rel_bias_table', 'mix_norm', 'w_in', 'b_gate', 'sb_w_o', 'nsa_q_norm', 'nsa_k_norm', 'nsa_cmp_pos',
        'nsa_cmp_w1', 'nsa_cmp_w2', 'nsa_w_o', 'mla_q_a_norm', 'mla_kv_a_norm', 'mla_w_uq', 'mla_w_ukv', 'mla_q_norm',
        'mla_k_norm', 'mla_w_o', 'w_out', 'ffn_norm', 'dense_w_gate', 'dense_w_up', 'dense_w_down', 'moe_router',
        'moe_w_gate', 'moe_w_up', 'moe_w_down']


def shape_constants():
    import math
    import numpy as np
    rel = np.arange(SEQ)
    n = np.maximum(rel, 1).astype(np.float32)
    large = 16 + (np.log(n / np.float32(16)) / np.float32(math.log(1024 / 16)) * np.float32(16)).astype(np.int32)
    bucket = np.where(rel < 16, rel, np.minimum(large, 31))
    onehot = np.zeros((33, 512), np.float32)
    for j in range(512):
        d = SEQ - 1 - j
        onehot[bucket[d] if d >= 0 else 32, j] = 1.0
    inv = np.float32(10000.0) ** (-np.arange(16, dtype=np.float32) / np.float32(16))
    ang = np.arange(SEQ, dtype=np.float32)[:, None] * inv[None, :]
    trig = np.stack([np.cos(ang), np.sin(ang)]).astype(np.float32)
    return onehot, np.ascontiguousarray(trig.reshape(2, NT, P, 16).transpose(2, 0, 1, 3))


def kernel(**inputs):
    import numpy as _np
    import concourse.bacc as _bacc
    from concourse import mybir as _mybir
    from concourse.bass_utils import run_bass_kernel_spmd as _run

    nc = _bacc.Bacc("TRN2", target_bir_lowering=False, num_devices=1)
    arrays, args = {}, {}
    onehot, trig = shape_constants()
    for name, arr in [(n, inputs[n]) for n in _INS] + [("bucket_onehot", onehot), ("rope_tables", trig)]:
        v = _np.ascontiguousarray(arr)
        arrays[f"in_{name}_dram"] = v
        args[name] = nc.dram_tensor(f"in_{name}_dram", v.shape, _mybir.dt.from_np(v.dtype), kind="ExternalInput").ap()
    out = nc.dram_tensor("out_0_dram", (1, SEQ, D), _mybir.dt.float32, kind="ExternalOutput").ap()
    trunk(nc, args, out)
    r = _run(nc, [arrays], core_ids=[0])
    return r.results[0]["out_0_dram"]
```

```python
from contextlib import ExitStack

import concourse.bass as bass
from concourse import mybir

ALU = mybir.AluOpType
ACT = mybir.ActivationFunctionType
F32 = mybir.dt.float32
F32R = mybir.dt.float32r
U32 = mybir.dt.uint32
I32 = mybir.dt.int32
AX = mybir.AxisListType

P = 128
SEQ, D = 256, 1024
NT = SEQ // P
KD = D // P
DEPTH = 2
HD = 64
EPS = 1e-6
NEG = -1e30

SBQ, SBK, SBV = 0, 256, 512
NQ, KC, VC, KS, VS, KW, VW, NG = 768, 1280, 1408, 1536, 1664, 1792, 1920, 2048
CQ, CKV, KR, GATES = 2072, 2328, 2456, 2488
IN_COLS = 5560
CHUNKS = [(c, min(512, GATES - c)) for c in range(0, GATES, 512)] + [(c, 512) for c in range(GATES, IN_COLS, 512)]
N_MIX_CHUNKS = 5

N_CMP = 15
MQ = 96
FF_DENSE, FF_EXPERT, N_EXPERTS = 2816, 3584, 8
EXPERT_UNITS = FF_EXPERT // 512
DENSE_GROUPS = [(f, min(512, FF_DENSE - f)) for f in range(0, FF_DENSE, 512)]

SLOT = 4096
RING = 4
MOE_RING = 6

JOBS = ([("mla", i, hp) for i in range(NT) for hp in range(2)]
        + [(kind, i, r) for i in range(NT) for r in range(4) for kind in ("sel", "win")])
FIRST_SPARSE = {i: JOBS.index(("sel", i, 0)) for i in range(NT)}
LAG_TURN, LAG_PV = 2, 3
STEPS = len(JOBS) + LAG_PV
LATE_GATES = {2 + 3 * n: (8 + n // 2, n % 2) for n in range(6)}


def pool_plan(order, banks):
    assert len(set(order)) == len(order)
    return {key: (banks[k % len(banks)], k // len(banks)) for k, key in enumerate(order)}


def bank_uses():
    turn, proj, score, outp = [], [], [], []
    for L in range(DEPTH):
        turn += [(L, "norm1", t, h) for t in range(NT) for h in range(2)]
        turn += [(L, "xt", t, b) for t in range(NT) for b in range(4)]
        turn += [(L, "kct")]
        turn += [(L, "mt", t, b) for t in range(NT) for b in range(2)]
        for j, (kind, i, r) in enumerate(JOBS):
            if j == FIRST_SPARSE[i]:
                turn += [(L, "pc", i, h) for h in range(2)]
            turn += [(L, "p", j)]
        turn += [(L, "merge", t, h) for t in range(NT) for h in range(2)]
        turn += [(L, "norm2", t, h) for t in range(NT) for h in range(2)]
        proj += [(L, "proj", c, t) for c in range(7) for t in range(NT)]
        proj += [(L, w, t) for t in range(NT) for w in ("uq", "ukv")]
        proj += [(L, "c1"), (L, "c2")]
        proj += [(L, "proj", 7, t) for t in range(NT)]
        proj += [(L, "proj", *LATE_GATES[s]) for s in sorted(LATE_GATES)]
        proj += [(L, "y", t, h, m) for t in range(NT) for h in range(2) for m in range(3)]
        proj += [(L, "out", t, h) for t in range(NT) for h in range(2)]
        score += [(L, "z", h) for h in range(4)] + [(L, "S", h) for h in range(4)]
        score += [(L, "sc", i) for i in range(NT)] + [(L, "s", j) for j in range(len(JOBS))]
        if L == 0:
            outp += [(L, "flip", h) for h in range(8)]
        outp += [(L, "sbo", hp) for hp in range(2)] + [(L, "mlao", i, hp) for i in range(NT) for hp in range(2)]
        outp += [(L, "nsao", i, r) for i in range(NT) for r in range(4)]
    plan = {}
    for order, banks in ((turn, (0, 1)), (proj, (2, 3)), (score, (4, 5)), (outp, (6, 7))):
        plan.update(pool_plan(order, banks))
    return plan


def weight_chunks():
    seq = []
    for L in range(DEPTH):
        seq += [(L, "in", c) for c in range(7)] + [(L, "small"), (L, "w1", 0), (L, "w1", 1)]
        seq += [(L, "in", c) for c in range(7, 11)] + [(L, "wo", 0), (L, "wo", 1), (L, "wout", 0), (L, "wout", 1)]
        if L == 0:
            seq += [(L, kind, g) for kind, g in DENSE_CHUNKS]
    return seq




def ffn_chunks(units):
    seq = [("gate", 0), ("up", 0)]
    for u in range(1, units):
        seq += [("gate", u), ("down", u - 1), ("up", u)]
    return seq + [("down", units - 1)]


DENSE_CHUNKS = ffn_chunks(len(DENSE_GROUPS))
EXPERT_CHUNKS = ffn_chunks(EXPERT_UNITS)
DENSE_HALVES = 2 * len(DENSE_CHUNKS)
EXPERT_HALVES = 2 * len(EXPERT_CHUNKS)
PAIRS = N_EXPERTS // 2
SPREAD_BANKS = (6, 7, 4, 5)
PAIR = 2
SPLIT_BUFS = 3
PASSES_OF_RING = PAIR * len(EXPERT_CHUNKS) // MOE_RING
assert PASSES_OF_RING * MOE_RING == PAIR * len(EXPERT_CHUNKS) and DENSE_HALVES % SPLIT_BUFS == 0 and EXPERT_HALVES % SPLIT_BUFS == 0

G_MIX, G_FFN, G_LAYER = 0, DEPTH * KD, 2 * DEPTH * KD
G_Q, G_KCMP, G_KSEL, G_KWIN, G_QA, G_KVA, G_PER_LAYER = 0, 1, 2, 3, 4, 6, 7
G_ROWS = G_LAYER + DEPTH * G_PER_LAYER
SMALL_IN = 16 * (9 + 8 * DEPTH)


def trunk(nc, a, out):
    uses = bank_uses()
    chunk_seq = weight_chunks()
    chunk_no = {key: n for n, key in enumerate(chunk_seq)}
    slot_no = {key: n % RING for n, key in enumerate(chunk_seq)}

    with ExitStack() as ctx:
        def sb(name, shape, dt=F32):
            return ctx.enter_context(nc.sbuf_tensor(name, shape, dt))

        def sem(name):
            return ctx.enter_context(nc.semaphore(name))

        ps = ctx.enter_context(nc.psum_tensor("ps", [P, 8, 512], F32))

        PROJ0 = RING * SLOT
        BIAS0 = PROJ0 + NT * IN_COLS
        TMP0 = BIAS0 + 8 * 384
        CMP0 = TMP0 + 1536
        MT0 = CMP0 + 768
        PROBST0 = MT0 + 2048
        PCT0 = PROBST0 + 1024
        arena_at = -(-nc.sbuf_base // 32) * 32
        arena = sb("arena", [P, PCT0 + 1024])
        proj = arena[:, PROJ0:BIAS0].rearrange("p (t n) -> p t n", t=NT)
        bias = arena[:, BIAS0:TMP0].rearrange("p (h k) -> p h k", h=8)
        tmp = arena[:, TMP0:CMP0]
        cmp_x = arena[:, CMP0:MT0].rearrange("p (v g n) -> p v g n", v=2, g=3)
        mT = arena[:, MT0:PROBST0].rearrange("p (h q) -> p h q", h=8)
        probsT = arena[:, PROBST0:PCT0].rearrange("p (b n) -> p b n", b=2)
        pcT = arena[:, PCT0:].rearrange("p (h q) -> p h q", h=8)

        def rounded(name, shape, at):
            return nc.alloc_sbuf_tensor_at(name, shape, F32R, offset=arena_at + 4 * at)

        w_hi = [rounded(f"w_hi{b}", [P, SLOT // 2], PROJ0 + b * (SLOT // 2)) for b in range(2)]
        w_lo = [rounded(f"w_lo{b}", [P, SLOT // 2], PROJ0 + SLOT + b * (SLOT // 2)) for b in range(2)]
        h_hi = rounded("h_hi", [P, KD, SEQ], PROJ0 + 2 * SLOT)
        h_lo = rounded("h_lo", [P, KD, SEQ], MT0)
        e_hi = rounded("e_hi", [P, KD, P], MT0)
        e_lo = rounded("e_lo", [P, KD, P], MT0 + 1024)
        a_hi = rounded("a_hi", [P, 2, 512], PROBST0)
        a_lo = rounded("a_lo", [P, 2, 512], PCT0)
        slot_at = [n * SLOT for n in range(RING)] + [PROJ0 + 2 * SLOT, PROJ0 + 3 * SLOT]
        slot_order = [slot_no[DEPTH - 1, kind, k] for kind in ("wo", "wout") for k in range(2)] + [RING, RING + 1]
        assert sorted(slot_order) == list(range(MOE_RING))
        assert PROJ0 + 4 * SLOT <= MT0 and PROJ0 + 2 * SLOT + 2048 <= BIAS0
        x = sb("x", [P, NT, D])
        xn = sb("xn", [P, NT, D])
        hT = sb("hT", [P, KD, SEQ])
        xT = sb("xT", [P, 13, SEQ])
        heads_at = -(-nc.sbuf_base // 32) * 32
        heads = sb("heads", [P, NT * 8 * MQ + NT * 4 * HD])
        mqk = heads[:, 0:NT * 8 * MQ].rearrange("p (t h d) -> p t h d", t=NT, h=8)
        mv = heads[:, NT * 8 * MQ:].rearrange("p (t h d) -> p t h d", t=NT, h=4)
        probs = mqk[:, :, :, :].rearrange("p t h d -> p (t h d)").rearrange("p (b n) -> p b n", b=3)
        pcs = cmp_x[:, 0, 0:2, :].rearrange("p g (h n) -> p g h n", h=8)
        yT_at = -(-nc.sbuf_base // 32) * 32
        yT = sb("yT", [P, 8, SEQ])
        w_hi.append(nc.alloc_sbuf_tensor_at("w_hi2", [P, SLOT // 2], F32R, offset=heads_at))
        w_lo.append(nc.alloc_sbuf_tensor_at("w_lo2", [P, SLOT // 2], F32R, offset=yT_at))
        ident = sb("ident", [P, P])
        tri_ge = sb("tri_ge", [P, P])
        ones = sb("ones", [P, P])
        stick_mask = sb("stick_mask", [P, 384])
        causal = sb("causal", [P, SEQ])
        gain_rows = pcT[:, 0, :]
        pos_rows = pcT[0:64, 1, :]
        rope_tmp = pcT[:, 0:4, :]
        flip = pcT[:, 4, :]
        gains = sb("gains", [P, 64])
        posT = sb("posT", [P, 4, 16])
        mla_gain = sb("mla_gain", [P, DEPTH, 2, MQ])
        trig = sb("trig", [P, 2, NT, 16])
        bgate = sb("bgate", [12, 512])
        router = sb("router", [P, KD, N_EXPERTS])
        table = sb("table", [64, 8])
        sums = sb("sums", [P, NT, 20])
        inv_n = sb("inv_n", [P, 20])
        mhalf = sb("mhalf", [P, 20])
        ssum = sb("ssum", [P, NT])
        msum = sb("msum", [P, NT, 8])
        ksum = sb("ksum", [P, 2])
        nmax = sb("nmax", [P, 3, 2])
        prob_sum = sb("prob_sum", [P, 3, 2])
        prec = sb("prob_scale", [P, 3, 2])
        ngate = sb("ngate", [P, NT, 24])
        cmax = sb("cmax", [P, 8])
        csum = sb("csum", [P, 8])
        valid = sb("valid", [P, NT])
        early = yT[:, :, :].rearrange("p a b -> p (a b)")
        ch_raw, ch, ce = (early[:, o:o + 4 * n].rearrange("p (f n) -> p f n", f=4) for o, n in ((0, 45), (180, 30), (300, 30)))
        ckv_c = cmp_x[0:16, 1, 0:2, :].rearrange("p g (f d) -> p (g f) d", f=2)
        csq = early[0:16, 512:640].rearrange("p (g d) -> p g d", g=2)
        kcT = sb("kcT", [P, 2, 16])
        NS = 2 * N_EXPERTS + 1
        xTf = xT[:, :, :].rearrange("p a b -> p (a b)")
        slots, comb = (xTf[:, o:o + NT * NS].rearrange("p (t e) -> p t e", t=NT) for o in (0, 64))
        route = xTf[:, 128:320].rearrange("p (v t e) -> p v t e", v=12, t=NT)
        top_i = sb("top_i", [P, NT, 8], U32)
        flag = sb("flag", [P, 2])
        flag_i = sb("flag_i", [P, 1], I32)
        now = sb("now", [P, 4])
        ye = xTf[:, 1024:2048]
        pick = xTf[:, 2048:2304].rearrange("p (t s) -> p t s", t=NT)
        put = xTf[:, 2304:2560].rearrange("p (t s) -> p t s", t=NT)
        putT = xTf[:, 2560:2816]
        iota = xTf[:, 2816:2944]
        tri_lt = xTf[:, 2944:3072]
        iota8 = xTf[:, 3072:3080]
        hTf = hT[:, :, :].rearrange("p k q -> p (k q)")
        act_g, act = (hTf[:, o:o + 1024].rearrange("p (b n) -> p b n", b=2) for o in (0, 1024))
        gathered_f = [hTf[:, o:o + 512] for o in (512, 1536)]
        stick = xn[:, :, :].rearrange("p a b -> p (a b)")[:, 0:1536].rearrange("p (h k) -> p h k", h=4)
        stick_tmp = tmp.rearrange("p (h k) -> p h k", h=4)
        rvec = tmp[0:8, 0:512]
        onehot = tmp[0:33, 512:1024]
        bias_dram = nc.dram_tensor("bias_by_distance", (8, 512), F32, kind="Internal").ap()

        bank_full = [sem(f"bank{b}_full") for b in range(8)]
        bank_free = [sem(f"bank{b}_free") for b in range(8)]
        slot_full = [sem(f"slot{s}_full") for s in range(MOE_RING)]
        small_in = sem("small_in")
        consts_ready = sem("consts_ready")
        bias_out, bias_in = sem("bias_out"), sem("bias_in")
        v_done, a_done, g_done = sem("vector_done"), sem("scalar_done"), sem("gpsimd_done")
        setup_pe, setup_dve = sem("setup_pe"), sem("setup_dve")
        sq_ready, sums_ready, rstd_ready, xn_ready = sem("sq_ready"), sem("sums_ready"), sem("rstd_ready"), sem("xn_ready")
        head_sq, head_sums, head_rstd, heads_normed = sem("head_sq"), sem("head_sums"), sem("head_rstd"), sem("heads_normed")
        cmp_x_ready = sem("cmp_x_ready")
        mla_in, mla_rope_in, mla_sq, mla_sums, mla_rstd, mla_ready = (
            sem("mla_in"), sem("mla_rope_in"), sem("mla_sq"), sem("mla_sums"), sem("mla_rstd"), sem("mla_ready"))
        ng_exp = sem("ng_exp")
        stick_out = sem("stick_out")
        keys_split = sem("keys_split")
        ch_ready, ch_exp, ch_act = sem("ch_ready"), sem("ch_exp"), sem("ch_act")
        ck_sums, ck_rstd, ck_ready = sem("ck_sums"), sem("ck_rstd"), sem("ck_ready")
        stick_z, stick_ln, stick_sp, stick_t, stick_w = (
            sem("stick_z"), sem("stick_ln"), sem("stick_sp"), sem("stick_t"), sem("stick_w"))
        cmp_s, cmp_e, cmp_p = sem("cmp_s"), sem("cmp_e"), sem("cmp_p")
        max_ready, exp_ready, probs_ready, pv_done = sem("max_ready"), sem("exp_ready"), sem("probs_ready"), sem("pv_done")
        gates_ready, merged, x_mixed = sem("gates_ready"), sem("merged"), sem("x_mixed")
        h_hi_ready, h_lo_ready = sem("h_hi_ready"), sem("h_lo_ready")
        hi_ready, lo_ready = sem("hi_ready"), sem("lo_ready")
        half_done = sem("half_done")
        silu_done, act_ready = sem("silu_done"), sem("act_ready")
        act_turned, a_hi_ready, a_lo_ready = sem("act_turned"), sem("a_hi_ready"), sem("a_lo_ready")
        x_dense = sem("x_dense")
        route_pe, route_dve, route_exp, routed = sem("route_pe"), sem("route_dve"), sem("route_exp"), sem("routed")
        now_ready, pick_ready = sem("now_ready"), sem("pick_ready")
        gathered, gains_applied, e_hi_ready, e_lo_ready = sem("gathered"), sem("gains_applied"), sem("e_hi_ready"), sem("e_lo_ready")
        put_turned, putT_ready = sem("put_turned"), sem("putT_ready")
        ye_ready, ye_copied, spread, added = sem("ye_ready"), sem("ye_copied"), sem("spread"), sem("added")
        x_final, out_done = sem("x_final"), sem("out_done")

        def bank(key):
            return uses[key][0]

        def bank_taken_over(pe, key):
            b, n = uses[key]
            if n > 0:
                pe.wait_ge(bank_free[b], n)

        def bank_written(eng, key):
            b, n = uses[key]
            eng.wait_ge(bank_full[b], n + 1)

        def bank_read(eng, key):
            b, n = uses[key]
            eng.wait_ge(bank_free[b], n + 1)

        def slot_of(key):
            return slot_no[key]

        landed_value, slot_total = [], [0] * MOE_RING
        for n, key in enumerate(chunk_seq):
            slot_total[n % RING] += 16 * {"small": 4, "wo": 3}.get(key[1], 1)
            landed_value.append(slot_total[n % RING])

        def weights_landed(pe, key):
            n = chunk_no[key]
            pe.wait_ge(slot_full[n % RING], landed_value[n])

        def expert_slot(n, k, w):
            o = slot_at[slot_order[n % MOE_RING]]
            return arena[:, o:o + k * w].rearrange("p (k w) -> p k w", k=k)

        def expert_landed(eng, pair, n):
            s = slot_order[n % MOE_RING]
            eng.wait_ge(slot_full[s], pair * (16 * PASSES_OF_RING) + (slot_total[s] + 16 * (n // MOE_RING + 1)))

        def chunk_shape(kind, w):
            return (w // P, D) if kind == "down" else (KD, w)

        def slot_view(s, k, w):
            return arena[:, s * SLOT:s * SLOT + k * w].rearrange("p (k w) -> p k w", k=k)

        block = ctx.enter_context(nc.Block())

        @block.sync
        def _(sp):
            def rows(ap):
                return ap.rearrange("(k p) n -> p k n", p=P)

            def chunk_free(key):
                L, kind = key[0], key[1]
                if kind == "in":
                    bank_written(sp, (L, "proj", key[2], NT - 1))
                elif kind in ("small", "w1"):
                    bank_written(sp, (L, "c2"))
                elif kind == "wo":
                    bank_written(sp, (L, "y", NT - 1, 1, 2))
                elif kind == "wout":
                    bank_written(sp, (L, "out", NT - 1, 1))
                else:
                    sp.wait_ge(lo_ready, 2 * DENSE_CHUNKS.index((kind, key[2])) + 2)

            for n, key in enumerate(chunk_seq):
                L, kind = key[0], key[1]
                if n >= RING:
                    chunk_free(chunk_seq[n - RING])
                s = n % RING
                full = slot_full[s]
                if kind == "in":
                    c0, w = CHUNKS[key[2]]
                    parts = [(slot_view(s, KD, w), rows(a["w_in"][L, :, c0:c0 + w]))]
                elif kind == "small":
                    v = slot_view(s, 1, 1536)[:, 0, :]
                    parts = [(v[:, 0:768].rearrange("p (k w) -> p k w", k=2), rows(a["mla_w_uq"][L])),
                             (v[:, 768:1280], a["mla_w_ukv"][L]),
                             (v[:, 1280:1408].rearrange("p (k w) -> p k w", k=2), rows(a["nsa_cmp_w2"][L, 0])),
                             (v[:, 1408:1536].rearrange("p (k w) -> p k w", k=2), rows(a["nsa_cmp_w2"][L, 1]))]
                elif kind == "w1":
                    parts = [(slot_view(s, 16, 256), rows(a["nsa_cmp_w1"][L, key[2]]))]
                elif kind == "wo":
                    v = slot_view(s, 4, D)
                    nsa = a["nsa_w_o"][L].rearrange("(g r d) n -> g d r n", g=2, r=4)
                    plain, pv, q0, qv = ((a["sb_w_o"][L], 0, 0, 2), (a["mla_w_o"][L], 2, 2, 0))[key[2]]
                    parts = [(v[:, pv:pv + 2, :], rows(plain))]
                    parts += [(v[64 * g:64 * g + 64, qv:qv + 2, :], nsa[g, :, q0:q0 + 2, :]) for g in range(2)]
                elif kind == "wout":
                    parts = [(slot_view(s, 4, D), rows(a["w_out"][L, 512 * key[2]:512 * key[2] + 512, :]))]
                elif kind in ("gate", "up"):
                    f, w = DENSE_GROUPS[key[2]]
                    parts = [(slot_view(s, KD, w), rows(a["dense_w_" + kind][0, :, f:f + w]))]
                else:
                    f, w = DENSE_GROUPS[key[2]]
                    parts = [(slot_view(s, w // P, D), rows(a["dense_w_down"][0, f:f + w, :]))]
                for dst, src in parts:
                    sp.dma_start(dst, src).then_inc(full, 16)

            def expert_loads(pair, first_expert, first=False):
                for o in range(PAIR):
                    for m, (kind, u) in enumerate(EXPERT_CHUNKS):
                        n = o * len(EXPERT_CHUNKS) + m
                        if not first or n >= MOE_RING:
                            sp.wait_ge(lo_ready, pair * (PAIR * EXPERT_HALVES) + (DENSE_HALVES + 2 * (n - MOE_RING + 1)))
                        elif n == 0:
                            bank_written(sp, (DEPTH - 1, "y", NT - 1, 1, 2))
                        elif n == 2:
                            bank_written(sp, (DEPTH - 1, "out", NT - 1, 1))
                        elif n == 4:
                            bank_read(sp, (DEPTH - 1, "out", NT - 1, 1))
                        e = first_expert + o
                        one = slice(e, e + 1) if first else bass.ds(e, 1)
                        if kind == "down":
                            src = a["moe_w_down"][0, one, 512 * u:512 * u + 512, :]
                        else:
                            src = a["moe_w_" + kind][0, one, :, 512 * u:512 * u + 512]
                        sp.dma_start(expert_slot(n, *chunk_shape(kind, 512)),
                                     src.rearrange("e (k p) n -> p (e k) n", p=P)).then_inc(slot_full[slot_order[n % MOE_RING]], 16)

            expert_loads(0, 0, first=True)
            with sp.Fori(1, PAIRS) as pair:
                expert_loads(pair, pair * PAIR)
            sp.wait_ge(routed, 2)
            crowded = sp.value_load(flag_i[0:1, 0:1], min_val=0, max_val=1)
            with sp.If(crowded > 0):
                with sp.Fori(PAIRS, 2 * PAIRS) as pair:
                    expert_loads(pair, pair * PAIR - N_EXPERTS)
            sp.wait_ge(x_final, 1)
            sp.dma_start(out[0].rearrange("(t p) d -> p t d", p=P), x[:, :, :]).then_inc(out_done, 16)
            sp.wait_ge(out_done, 16)

        @block.gpsimd
        def _(pool):
            g = [0]

            def link(ins):
                g[0] += 1
                ins.then_inc(g_done, 1)
                pool.wait_ge(g_done, g[0])

            link(nc.gpsimd.memset(gain_rows, 0.0))
            link(nc.gpsimd.memset(table[32:64, :], NEG))
            link(nc.gpsimd.memset(ident[:, :], 0.0))
            link(nc.gpsimd.affine_select(out=ident[:, :], in_=ident[:, :], compare_op=ALU.not_equal, fill=1.0,
                                         base=0, pattern=[[-1, P]], channel_multiplier=1))
            link(nc.gpsimd.memset(flip, 0.0))
            link(nc.gpsimd.affine_select(out=flip, in_=flip, compare_op=ALU.not_equal, fill=1.0,
                                         base=-(P - 1), pattern=[[1, P]], channel_multiplier=1))
            link(nc.gpsimd.memset(ones[:, :], 1.0))
            link(nc.gpsimd.affine_select(out=tri_ge[:, :], in_=ones[:, :], compare_op=ALU.is_ge, fill=0.0,
                                         base=0, pattern=[[-1, P]], channel_multiplier=1))
            link(nc.gpsimd.memset(stick_mask[:, :], 0.0))
            for c in (0, 256):
                link(nc.gpsimd.affine_select(out=stick_mask[:, c:c + P], in_=stick_mask[:, c:c + P],
                                             compare_op=ALU.is_ge, fill=NEG, base=-1, pattern=[[1, P]],
                                             channel_multiplier=-1))
            link(nc.gpsimd.memset(causal[:, :], 0.0))
            link(nc.gpsimd.affine_select(out=causal[:, :], in_=causal[:, :], compare_op=ALU.is_ge, fill=NEG,
                                         base=P, pattern=[[-1, SEQ]], channel_multiplier=1))
            link(nc.gpsimd.memset(valid[:, :], 1.0))
            link(nc.gpsimd.affine_select(out=valid[:, 0:1], in_=valid[:, 0:1], compare_op=ALU.is_ge, fill=0.0,
                                         base=-31, pattern=[[0, 1]], channel_multiplier=1))
            link(nc.gpsimd.memset(inv_n[:, 0:18], 1.0 / HD))
            link(nc.gpsimd.memset(inv_n[:, 18:19], 1.0 / 256))
            link(nc.gpsimd.memset(inv_n[:, 19:20], 1.0 / 128))
            link(nc.gpsimd.memset(mhalf[:, :], -0.5))
            link(nc.gpsimd.memset(kcT[:, :, :], 0.0))
            nc.gpsimd.memset(cmp_x[:, :, 2, :], 0.0).then_inc(consts_ready, 1)

            def inverse_norm(s, n, done):
                link(nc.gpsimd.tensor_scalar(s, s, 1.0 / n, EPS, ALU.mult, ALU.add))
                w = s.shape[-1]
                nc.gpsimd.tensor_tensor(s, s, mhalf[0:s.shape[0], 0:w], ALU.pow).then_inc(done, 1)

            def residual_norm(N):
                for t in range(NT):
                    pool.wait_ge(sq_ready, NT * N + t + 1)
                    inverse_norm(ssum[:, t:t + 1], D, rstd_ready)

            for L in range(DEPTH):
                residual_norm(2 * L)
                for t in range(NT):
                    pool.wait_ge(head_sums, NT * L + t + 1)
                    link(nc.gpsimd.tensor_tensor(sums[:, t, :], sums[:, t, :], inv_n[:, :], ALU.mult))
                    link(nc.gpsimd.tensor_scalar(sums[:, t, :], sums[:, t, :], 1.0, EPS, ALU.mult, ALU.add))
                    nc.gpsimd.tensor_tensor(sums[:, t, :], sums[:, t, :], mhalf[:, :], ALU.pow).then_inc(head_rstd, 1)
                for t in range(NT):
                    pool.wait_ge(mla_sums, NT * L + t + 1)
                    inverse_norm(msum[:, t, :], MQ, mla_rstd)
                pool.wait_ge(ck_sums, L + 1)
                inverse_norm(ksum[0:N_CMP, :], HD, ck_rstd)
                residual_norm(2 * L + 1)

            bank_read(pool, (DEPTH - 1, "out", NT - 1, 1))
            link(nc.gpsimd.affine_select(out=tri_lt, in_=ones[:, :], compare_op=ALU.is_ge, fill=0.0,
                                         base=-1, pattern=[[1, P]], channel_multiplier=-1))
            link(nc.gpsimd.iota(iota, [[1, P]], base=0, channel_multiplier=0, allow_small_or_imprecise_dtypes=True))
            nc.gpsimd.iota(iota8, [[1, 8]], base=0, channel_multiplier=0,
                           allow_small_or_imprecise_dtypes=True).then_inc(consts_ready, 1)

        @block.scalar
        def _(act_e):
            c = [0]

            def link(ins):
                c[0] += 1
                ins.then_inc(a_done, 1)
                act_e.wait_ge(a_done, c[0])

            act = nc.scalar.activation

            def read_out(key, dst, src):
                bank_written(act_e, key)
                nc.scalar.copy(dst, src).then_inc(bank_free[bank(key)], 1)

            act_e.dma_start(x[:, :, :], a["x"][0].rearrange("(t p) d -> p t d", p=P)).then_inc(small_in, 16)
            act_e.dma_start(table[0:32, :], a["rel_bias_table"]).then_inc(small_in, 16)
            act_e.dma_start(onehot, a["bucket_onehot"]).then_inc(small_in, 16)
            act_e.dma_start(pos_rows, a["nsa_cmp_pos"].rearrange("l k (m j) d -> (l k m) (j d)", j=2)).then_inc(small_in, 16)
            act_e.dma_start(trig[:, :, :, :], a["rope_tables"]).then_inc(small_in, 16)
            act_e.dma_start(bgate[:, :], a["b_gate"].rearrange("l (c n) -> (l c) n", n=512)).then_inc(small_in, 16)
            act_e.dma_start(router[:, :, :], a["moe_router"][0].rearrange("(k p) e -> p k e", p=P)).then_inc(small_in, 16)
            act_e.wait_ge(g_done, 1)
            act_e.dma_start(gain_rows[G_MIX:G_MIX + 16, :], a["mix_norm"].rearrange("l (r c) -> (l r) c", c=P)).then_inc(small_in, 16)
            act_e.dma_start(gain_rows[G_FFN:G_FFN + 16, :], a["ffn_norm"].rearrange("l (r c) -> (l r) c", c=P)).then_inc(small_in, 16)
            for L in range(DEPTH):
                r = G_LAYER + L * G_PER_LAYER
                for half in (0, HD):
                    act_e.dma_start(gain_rows[r + G_Q:r + G_Q + 1, half:half + HD], a["nsa_q_norm"][L:L + 1, :]).then_inc(small_in, 16)
                    act_e.dma_start(gain_rows[r + G_KCMP:r + G_KCMP + 3, half:half + HD], a["nsa_k_norm"][L]).then_inc(small_in, 16)
                act_e.dma_start(gain_rows[r + G_QA:r + G_QA + 2, :], a["mla_q_a_norm"][L].rearrange("(r c) -> r c", c=P)).then_inc(small_in, 16)
                act_e.dma_start(gain_rows[r + G_KVA:r + G_KVA + 1, :], a["mla_kv_a_norm"][L:L + 1, :]).then_inc(small_in, 16)
                act_e.dma_start(mla_gain[:, L, 0, :], a["mla_q_norm"][L].partition_broadcast(P)).then_inc(small_in, 16)
                act_e.dma_start(mla_gain[:, L, 1, :], a["mla_k_norm"][L].partition_broadcast(P)).then_inc(small_in, 16)
            act_e.wait_ge(setup_dve, 1)
            act_e.dma_start(bias_dram, rvec).then_inc(bias_out, 16)
            act_e.wait_ge(bias_out, 16)
            toeplitz = bass.AP(bias_dram.tensor, 0, [[1, P], [512, 8], [1, 384]])
            act_e.dma_start(bias, toeplitz).then_inc(bias_in, 16)

            def residual_squares(N):
                for t in range(NT):
                    if N == 0:
                        act_e.wait_ge(small_in, SMALL_IN)
                    elif N % 2:
                        bank_read(act_e, (N // 2, "out", t, 0))
                        bank_read(act_e, (N // 2, "out", t, 1))
                    else:
                        act_e.wait_ge(x_dense, t + 1)
                    act(xn[:, t, :], x[:, t, :], ACT.Square, accum_out=ssum[:, t:t + 1]).then_inc(sq_ready, 1)

            def projection_out(L, c, t):
                c0, w = CHUNKS[c]
                key = (L, "proj", c, t)
                read_out(key, proj[:, t, c0:c0 + w], ps[:, bank(key), 0:w])

            def mixers(L):
                residual_squares(2 * L)
                for c_ in range(N_MIX_CHUNKS):
                    projection_out(L, c_, 0)
                for t in range(NT):
                    for c_ in range(1, N_MIX_CHUNKS):
                        bank_read(act_e, (L, "proj", c_, t))
                    if t == 1:
                        act_e.wait_ge(head_sums, NT * L + 1)
                    act(tmp[:, 0:1152], proj[:, t, NQ:NQ + 1152], ACT.Square).then_inc(head_sq, 1)
                    act(tmp[:, 1152:1536], proj[:, t, CQ:CQ + 384], ACT.Square).then_inc(head_sq, 1)
                for t in range(NT):
                    act(ngate[:, t, :], proj[:, t, NG:NG + 24], ACT.Exp, scale=-1.0).then_inc(ng_exp, 1)
                projection_out(L, 5, 0)
                for t in range(NT):
                    key = (L, "xt", t, 0)
                    read_out(key, xT[:, 0:4, P * t:P * t + P], ps[:, bank(key), :].rearrange("p (j q) -> p j q", j=4))
                projection_out(L, 6, 0)
                for t in range(NT):
                    key = (L, "uq", t)
                    read_out(key, mqk[:, t, 0:4, :], ps[:, bank(key), 0:384].rearrange("p (h d) -> p h d", h=4))
                    key = (L, "ukv", t)
                    both = ps[:, bank(key), :].rearrange("p (h d) -> p h d", h=4)
                    bank_written(act_e, key)
                    nc.scalar.copy(mqk[:, t, 4:8, 0:HD], both[:, :, 0:HD]).then_inc(mla_in, 1)
                    nc.scalar.copy(mv[:, t, :, :], both[:, :, HD:P]).then_inc(bank_free[bank(key)], 1)
                for t in range(NT):
                    act_e.wait_ge(mla_in, NT * L + t + 1)
                    bank_read(act_e, (L, "uq", t))
                    act_e.wait_ge(mla_rope_in, L + 1)
                    act_e.wait_ge(*((head_sums, NT * L + NT) if t == 0 else (mla_sums, NT * L + 1)))
                    act(tmp[:, 0:768], mqk[:, t, :, :].rearrange("p h d -> p (h d)"), ACT.Square).then_inc(mla_sq, 1)
                key = (L, "c1")
                read_out(key, ch_raw[:, :, :], ps[:, bank(key), 0:180].rearrange("p (f n) -> p f n", f=4))
                act_e.wait_ge(ch_ready, L + 1)
                act(ce[:, :, :], ch[:, :, :], ACT.Exp, scale=-1.0).then_inc(ch_exp, 1)
                projection_out(L, 7, 0)
                act_e.wait_ge(stick_z, L + 1)
                act_e.wait_ge(mla_sums, NT * L + NT)
                link(act(stick_tmp[:, :, :], stick, ACT.Abs))
                link(act(tmp, tmp, ACT.Exp, scale=-1.0))
                act(tmp, tmp, ACT.Ln, bias=1.0).then_inc(stick_ln, 1)
                for t in range(NT):
                    for b in range(2):
                        key = (L, "mt", t, b)
                        read_out(key, mT[0:MQ, 4 * b:4 * b + 4, P * t:P * t + P],
                                 ps[0:MQ, bank(key), :].rearrange("p (j q) -> p j q", j=4))
                act_e.wait_ge(stick_t, L + 1)
                act(stick, stick, ACT.Exp).then_inc(stick_w, 1)
                for i in range(NT):
                    act_e.wait_ge(cmp_s, NT * L + i + 1)
                    act(pcs[:, i, :, 0:N_CMP], pcs[:, i, :, 0:N_CMP], ACT.Exp).then_inc(cmp_e, 1)
                for hp in range(2):
                    key = (L, "sbo", hp)
                    act_e.wait_ge(stick_out, 2 * L + hp + 1)
                    nc.scalar.copy(yT[:, hp, :], ps[:, bank(key), 0:SEQ]).then_inc(bank_free[bank(key)], 1)
                for s in range(STEPS):
                    if s < len(JOBS):
                        job_exp(L, s)
                    if 0 <= s - LAG_TURN < len(JOBS):
                        job_turned(L, s - LAG_TURN)
                    if 0 <= s - LAG_PV < len(JOBS):
                        job_out(L, s - LAG_PV)
                    if s in LATE_GATES and LATE_GATES[s][1] == 0:
                        projection_out(L, *LATE_GATES[s])
                for t in range(NT):
                    for c_ in range(N_MIX_CHUNKS, len(CHUNKS)):
                        bank_read(act_e, (L, "proj", c_, t))
                    act(proj[:, t, GATES:], proj[:, t, GATES:], ACT.Sigmoid).then_inc(gates_ready, 1)
                for t in range(NT):
                    for h in range(2):
                        key = (L, "merge", t, h)
                        read_out(key, hT[:, 4 * h:4 * h + 4, P * t:P * t + P],
                                 ps[:, bank(key), :].rearrange("p (j q) -> p j q", j=4))
                residual_squares(2 * L + 1)

            def job_exp(L, j):
                kind, i, r = JOBS[j]
                nk = P * (i + 1)
                n = len(JOBS) * L + j
                b = n % 3
                act_e.wait_ge(max_ready, n + 1)
                v = probs[:, b, 0:2 * nk].rearrange("p (a k) -> p a k", a=2)
                for h in range(2):
                    act(v[:, h, :], v[:, h, :], ACT.Exp, bias=nmax[:, b, h:h + 1],
                        accum_out=prob_sum[:, b, h:h + 1]).then_inc(exp_ready, 1)

            def job_turned(L, j):
                kind, i, r = JOBS[j]
                n = len(JOBS) * L + j
                if n >= 2:
                    act_e.wait_ge(pv_done, n - 1)
                key = (L, "p", j)
                w = 2 * (i + 1) * P
                read_out(key, probsT[:, n % 2, 0:w], ps[:, bank(key), 0:w])

            def job_out(L, j):
                kind, i, r = JOBS[j]
                if kind == "sel":
                    return
                act_e.wait_ge(pv_done, len(JOBS) * L + j + 1)
                key = (L, "mlao", i, r) if kind == "mla" else (L, "nsao", i, r)
                to = 6 + r if kind == "mla" else 2 + r
                nc.scalar.copy(yT[:, to, P * i:P * i + P], ps[:, bank(key), 0:P]).then_inc(bank_free[bank(key)], 1)

            def split_normed(t, h):
                bank_read(act_e, (0, "norm2", t, h))
                v = (slice(None), slice(4 * h, 4 * h + 4), slice(P * t, P * t + P))
                nc.scalar.copy(h_hi[v], hT[v]).then_inc(h_hi_ready, 1)

            def ffn_rounded_parts(chunks, q0, n0, tiles, widths, landed, slot, gate_bank, turn_bank, extra=None):
                T = len(tiles)

                def turned(u):
                    for t in tiles:
                        n = n0 + (u * T + t)
                        act_e.wait_ge(act_turned, n + 1)
                        w = widths[u]
                        nc.scalar.copy(a_hi[:, t if T > 1 else u % 2, 0:w], ps[:, turn_bank(t), 0:w]).then_inc(a_hi_ready, 1)

                for m, (kind, u) in enumerate(chunks):
                    rows, cols = chunk_shape(kind, widths[u])
                    src = slot(m, rows, cols).rearrange("p k w -> p (k w)")
                    w = rows * cols // 2
                    landed(act_e, m)
                    for half in range(2):
                        q = 2 * m + half
                        if not isinstance(q0, int) or q0 + q >= SPLIT_BUFS:
                            act_e.wait_ge(half_done, q0 + (q + 1 - SPLIT_BUFS))
                        used = q - SPLIT_BUFS
                        before_kind, before_u = chunks[used // 2] if used >= 0 else (None, None)
                        if before_kind == "gate" and used % 2 == 1:
                            for t in tiles:
                                g = widths[before_u]
                                act(act_g[:, t, 0:g], ps[:, gate_bank(t), 0:g], ACT.Silu).then_inc(silu_done, 1)
                        if before_kind == "gate" and used % 2 == 0 and before_u > 0:
                            turned(before_u - 1)
                        nc.scalar.copy(w_hi[q % SPLIT_BUFS][:, 0:w], src[:, w * half:w * half + w]).then_inc(hi_ready, 1)
                        if extra and q == 6:
                            extra()
                turned(len(widths) - 1)

            def dense_slot(m, rows, cols):
                return slot_view(slot_of((0, *DENSE_CHUNKS[m])), rows, cols)

            mixers(0)
            for t in range(NT):
                for h in range(2):
                    split_normed(t, h)
            ffn_rounded_parts(DENSE_CHUNKS, 0, 0, range(NT), [w for _, w in DENSE_GROUPS],
                              lambda eng, m: weights_landed(eng, (0, *DENSE_CHUNKS[m])), dense_slot,
                              lambda t: t, lambda t: 2 + t)
            mixers(1)

            act_e.wait_ge(route_dve, 1)
            act(route[:, 2, :, 1:2], route[:, 2, :, 0:1], ACT.Exp).then_inc(route_exp, 1)

            def put_out(it):
                act_e.wait_ge(put_turned, it + 1)
                nc.scalar.copy(putT, ps[:, 1, 0:SEQ]).then_inc(putT_ready, 1)

            def gathered_rounded(it):
                for h in range(2):
                    act_e.wait_ge(gains_applied, it * 2 + (h + 1))
                    nc.scalar.copy(e_hi[:, 4 * h:4 * h + 4, :], gathered_f[h].rearrange("p (j s) -> p j s", j=4)).then_inc(e_hi_ready, 1)

            gathered_rounded(0)
            act_e.sem_inc(ye_ready, 1)

            def expert(pair, o):
                it = pair * PAIR + o
                c0 = o * len(EXPERT_CHUNKS)
                ffn_rounded_parts(EXPERT_CHUNKS, it * EXPERT_HALVES + DENSE_HALVES,
                                  it * EXPERT_UNITS + NT * len(DENSE_GROUPS), (0,), [512] * EXPERT_UNITS,
                                  lambda eng, m: expert_landed(eng, pair, c0 + m),
                                  lambda m, rows, cols: expert_slot(c0 + m, rows, cols), lambda t: 2, lambda t: 0,
                                  extra=lambda: put_out(it))
                gathered_rounded(it + 1)
                act_e.wait_ge(half_done, (it + 1) * EXPERT_HALVES + DENSE_HALVES)
                act_e.wait_ge(spread, it * 4 + 1)
                nc.scalar.copy(ye[:, 0:512], ps[:, 4, :]).then_inc(ye_ready, 1)

            with act_e.Fori(0, PAIRS) as pair:
                for o in range(PAIR):
                    expert(pair, o)
            act_e.wait_ge(routed, 2)
            crowded = act_e.value_load(flag_i[0:1, 0:1], min_val=0, max_val=1)
            with act_e.If(crowded > 0):
                with act_e.Fori(PAIRS, 2 * PAIRS) as pair:
                    for o in range(PAIR):
                        expert(pair, o)

        @block.vector
        def _(dve):
            c = [0]
            V = nc.vector

            def link(ins):
                c[0] += 1
                ins.then_inc(v_done, 1)
                dve.wait_ge(v_done, c[0])

            def bc(ap, n):
                return ap.unsqueeze(len(ap.shape)).to_broadcast(list(ap.shape) + [n])

            def turned_with_gains(key, dst, col):
                bank_written(dve, key)
                k = dst.shape[1]
                V.tensor_tensor(dst, ps[:, bank(key), 0:k * P].rearrange("p (j q) -> p j q", j=k),
                                bc(gains[:, col:col + k], P), ALU.mult).then_inc(bank_free[bank(key)], 1)

            def residual_norm(L, which, col):
                N = 2 * L + (which == "norm2")
                for t in range(NT):
                    dve.wait_ge(rstd_ready, NT * N + t + 1)
                    V.tensor_scalar(xn[:, t, :], x[:, t, :], ssum[:, t:t + 1], None, ALU.mult).then_inc(xn_ready, 1)
                for t in range(NT):
                    for h in range(2):
                        turned_with_gains((L, which, t, h), hT[:, 4 * h:4 * h + 4, P * t:P * t + P], col + 4 * h)

            def projection_out(L, c_, t):
                c0, w = CHUNKS[c_]
                key = (L, "proj", c_, t)
                bank_written(dve, key)
                V.tensor_copy(proj[:, t, c0:c0 + w], ps[:, bank(key), 0:w]).then_inc(bank_free[bank(key)], 1)

            dve.wait_ge(setup_pe, 1)
            link(V.tensor_copy(gains[:, :], ps[:, 6, 0:64]))
            link(V.tensor_copy(posT[:, :, :].rearrange("p a b -> p (a b)"), ps[:, 6, P:P + 64]))
            V.tensor_copy(rvec, ps[0:8, 7, :]).then_inc(setup_dve, 1)

            def head_norms(L, t):
                dve.wait_ge(head_sq, 2 * (NT * L + t) + 2)
                V.tensor_reduce(sums[:, t, 0:18], tmp[:, 0:1152].rearrange("p (h d) -> p h d", d=HD), AX.X, ALU.add)
                V.tensor_reduce(sums[:, t, 18:19], tmp[:, 1152:1408], AX.X, ALU.add)
                V.tensor_reduce(sums[:, t, 19:20], tmp[:, 1408:1536], AX.X, ALU.add).then_inc(head_sums, 1)
                dve.wait_ge(head_rstd, NT * L + t + 1)
                q = proj[:, t, NQ:NQ + 512].rearrange("p (g r d) -> p g r d", g=2, r=4)
                pairs = xn[:, t, 0:512].rearrange("p (r g d) -> p g r d", r=4, g=2)
                for g in range(2):
                    V.tensor_tensor(pairs[:, g], q[:, g], bc(sums[:, t, 4 * g:4 * g + 4], HD), ALU.mult)
                for c0, n, s0 in ((KS, 2, 12), (KW, 2, 16)):
                    v = proj[:, t, c0:c0 + n * HD].rearrange("p (h d) -> p h d", d=HD)
                    V.tensor_tensor(v, v, bc(sums[:, t, s0:s0 + n], HD), ALU.mult)
                V.tensor_scalar(proj[:, t, CQ:CQ + 256], proj[:, t, CQ:CQ + 256], sums[:, t, 18:19], None, ALU.mult)
                V.tensor_scalar(proj[:, t, CKV:CKV + P], proj[:, t, CKV:CKV + P], sums[:, t, 19:20], None,
                                ALU.mult).then_inc(heads_normed, 1)

            def turned_mixer_inputs(L, t):
                g0 = G_LAYER + L * G_PER_LAYER
                q = slice(P * t, P * t + P)
                key = (L, "xt", t, 1)
                bank_written(dve, key)
                V.tensor_scalar(xT[:, 4:8, q], ps[:, bank(key), :].rearrange("p (j q) -> p j q", j=4),
                                gains[:, g0 + G_Q:g0 + G_Q + 1], None, ALU.mult).then_inc(bank_free[bank(key)], 1)
                key = (L, "xt", t, 2)
                bank_written(dve, key)
                b = ps[:, bank(key), :]
                for kv in range(2):
                    for g in range(2):
                        for par in range(2):
                            src = b[64 * g:64 * g + 64, (2 + kv) * P:(3 + kv) * P].rearrange("p (m j) -> p m j", j=2)
                            V.tensor_copy(cmp_x[64 * par:64 * par + 64, kv, g, 64 * t:64 * t + 64], src[:, :, par])
                if t == 0:
                    V.tensor_copy(cmp_x[:, :, 2, 0:16], posT[:, 2 * L:2 * L + 2, :])
                V.tensor_tensor(xT[:, 8:10, q], b[:, 0:2 * P].rearrange("p (j q) -> p j q", j=2),
                                bc(gains[:, g0 + G_KSEL:g0 + G_KSEL + 2], P), ALU.mult).then_inc(bank_free[bank(key)], 1)
                turned_with_gains((L, "xt", t, 3), xT[:, 10:13, q], g0 + G_QA)

            def latent_heads(L, t):
                m = mqk[:, t, :, :]
                dve.wait_ge(mla_sq, NT * L + t + 1)
                V.tensor_reduce(msum[:, t, :], tmp[:, 0:768].rearrange("p (h d) -> p h d", d=MQ), AX.X,
                                ALU.add).then_inc(mla_sums, 1)
                dve.wait_ge(mla_rstd, NT * L + t + 1)
                link(V.tensor_tensor(m, m, bc(msum[:, t, :], MQ), ALU.mult))
                for w in range(2):
                    v = m[:, 4 * w:4 * w + 4, :]
                    gain = mla_gain[:, L, w, :].unsqueeze(1).to_broadcast([P, 4, MQ])
                    ins = V.tensor_tensor(v, v, gain, ALU.mult)
                link(ins)
                x1, x2 = m[:, :, 64:80], m[:, :, 80:96]
                cos, sin = (trig[:, f, t, :].unsqueeze(1).to_broadcast([P, 8, 16]) for f in range(2))
                r = rope_tmp.rearrange("p f (h d) -> p f h d", h=8)
                V.tensor_tensor(r[:, 0], x1, cos, ALU.mult)
                V.tensor_tensor(r[:, 1], x2, sin, ALU.mult)
                V.tensor_tensor(r[:, 2], x2, cos, ALU.mult)
                link(V.tensor_tensor(r[:, 3], x1, sin, ALU.mult))
                V.tensor_tensor(x1, r[:, 0], r[:, 1], ALU.subtract)
                V.tensor_tensor(x2, r[:, 2], r[:, 3], ALU.add).then_inc(mla_ready, 1)

            def mixers(L):
                residual_norm(L, "norm1", G_MIX + KD * L)
                g0 = G_LAYER + L * G_PER_LAYER
                for c_ in range(N_MIX_CHUNKS):
                    projection_out(L, c_, 1)
                for t in range(NT):
                    bank_read(dve, (L, "proj", 4, t))
                    ins = V.tensor_copy(mqk[:, t, 4:8, HD:MQ], proj[:, t, KR:KR + 32].unsqueeze(1).to_broadcast([P, 4, 32]))
                ins.then_inc(mla_rope_in, 1)
                for t in range(NT):
                    head_norms(L, t)
                dve.wait_ge(ng_exp, NT * L + NT)
                flat = ngate[:, :, :].rearrange("p t n -> p (t n)")
                link(V.tensor_scalar(flat, flat, 1.0, None, ALU.add))
                link(V.reciprocal(flat, flat))
                projection_out(L, 5, 1)
                for t in range(NT):
                    turned_mixer_inputs(L, t)
                projection_out(L, 6, 1)
                for t in range(NT):
                    latent_heads(L, t)
                for t in range(NT):
                    bank_read(dve, (L, "uq", t))
                    bank_read(dve, (L, "ukv", t))
                link(V.tensor_copy(xT[64:P, 10:12, :], xT[64:P, 8:10, :]))
                V.memset(xT[64:P, 8:10, :], 0.0)
                V.memset(xT[0:64, 10:12, :], 0.0).then_inc(keys_split, 1)
                bank_read(dve, (L, "c1"))
                V.tensor_tensor(ch[:, :, :], ch_raw[:, :, 0:30], ch_raw[:, :, 30:31].to_broadcast([P, 4, 30]),
                                ALU.add).then_inc(ch_ready, 1)
                dve.wait_ge(ch_exp, L + 1)
                link(V.tensor_scalar(ce[:, :, :], ce[:, :, :], 1.0, None, ALU.add))
                link(V.reciprocal(ce[:, :, :], ce[:, :, :]))
                V.tensor_tensor(ch[:, :, :], ch[:, :, :], ce[:, :, :], ALU.mult).then_inc(ch_act, 1)
                for h in range(4):
                    key = (L, "z", h)
                    bank_written(dve, key)
                    V.scalar_tensor_tensor(out=stick[:, h, :], in0=ps[:, bank(key), 0:384], scalar=HD ** -0.5,
                                           in1=stick_mask[:, :], op0=ALU.mult, op1=ALU.add).then_inc(bank_free[bank(key)], 1)
                bank_read(dve, (L, "z", 2))
                bank_read(dve, (L, "z", 3))
                link(V.tensor_copy(cmax[0:1, 0:1], ones[0:1, 0:1]))
                dve.sem_inc(stick_z, 1)
                key = (L, "c2")
                bank_written(dve, key)
                V.tensor_copy(ckv_c[0:N_CMP, :, :], ps[0:N_CMP, bank(key), 0:4 * HD].rearrange("p (f d) -> p f d", f=4)).then_inc(bank_free[bank(key)], 1)
                bank_read(dve, key)
                link(V.tensor_tensor(csq[0:N_CMP, :, :], ckv_c[0:N_CMP, 0:2, :], ckv_c[0:N_CMP, 0:2, :], ALU.mult))
                V.tensor_reduce(ksum[0:N_CMP, :], csq[0:N_CMP, :, :], AX.X, ALU.add).then_inc(ck_sums, 1)
                dve.wait_ge(ck_rstd, L + 1)
                V.tensor_tensor(ckv_c[0:N_CMP, 0:2, :], ckv_c[0:N_CMP, 0:2, :], bc(ksum[0:N_CMP, :], HD),
                                ALU.mult).then_inc(ck_ready, 1)
                projection_out(L, 7, 1)
                key = (L, "kct")
                bank_written(dve, key)
                for g in range(2):
                    r = slice(64 * g, 64 * g + 64)
                    ins = V.tensor_scalar(kcT[r, g, 0:N_CMP], ps[r, bank(key), 0:N_CMP],
                                          gains[r, g0 + G_KCMP:g0 + G_KCMP + 1], None, ALU.mult)
                ins.then_inc(bank_free[bank(key)], 1)
                dve.wait_ge(stick_ln, L + 1)
                V.scalar_tensor_tensor(out=stick_tmp[:, :, :], in0=stick, scalar=0.0, in1=stick_tmp[:, :, :],
                                       op0=ALU.max, op1=ALU.add).then_inc(stick_sp, 1)
                for h in range(4):
                    key = (L, "S", h)
                    bank_written(dve, key)
                    V.tensor_tensor(stick[:, h, :], stick[:, h, :], ps[:, bank(key), 0:384],
                                    ALU.subtract).then_inc(bank_free[bank(key)], 1)
                bank_read(dve, (L, "S", 2))
                bank_read(dve, (L, "S", 3))
                dve.sem_inc(stick_t, 1)
                if L == 0:
                    for h in range(8):
                        key = (0, "flip", h)
                        bank_written(dve, key)
                        V.tensor_copy(bias[:, h, :], ps[:, bank(key), 0:384]).then_inc(bank_free[bank(key)], 1)
                    for h in (6, 7):
                        bank_read(dve, (0, "flip", h))
                for i in range(NT):
                    key = (L, "sc", i)
                    bank_written(dve, key)
                    s = pcs[:, i, :, 0:N_CMP]
                    k0 = 31 + P * (1 - i)
                    V.scalar_tensor_tensor(out=s, in0=ps[:, bank(key), 0:P].rearrange("p (h n) -> p h n", h=8)[:, :, 0:N_CMP],
                                           scalar=HD ** -0.5, in1=bias[:, :, k0:k0 + 16 * (N_CMP - 1) + 1:16],
                                           op0=ALU.mult, op1=ALU.add).then_inc(bank_free[bank(key)], 1)
                    bank_read(dve, key)
                    link(V.tensor_reduce(cmax[:, :], s, AX.X, ALU.max))
                    V.tensor_tensor(s, s, bc(cmax[:, :], N_CMP), ALU.subtract).then_inc(cmp_s, 1)
                    dve.wait_ge(cmp_e, NT * L + i + 1)
                    link(V.tensor_reduce(csum[:, :], s, AX.X, ALU.add))
                    link(V.reciprocal(csum[:, :], csum[:, :]))
                    link(V.scalar_tensor_tensor(out=csum[:, :], in0=csum[:, :], scalar=valid[:, i:i + 1],
                                                in1=ngate[:, i, 0:24:3], op0=ALU.mult, op1=ALU.mult))
                    V.tensor_tensor(s, s, bc(csum[:, :], N_CMP), ALU.mult).then_inc(cmp_p, 1)
                for s in range(STEPS):
                    if s < len(JOBS):
                        job_scores(L, s)
                    if 0 <= s - 1 < len(JOBS):
                        job_scale(L, s - 1)
                    for i in range(NT):
                        if s - LAG_TURN == FIRST_SPARSE[i]:
                            compressed_turned(L, i)
                    if s in LATE_GATES and LATE_GATES[s][1] == 1:
                        projection_out(L, *LATE_GATES[s])
                for t in range(NT):
                    dve.wait_ge(gates_ready, NT * L + t + 1)
                    for h in range(2):
                        to = xn[:, t, 512 * h:512 * h + 512]
                        for m in range(3):
                            key = (L, "y", t, h, m)
                            gate = proj[:, t, GATES + D * m + 512 * h:GATES + D * m + 512 * h + 512]
                            dst = to if m == 0 else tmp[:, 512 * (m - 1):512 * m]
                            bank_written(dve, key)
                            V.tensor_tensor(dst, ps[:, bank(key), :], gate, ALU.mult).then_inc(bank_free[bank(key)], 1)
                            bank_read(dve, key)
                            if m == 1:
                                link(V.tensor_tensor(to, to, dst, ALU.add))
                            if m == 2:
                                V.tensor_tensor(to, to, dst, ALU.add).then_inc(merged, 1)
                                dve.wait_ge(merged, 4 * L + 2 * t + h + 1)
                for t in range(NT):
                    for h in range(2):
                        key = (L, "out", t, h)
                        bank_written(dve, key)
                        V.tensor_tensor(x[:, t, 512 * h:512 * h + 512], x[:, t, 512 * h:512 * h + 512],
                                        ps[:, bank(key), :], ALU.add).then_inc(bank_free[bank(key)], 1)
                residual_norm(L, "norm2", G_FFN + KD * L)

            def job_scores(L, j):
                kind, i, r = JOBS[j]
                nk = P * (i + 1)
                n = len(JOBS) * L + j
                b = n % 3
                if j >= 3:
                    bank_written(dve, (L, "p", j - 3))
                v = probs[:, b, 0:2 * nk].rearrange("p (a k) -> p a k", a=2)
                k0 = P * (1 - i)
                if kind == "mla":
                    add = causal[:, k0:SEQ].unsqueeze(1).to_broadcast([P, 2, nk])
                    scale = MQ ** -0.5
                else:
                    add = bias[:, r:8:4, k0:SEQ]
                    scale = HD ** -0.5
                key = (L, "s", j)
                bank_written(dve, key)
                V.scalar_tensor_tensor(out=v, in0=ps[:, bank(key), 0:2 * nk].rearrange("p (a k) -> p a k", a=2),
                                       scalar=scale, in1=add, op0=ALU.mult, op1=ALU.add).then_inc(bank_free[bank(key)], 1)
                bank_read(dve, key)
                V.tensor_reduce(nmax[:, b, :], v, AX.X, ALU.max, negate=True).then_inc(max_ready, 1)

            def job_scale(L, j):
                kind, i, r = JOBS[j]
                nk = P * (i + 1)
                n = len(JOBS) * L + j
                b = n % 3
                dve.wait_ge(exp_ready, 2 * n + 2)
                link(V.reciprocal(prec[:, b, :], prob_sum[:, b, :]))
                if kind != "mla":
                    g = 3 * r + (1 if kind == "sel" else 2)
                    link(V.tensor_tensor(prec[:, b, :], prec[:, b, :], ngate[:, i, g:g + 13:12], ALU.mult))
                v = probs[:, b, 0:2 * nk].rearrange("p (a k) -> p a k", a=2)
                V.tensor_tensor(v, v, bc(prec[:, b, :], nk), ALU.mult).then_inc(probs_ready, 1)

            def compressed_turned(L, i):
                for h in range(2):
                    key = (L, "pc", i, h)
                    if i > 0 and h == 0:
                        dve.wait_ge(pv_done, len(JOBS) * L + FIRST_SPARSE[i])
                    bank_written(dve, key)
                    V.tensor_copy(pcT[0:N_CMP, 4 * h:4 * h + 4, :],
                                  ps[0:N_CMP, bank(key), :].rearrange("p (h q) -> p h q", h=4)).then_inc(bank_free[bank(key)], 1)

            def ffn_remainders(chunks, q0, n0, tiles, widths, slot, up_bank, turn_bank, extra=None):
                T = len(tiles)

                def turned(u):
                    for t in tiles:
                        n = n0 + (u * T + t)
                        w, b = widths[u], t if T > 1 else u % 2
                        dve.wait_ge(a_hi_ready, n + 1)
                        V.tensor_tensor(a_lo[:, b, 0:w], ps[:, turn_bank(t), 0:w], a_hi[:, b, 0:w].bitcast(F32),
                                        ALU.subtract).then_inc(a_lo_ready, 1)

                def hidden(u, q):
                    dve.wait_ge(half_done, q0 + (q + 1))
                    for t in tiles:
                        g = widths[u]
                        dve.wait_ge(silu_done, n0 + (u * T + t + 1))
                        V.tensor_tensor(act[:, t, 0:g], act_g[:, t, 0:g], ps[:, up_bank(t), 0:g],
                                        ALU.mult).then_inc(act_ready, 1)

                for m, (kind, u) in enumerate(chunks):
                    rows, cols = chunk_shape(kind, widths[u])
                    src = slot(m, rows, cols).rearrange("p k w -> p (k w)")
                    w = rows * cols // 2
                    for half in range(2):
                        q = 2 * m + half
                        used = q - SPLIT_BUFS
                        before_kind, before_u = chunks[used // 2] if used >= 0 else (None, None)
                        if before_kind == "up" and used % 2 == 1:
                            hidden(before_u, used)
                        if before_kind == "gate" and used % 2 == 0 and before_u > 0:
                            turned(before_u - 1)
                        dve.wait_ge(hi_ready, q0 + (q + 1))
                        V.tensor_tensor(w_lo[q % SPLIT_BUFS][:, 0:w], src[:, w * half:w * half + w],
                                        w_hi[q % SPLIT_BUFS][:, 0:w].bitcast(F32), ALU.subtract).then_inc(lo_ready, 1)
                        if extra and q == 12:
                            extra()
                hidden(len(widths) - 1, 2 * len(chunks) - SPLIT_BUFS)
                turned(len(widths) - 1)

            mixers(0)
            for t in range(NT):
                for h in range(2):
                    v = (slice(None), slice(4 * h, 4 * h + 4), slice(P * t, P * t + P))
                    dve.wait_ge(h_hi_ready, 2 * t + h + 1)
                    V.tensor_tensor(h_lo[v], hT[v], h_hi[v].bitcast(F32), ALU.subtract).then_inc(h_lo_ready, 1)
            dve.wait_ge(h_lo_ready, 4)
            ffn_remainders(DENSE_CHUNKS, 0, 0, range(NT), [w for _, w in DENSE_GROUPS],
                           lambda m, rows, cols: slot_view(slot_of((0, *DENSE_CHUNKS[m])), rows, cols),
                           lambda t: 2 + t, lambda t: 2 + t)
            dve.wait_ge(half_done, DENSE_HALVES)
            for t in range(NT):
                for h in range(2):
                    v = x[:, t, 512 * h:512 * h + 512]
                    ins = V.tensor_tensor(v, v, ps[:, 4 + 2 * t + h, :], ALU.add)
                ins.then_inc(x_dense, 1)
            mixers(1)

            dve.wait_ge(route_pe, 1)
            dve.wait_ge(consts_ready, 2)
            logits, top, w_top, oh0, oh1, sel = (route[:, n] for n in range(6))
            slot1 = route[:, 6]
            link(V.tensor_copy(logits, ps[:, 1, 0:16].rearrange("p (t e) -> p t e", t=NT)))
            for t in range(NT):
                link(V.max(top[:, t, :], logits[:, t, :]))
                link(V.max_index(top_i[:, t, :], top[:, t, :], logits[:, t, :]))
            top_f = route[:, 7]
            link(V.tensor_copy(top_f, top_i[:, :, :]))
            V.tensor_tensor(w_top[:, :, 0:1], top[:, :, 1:2], top[:, :, 0:1], ALU.subtract).then_inc(route_dve, 1)
            dve.wait_ge(route_exp, 1)
            link(V.tensor_scalar(w_top[:, :, 2:3], w_top[:, :, 1:2], 1.0, None, ALU.add))
            link(V.reciprocal(w_top[:, :, 3:4], w_top[:, :, 2:3]))
            link(V.tensor_tensor(w_top[:, :, 4:5], w_top[:, :, 1:2], w_top[:, :, 3:4], ALU.mult))
            for t in range(NT):
                V.tensor_scalar(oh0[:, t, :], iota8, top_f[:, t, 0:1], None, ALU.is_equal)
                link(V.tensor_scalar(oh1[:, t, :], iota8, top_f[:, t, 1:2], None, ALU.is_equal))
                link(V.tensor_scalar(comb[:, t, 0:8], oh1[:, t, :], w_top[:, t, 4:5], None, ALU.mult))
                link(V.scalar_tensor_tensor(out=comb[:, t, 0:8], in0=oh0[:, t, :], scalar=w_top[:, t, 3:4],
                                            in1=comb[:, t, 0:8], op0=ALU.mult, op1=ALU.add))
            V.tensor_copy(comb[:, :, 8:16], comb[:, :, 0:8])
            V.memset(comb[:, :, 16:17], 0.0)
            V.tensor_tensor(sel, oh0, oh1, ALU.add).then_inc(route_dve, 1)
            dve.wait_ge(route_pe, 2)
            link(V.scalar_tensor_tensor(out=slot1, in0=ps[:, 1, 0:16].rearrange("p (t e) -> p t e", t=NT), scalar=1.0,
                                        in1=sel, op0=ALU.add, op1=ALU.mult))
            link(V.tensor_scalar(slots[:, :, 0:8], slot1, -1.0, None, ALU.add))
            V.tensor_scalar(slots[:, :, 8:16], slot1, -1.0 - P, None, ALU.add)
            V.memset(slots[:, :, 16:17], -1.0)
            link(V.tensor_reduce(flag[:, 0:1], ps[:, 1, 16:24], AX.X, ALU.max))
            link(V.tensor_scalar(flag[:, 1:2], flag[:, 0:1], P + 0.5, None, ALU.is_gt))
            V.tensor_copy(flag_i[:, :], flag[:, 1:2]).then_inc(routed, 1)
            dve.wait_ge(routed, 1)
            V.tensor_copy(now[:, 0:1], flag[:, 0:1]).then_inc(routed, 1)
            dve.wait_ge(routed, 2)

            def pick_tokens(it, first=False):
                if not first:
                    dve.wait_ge(gathered, it * 2)
                    dve.wait_ge(put_turned, it)
                V.tensor_copy(now[:, 0:2], slots[:, :, bass.ds(it, 1)].rearrange("p t o -> p (t o)"))
                V.tensor_copy(now[:, 2:4], comb[:, :, bass.ds(it, 1)].rearrange("p t o -> p (t o)")).then_inc(now_ready, 1)
                dve.wait_ge(now_ready, it + 1)
                for t in range(NT):
                    V.tensor_scalar(pick[:, t, :], iota, now[:, t:t + 1], None, ALU.is_equal)
                    ins = V.tensor_scalar(put[:, t, :], iota, now[:, t:t + 1], now[:, 2 + t:3 + t], ALU.is_equal, ALU.mult)
                ins.then_inc(pick_ready, 1)

            ffn_gain = G_FFN + KD * (DEPTH - 1)

            def gathered_out(it):
                for h in range(2):
                    dve.wait_ge(gathered, it * 2 + (h + 1))
                    V.tensor_tensor(gathered_f[h].rearrange("p (j s) -> p j s", j=4),
                                    ps[:, 6 + h, :].rearrange("p (j s) -> p j s", j=4),
                                    bc(gains[:, ffn_gain + 4 * h:ffn_gain + 4 * h + 4], P), ALU.mult).then_inc(gains_applied, 1)
                for h in range(2):
                    dve.wait_ge(e_hi_ready, it * 2 + (h + 1))
                    V.tensor_tensor(e_lo[:, 4 * h:4 * h + 4, :], gathered_f[h].rearrange("p (j s) -> p j s", j=4),
                                    e_hi[:, 4 * h:4 * h + 4, :].bitcast(F32), ALU.subtract).then_inc(e_lo_ready, 1)

            pick_tokens(0, True)
            gathered_out(0)
            dve.sem_inc(added, 1)

            def add_spread(it):
                for k in range(4):
                    t, h = k // 2, k % 2
                    dve.wait_ge(spread, it * 4 + (k + 2))
                    dve.wait_ge(added, it * 4 + (k + 1))
                    v = x[:, t, 512 * h:512 * h + 512]
                    V.tensor_tensor(v, v, ps[:, SPREAD_BANKS[k], :], ALU.add).then_inc(added, 1)

            def expert(pair, o):
                it = pair * PAIR + o
                c0 = o * len(EXPERT_CHUNKS)
                ffn_remainders(EXPERT_CHUNKS, it * EXPERT_HALVES + DENSE_HALVES,
                               it * EXPERT_UNITS + NT * len(DENSE_GROUPS), (0,), [512] * EXPERT_UNITS,
                               lambda m, rows, cols: expert_slot(c0 + m, rows, cols), lambda t: 3, lambda t: 0,
                               extra=lambda: pick_tokens(it + 1))
                gathered_out(it + 1)
                dve.wait_ge(half_done, (it + 1) * EXPERT_HALVES + DENSE_HALVES)
                dve.wait_ge(spread, it * 4 + 1)
                V.tensor_copy(ye[:, 512:1024], ps[:, 5, :]).then_inc(ye_copied, 1)
                add_spread(it)

            with dve.Fori(0, PAIRS) as pair:
                for o in range(PAIR):
                    expert(pair, o)
            crowded = dve.value_load(flag_i[0:1, 0:1], min_val=0, max_val=1)
            with dve.If(crowded > 0):
                with dve.Fori(PAIRS, 2 * PAIRS) as pair:
                    for o in range(PAIR):
                        expert(pair, o)
            V.tensor_copy(now[:, 0:1], flag[:, 0:1]).then_inc(x_final, 1)

        @block.tensor
        def _(pe):
            mm, turn = nc.tensor.matmul, nc.tensor.transpose

            def done(ins, key):
                ins.then_inc(bank_full[bank(key)], 1)

            pe.wait_ge(consts_ready, 1)
            pe.wait_ge(small_in, SMALL_IN)
            turn(ps[:, 6, 0:P], gain_rows, ident[:, :])
            turn(ps[:, 6, P:P + 64], pos_rows, ident[0:64, 0:64])
            mm(ps[0:8, 7, :], table[0:33, 0:8], onehot, start=True, stop=True).then_inc(setup_pe, 1)
            pe.wait_ge(setup_dve, 1)

            def turn_residual(key, t, h):
                bank_taken_over(pe, key)
                for j in range(4):
                    ins = turn(ps[:, bank(key), P * j:P * j + P], xn[:, t, P * (4 * h + j):P * (4 * h + j + 1)], ident[:, :])
                done(ins, key)

            def turned_norm(L, which):
                N = 2 * L + (which == "norm2")
                for t in range(NT):
                    pe.wait_ge(xn_ready, NT * N + t + 1)
                    for h in range(2):
                        turn_residual((L, which, t, h), t, h)

            def project(L, c, t):
                c0, w = CHUNKS[c]
                key = (L, "proj", c, t)
                bank_taken_over(pe, key)
                weights_landed(pe, (L, "in", c))
                if c == 0:
                    for h in range(2):
                        bank_read(pe, (L, "norm1", t, h))
                wv = slot_view(slot_of((L, "in", c)), KD, w)
                b = ps[:, bank(key), 0:w]
                gate = c >= N_MIX_CHUNKS
                for k in range(KD):
                    ins = mm(b, hT[:, k, P * t:P * t + P], wv[:, k, :], start=(k == 0), stop=(k == KD - 1 and not gate))
                if gate:
                    row = 6 * L + c - N_MIX_CHUNKS
                    ins = mm(b, ident[0:12, row:row + 1].to_broadcast([12, P]), bgate[0:12, :], start=False, stop=True)
                done(ins, key)

            def turn_mixer_inputs(L, t):
                pe.wait_ge(heads_normed, NT * L + t + 1)
                p = proj[:, t, :]
                pairs = [xn[:, t, P * r:P * r + P] for r in range(4)]
                sources = [[p[:, c0:c0 + P] for c0 in (SBQ, SBQ + P, SBK, SBK + P)], pairs,
                           [p[:, c0:c0 + P] for c0 in (KS, KW, KC, VC)],
                           [p[:, c0:c0 + P] for c0 in (CQ, CQ + P, CKV)]]
                for b, group in enumerate(sources):
                    key = (L, "xt", t, b)
                    bank_taken_over(pe, key)
                    for j, src in enumerate(group):
                        ins = turn(ps[:, bank(key), P * j:P * j + P], src, ident[:, :])
                    done(ins, key)

            def latent_up(L, t):
                small = slot_view(slot_of((L, "small")), 1, 1536)[:, 0, :]
                bank_read(pe, (L, "xt", t, 3))
                weights_landed(pe, (L, "small"))
                key = (L, "uq", t)
                bank_taken_over(pe, key)
                for k in range(2):
                    ins = mm(ps[:, bank(key), 0:384], xT[:, 10 + k, P * t:P * t + P], small[:, 384 * k:384 * k + 384],
                             start=(k == 0), stop=(k == 1))
                done(ins, key)
                key = (L, "ukv", t)
                bank_taken_over(pe, key)
                done(mm(ps[:, bank(key), :], xT[:, 12, P * t:P * t + P], small[:, 768:1280], start=True, stop=True), key)

            def compress_hidden(L):
                key = (L, "c1")
                bank_taken_over(pe, key)
                for t in range(NT):
                    bank_read(pe, (L, "xt", t, 2))
                for kv in range(2):
                    weights_landed(pe, (L, "w1", kv))
                    w1 = slot_view(slot_of((L, "w1", kv)), 16, 256)
                    for hc in range(2):
                        o = (2 * kv + hc) * 45
                        for c in range(16):
                            ins = mm(ps[:, bank(key), o:o + 45], w1[:, c, P * hc:P * hc + P],
                                     cmp_x[:, kv, :, c:c + 8 * (N_CMP - 1) + 1:8], start=(c == 0), stop=(c == 15))
                done(ins, key)

            def compress_out(L):
                key = (L, "c2")
                small = slot_view(slot_of((L, "small")), 1, 1536)[:, 0, :]
                bank_taken_over(pe, key)
                pe.wait_ge(ch_act, L + 1)
                for kv in range(2):
                    for g in range(2):
                        o = (2 * kv + g) * HD
                        for hc in range(2):
                            w = 1280 + P * kv + HD * hc
                            ins = mm(ps[0:N_CMP, bank(key), o:o + HD], ch[:, 2 * kv + hc, N_CMP * g:N_CMP * g + N_CMP],
                                     small[:, w:w + HD], start=(hc == 0), stop=(hc == 1))
                done(ins, key)

            def job_scores(L, j):
                kind, i, r = JOBS[j]
                nk = P * (i + 1)
                key = (L, "s", j)
                bank_taken_over(pe, key)
                for h in range(2):
                    o = ps[:, bank(key), h * nk:h * nk + nk]
                    if kind == "mla":
                        ins = mm(o, mT[0:MQ, 2 * r + h, P * i:P * i + P], mT[0:MQ, 4 + 2 * r + h, 0:nk], start=True, stop=True)
                    else:
                        row = (8 if kind == "sel" else 9) + 2 * h
                        ins = mm(o, xT[:, 4 + r, P * i:P * i + P], xT[:, row, 0:nk], start=True, stop=True)
                done(ins, key)

            def job_turn(L, j):
                kind, i, r = JOBS[j]
                nk = P * (i + 1)
                n = len(JOBS) * L + j
                key = (L, "p", j)
                bank_taken_over(pe, key)
                pe.wait_ge(probs_ready, n + 1)
                for c in range(2 * (i + 1)):
                    ins = turn(ps[:, bank(key), P * c:P * c + P], probs[:, n % 3, P * c:P * c + P], ident[:, :])
                done(ins, key)

            def compressed_turn(L, i):
                pe.wait_ge(cmp_p, NT * L + i + 1)
                for half in range(2):
                    key = (L, "pc", i, half)
                    bank_taken_over(pe, key)
                    for h in range(4):
                        ins = turn(ps[0:N_CMP, bank(key), P * h:P * h + P], pcs[:, i, 4 * half + h, 0:N_CMP], ident[:, :])
                    done(ins, key)

            def job_value(L, j):
                kind, i, r = JOBS[j]
                n = len(JOBS) * L + j
                key = (L, "mlao", i, r) if kind == "mla" else (L, "nsao", i, r)
                if kind != "win":
                    bank_taken_over(pe, key)
                bank_read(pe, (L, "p", j))
                if kind == "win" and r == 0:
                    for h in range(2):
                        bank_read(pe, (L, "pc", i, h))
                for h in range(2):
                    o = ps[64 * h:64 * h + 64, bank(key), 0:P]
                    for kc in range(i + 1):
                        if kind == "mla":
                            v = mv[:, kc, 2 * r + h, :]
                        else:
                            v0 = (VS if kind == "sel" else VW) + HD * h
                            v = proj[:, kc, v0:v0 + HD]
                        c = h * (i + 1) + kc
                        ins = mm(o, v, probsT[:, n % 2, P * c:P * c + P], start=(kind != "win" and kc == 0),
                                 stop=(kind == "mla" and kc == i))
                    if kind == "win":
                        ins = mm(o, ckv_c[0:N_CMP, 2 + h, :], pcT[0:N_CMP, 4 * h + r, :], start=False, stop=True)
                ins.then_inc(pv_done, 1)

            def mixers(L):
                turned_norm(L, "norm1")
                for c in range(6):
                    for t in range(NT):
                        project(L, c, t)
                for t in range(NT):
                    turn_mixer_inputs(L, t)
                for t in range(NT):
                    project(L, 6, t)
                for t in range(NT):
                    latent_up(L, t)
                compress_hidden(L)
                for t in range(NT):
                    bank_read(pe, (L, "xt", t, 0))
                for h in range(4):
                    key = (L, "z", h)
                    bank_taken_over(pe, key)
                    r = slice(64 * (h % 2), 64 * (h % 2) + 64)
                    mm(ps[:, bank(key), 0:SEQ], xT[r, 2 + h // 2, 0:P], xT[r, h // 2, :], start=True, stop=True)
                    done(mm(ps[:, bank(key), SEQ:SEQ + P], xT[r, 2 + h // 2, P:SEQ], xT[r, h // 2, P:SEQ],
                            start=True, stop=True), key)
                compress_out(L)
                for t in range(NT):
                    project(L, 7, t)
                key = (L, "kct")
                bank_taken_over(pe, key)
                pe.wait_ge(ck_ready, L + 1)
                done(turn(ps[:, bank(key), 0:N_CMP], ckv_c[0:N_CMP, 0:2, :].rearrange("p g d -> p (g d)"),
                          ident[0:N_CMP, 0:N_CMP]), key)
                for t in range(NT):
                    pe.wait_ge(mla_ready, NT * L + t + 1)
                    for b in range(2):
                        key = (L, "mt", t, b)
                        bank_taken_over(pe, key)
                        for j in range(4):
                            ins = turn(ps[0:MQ, bank(key), P * j:P * j + P], mqk[:, t, 4 * b + j, :], ident[:, :])
                        done(ins, key)
                pe.wait_ge(stick_sp, L + 1)
                for h in range(4):
                    key = (L, "S", h)
                    bank_taken_over(pe, key)
                    b = ps[:, bank(key), :]
                    mm(b[:, 0:SEQ], tri_ge[:, :], stick_tmp[:, h, 0:SEQ], start=True, stop=False)
                    mm(b[:, P:SEQ], ones[:, :], stick_tmp[:, h, SEQ:SEQ + P], start=False, stop=True)
                    done(mm(b[:, SEQ:SEQ + P], tri_ge[:, :], stick_tmp[:, h, SEQ:SEQ + P], start=True, stop=True), key)
                if L == 0:
                    pe.wait_ge(bias_in, 16)
                    for h in range(8):
                        key = (0, "flip", h)
                        bank_taken_over(pe, key)
                        done(mm(ps[:, bank(key), 0:384], flip, bias[:, h, :], start=True, stop=True), key)
                bank_read(pe, (L, "kct"))
                pe.wait_ge(keys_split, L + 1)
                for i in range(NT):
                    key = (L, "sc", i)
                    bank_taken_over(pe, key)
                    for h in range(8):
                        g, r = h // 4, h % 4
                        ins = mm(ps[:, bank(key), 16 * h:16 * h + N_CMP], xT[:, 4 + r, P * i:P * i + P],
                                 kcT[:, g, 0:N_CMP], start=True, stop=True)
                    done(ins, key)
                pe.wait_ge(stick_w, L + 1)
                for hp in range(2):
                    key = (L, "sbo", hp)
                    bank_taken_over(pe, key)
                    for a_ in range(2):
                        h = 2 * hp + a_
                        o = ps[64 * a_:64 * a_ + 64, bank(key), :]
                        v0 = SBV + HD * h
                        mm(o[:, 0:SEQ], proj[:, 0, v0:v0 + HD], stick[:, h, 0:SEQ], start=True, stop=False)
                        ins = mm(o[:, P:SEQ], proj[:, 1, v0:v0 + HD], stick[:, h, SEQ:SEQ + P], start=False, stop=True)
                    ins.then_inc(stick_out, 1)
                for t in range(NT):
                    for b in range(2):
                        bank_read(pe, (L, "mt", t, b))
                for s in range(STEPS):
                    if s < len(JOBS):
                        job_scores(L, s)
                    if 0 <= s - LAG_PV < len(JOBS):
                        job_value(L, s - LAG_PV)
                    j = s - LAG_TURN
                    if 0 <= j < len(JOBS):
                        for i in range(NT):
                            if j == FIRST_SPARSE[i]:
                                compressed_turn(L, i)
                        job_turn(L, j)
                    if s in LATE_GATES:
                        project(L, *LATE_GATES[s])
                for r in (2, 3):
                    bank_read(pe, (L, "nsao", NT - 1, r))
                for k in range(2):
                    weights_landed(pe, (L, "wo", k))
                wo = [slot_view(slot_of((L, "wo", k)), 4, D) for k in range(2)]
                for t in range(NT):
                    for h in range(2):
                        for m, ks in enumerate(((0, 1), (2, 3, 4, 5), (6, 7))):
                            key = (L, "y", t, h, m)
                            bank_taken_over(pe, key)
                            for k in ks:
                                ins = mm(ps[:, bank(key), :], yT[:, k, P * t:P * t + P],
                                         wo[k // 4][:, k % 4, 512 * h:512 * h + 512], start=(k == ks[0]), stop=(k == ks[-1]))
                            done(ins, key)
                for t in range(NT):
                    for h in range(2):
                        pe.wait_ge(merged, 4 * L + 2 * t + h + 1)
                        turn_residual((L, "merge", t, h), t, h)
                for k in range(2):
                    weights_landed(pe, (L, "wout", k))
                wout = [slot_view(slot_of((L, "wout", k)), 4, D) for k in range(2)]
                for t in range(NT):
                    for h in range(2):
                        bank_read(pe, (L, "merge", t, h))
                    for h in range(2):
                        key = (L, "out", t, h)
                        bank_taken_over(pe, key)
                        for k in range(KD):
                            ins = mm(ps[:, bank(key), :], hT[:, k, P * t:P * t + P],
                                     wout[k // 4][:, k % 4, 512 * h:512 * h + 512], start=(k == 0), stop=(k == KD - 1))
                        done(ins, key)
                turned_norm(L, "norm2")

            def ffn(chunks, q0, n0, tiles, widths, hi, lo, gate_bank, up_bank, turn_bank, y_bank, before_last=None,
                    before_last_down=None, y_free=None, extra=None):
                T = len(tiles)

                def products(q, kind, u, half):
                    rows, cols = chunk_shape(kind, widths[u])
                    rows //= 2
                    wh, wl = (v[q % SPLIT_BUFS][:, 0:rows * cols].rearrange("p (k w) -> p k w", k=rows) for v in (w_hi, w_lo))
                    first = half == 0 and (kind != "down" or u == 0)
                    last = half == 1 and (kind != "down" or u == len(widths) - 1)

                    def sweep(weights, which, opening, closing):
                        for t in tiles:
                            for k in range(rows):
                                kk = half * rows + k
                                for n, part in enumerate(which):
                                    if kind == "down":
                                        b = t if T > 1 else u % 2
                                        lhs = (a_hi, a_lo)[part][:, b, P * kk:P * kk + P]
                                    else:
                                        lhs = (hi, lo)[part](kk, t)
                                    for h in range(2 if kind == "down" else 1):
                                        if kind == "down":
                                            out_, rhs = ps[:, y_bank(t) + h, :], weights[:, k, 512 * h:512 * h + 512]
                                        else:
                                            out_ = ps[:, (gate_bank if kind == "gate" else up_bank)(t), 0:cols]
                                            rhs = weights[:, k, :]
                                        ins = mm(out_, lhs, rhs, start=(opening and k == 0 and n == 0),
                                                 stop=(closing and k == rows - 1 and n == len(which) - 1))
                        return ins

                    pe.wait_ge(hi_ready, q0 + (q + 1))
                    sweep(wh, (0, 1), first, False)
                    pe.wait_ge(lo_ready, q0 + (q + 1))
                    sweep(wl, (0,), False, last).then_inc(half_done, 1)

                def turn_hidden(u):
                    for t in tiles:
                        pe.wait_ge(act_ready, n0 + (u * T + t + 1))
                        for j in range(widths[u] // P):
                            ins = turn(ps[:, turn_bank(t), P * j:P * j + P], act[:, t, P * j:P * j + P], ident[:, :])
                        ins.then_inc(act_turned, 1)

                for m, (kind, u) in enumerate(chunks):
                    if kind == "gate" and u > 0:
                        pe.wait_ge(silu_done, n0 + u * T)
                    if kind == "up" and u > 0:
                        pe.wait_ge(a_lo_ready, n0 + u * T)
                    if kind == "down":
                        if u == len(widths) - 1:
                            if before_last:
                                before_last()
                            turn_hidden(u)
                            if before_last_down:
                                before_last_down()
                        pe.wait_ge(a_lo_ready, n0 + (u + 1) * T)
                        if u == 0 and y_free:
                            y_free()
                    for half in range(2):
                        products(2 * m + half, kind, u, half)
                        if kind == "gate" and half == 0 and u > 0:
                            turn_hidden(u - 1)
                        if extra and m == 1 and half == 1:
                            extra()

            mixers(0)

            pe.wait_ge(h_hi_ready, 4)
            pe.wait_ge(h_lo_ready, 4)
            ffn(DENSE_CHUNKS, 0, 0, range(NT), [w for _, w in DENSE_GROUPS],
                lambda k, t: h_hi[:, k, P * t:P * t + P], lambda k, t: h_lo[:, k, P * t:P * t + P],
                lambda t: t, lambda t: 2 + t, lambda t: 2 + t, lambda t: 4 + 2 * t)
            mixers(1)

            for t in range(NT):
                for h in range(2):
                    bank_read(pe, (DEPTH - 1, "norm2", t, h))
            for t in range(NT):
                for k in range(KD):
                    ins = mm(ps[:, 1, 8 * t:8 * t + 8], hT[:, k, P * t:P * t + P], router[:, k, :],
                             start=(k == 0), stop=(k == KD - 1))
            ins.then_inc(route_pe, 1)
            pe.wait_ge(route_dve, 2)
            pe.wait_ge(consts_ready, 2)
            sel = route[:, 5]
            mm(ps[:, 1, 0:8], tri_lt, sel[:, 0, :], start=True, stop=True)
            mm(ps[:, 1, 8:16], ones[:, :], sel[:, 0, :], start=True, stop=False)
            mm(ps[:, 1, 8:16], tri_lt, sel[:, 1, :], start=False, stop=True)
            mm(ps[:, 1, 16:24], ones[:, :], sel[:, 0, :], start=True, stop=False)
            mm(ps[:, 1, 16:24], ones[:, :], sel[:, 1, :], start=False, stop=True).then_inc(route_pe, 1)

            def gather(it, h, first=False):
                if h == 0:
                    pe.wait_ge(pick_ready, it + 1)
                if not first:
                    pe.wait_ge(added, it * 4 - 3)
                for j in range(4):
                    k = 4 * h + j
                    for t in range(NT):
                        ins = mm(ps[:, 6 + h, P * j:P * j + P], xn[:, t, P * k:P * k + P], pick[:, t, :],
                                 start=(t == 0), stop=(t == NT - 1))
                ins.then_inc(gathered, 1)

            def turn_put(it):
                for t in range(NT):
                    ins = turn(ps[:, 1, P * t:P * t + P], put[:, t, :], ident[:, :])
                ins.then_inc(put_turned, 1)

            gather(0, 0, True)
            gather(0, 1, True)
            pe.wait_ge(routed, 2)
            pe.sem_inc(spread, 1)

            def expert(pair, o):
                it = pair * PAIR + o
                pe.wait_ge(e_lo_ready, it * 2 + 2)
                ffn(EXPERT_CHUNKS, it * EXPERT_HALVES + DENSE_HALVES, it * EXPERT_UNITS + NT * len(DENSE_GROUPS),
                    (0,), [512] * EXPERT_UNITS, lambda k, t: e_hi[:, k, :], lambda k, t: e_lo[:, k, :],
                    lambda t: 2, lambda t: 3, lambda t: 0, lambda t: 4,
                    before_last=lambda: gather(it + 1, 0), before_last_down=lambda: gather(it + 1, 1),
                    extra=lambda: turn_put(it), y_free=lambda: pe.wait_ge(added, it * 4 + 1))
                pe.wait_ge(ye_ready, it + 2)
                pe.wait_ge(ye_copied, it + 1)
                pe.wait_ge(putT_ready, it + 1)
                for k in range(4):
                    t, h = k // 2, k % 2
                    if k < 2:
                        pe.wait_ge(gains_applied, it * 2 + (3 + k))
                    mm(ps[:, SPREAD_BANKS[k], :], putT[:, P * t:P * t + P], ye[:, 512 * h:512 * h + 512],
                       start=True, stop=True).then_inc(spread, 1)

            with pe.Fori(0, PAIRS) as pair:
                for o in range(PAIR):
                    expert(pair, o)
            crowded = pe.value_load(flag_i[0:1, 0:1], min_val=0, max_val=1)
            with pe.If(crowded > 0):
                with pe.Fori(PAIRS, 2 * PAIRS) as pair:
                    for o in range(PAIR):
                        expert(pair, o)


_INS = ['x', 'rel_bias_table', 'mix_norm', 'w_in', 'b_gate', 'sb_w_o', 'nsa_q_norm', 'nsa_k_norm', 'nsa_cmp_pos',
        'nsa_cmp_w1', 'nsa_cmp_w2', 'nsa_w_o', 'mla_q_a_norm', 'mla_kv_a_norm', 'mla_w_uq', 'mla_w_ukv', 'mla_q_norm',
        'mla_k_norm', 'mla_w_o', 'w_out', 'ffn_norm', 'dense_w_gate', 'dense_w_up', 'dense_w_down', 'moe_router',
        'moe_w_gate', 'moe_w_up', 'moe_w_down']


def shape_constants():
    import math
    import numpy as np
    rel = np.arange(SEQ)
    n = np.maximum(rel, 1).astype(np.float32)
    large = 16 + (np.log(n / np.float32(16)) / np.float32(math.log(1024 / 16)) * np.float32(16)).astype(np.int32)
    bucket = np.where(rel < 16, rel, np.minimum(large, 31))
    onehot = np.zeros((33, 512), np.float32)
    for j in range(512):
        d = SEQ - 1 - j
        onehot[bucket[d] if d >= 0 else 32, j] = 1.0
    inv = np.float32(10000.0) ** (-np.arange(16, dtype=np.float32) / np.float32(16))
    ang = np.arange(SEQ, dtype=np.float32)[:, None] * inv[None, :]
    trig = np.stack([np.cos(ang), np.sin(ang)]).astype(np.float32)
    return onehot, np.ascontiguousarray(trig.reshape(2, NT, P, 16).transpose(2, 0, 1, 3))


def kernel(**inputs):
    import numpy as _np
    import concourse.bacc as _bacc
    from concourse import mybir as _mybir
    from concourse.bass_utils import run_bass_kernel_spmd as _run

    nc = _bacc.Bacc("TRN2", target_bir_lowering=False, num_devices=1)
    arrays, args = {}, {}
    onehot, trig = shape_constants()
    for name, arr in [(n, inputs[n]) for n in _INS] + [("bucket_onehot", onehot), ("rope_tables", trig)]:
        v = _np.ascontiguousarray(arr)
        arrays[f"in_{name}_dram"] = v
        args[name] = nc.dram_tensor(f"in_{name}_dram", v.shape, _mybir.dt.from_np(v.dtype), kind="ExternalInput").ap()
    out = nc.dram_tensor("out_0_dram", (1, SEQ, D), _mybir.dt.float32, kind="ExternalOutput").ap()
    trunk(nc, args, out)
    r = _run(nc, [arrays], core_ids=[0])
    return r.results[0]["out_0_dram"]
```

```python
from contextlib import ExitStack

import concourse.bass as bass
from concourse import mybir

ALU = mybir.AluOpType
ACT = mybir.ActivationFunctionType
F32 = mybir.dt.float32
F32R = mybir.dt.float32r
U32 = mybir.dt.uint32
I32 = mybir.dt.int32
AX = mybir.AxisListType

P = 128
SEQ, D = 256, 1024
NT = SEQ // P
KD = D // P
DEPTH = 2
HD = 64
EPS = 1e-6
NEG = -1e30

SBQ, SBK, SBV = 0, 256, 512
NQ, KC, VC, KS, VS, KW, VW, NG = 768, 1280, 1408, 1536, 1664, 1792, 1920, 2048
CQ, CKV, KR, GATES = 2072, 2328, 2456, 2488
IN_COLS = 5560
CHUNKS = [(c, min(512, GATES - c)) for c in range(0, GATES, 512)] + [(c, 512) for c in range(GATES, IN_COLS, 512)]
N_MIX_CHUNKS = 5
BGATE_LO = 32
SPLIT_CHUNKS = 7
IN_HALVES = 2 * SPLIT_CHUNKS

N_CMP = 15
CMP_ROWS = 2 * 16 + N_CMP
MQ = 96
FF_DENSE, FF_EXPERT, N_EXPERTS = 2816, 3584, 8
EXPERT_UNITS = FF_EXPERT // 512
DENSE_GROUPS = [(f, min(512, FF_DENSE - f)) for f in range(0, FF_DENSE, 512)]

SLOT = 4096
RING = 4
MOE_RING = 6

JOBS = ([("mla", i, hp) for i in range(NT) for hp in range(2)]
        + [(kind, i, r) for i in range(NT) for r in range(4) for kind in ("sel", "win")])
FIRST_SPARSE = {i: JOBS.index(("sel", i, 0)) for i in range(NT)}
LAG_TURN, LAG_PV = 2, 3
STEPS = len(JOBS) + LAG_PV
LATE_UNITS = [(c, t) for c in (8, 9, 10) for t in range(NT)]
LATE_STEPS = STEPS - 2
LATE_PRODUCTS = [[(unit, k) for n, (unit, k) in enumerate((u, k) for u in LATE_UNITS for k in range(KD))
                  if n * LATE_STEPS // (len(LATE_UNITS) * KD) == s] for s in range(STEPS)]
LATE_GATES = {s: unit for s, products in enumerate(LATE_PRODUCTS) for unit, k in products if k == KD - 1}
assert len(LATE_GATES) == len(LATE_UNITS)


def bank_uses():
    banks = {"turn": (0, 1), "proj": (2, 3), "score": (4, 5), "outp": (6, 7), "wide": (2, 3, 4, 5)}
    turns, count, plan = {kind: 0 for kind in banks}, [0] * 8, {}

    def use(kind, keys):
        for key in keys:
            b = banks[kind][turns[kind] % len(banks[kind])]
            assert key not in plan
            plan[key] = (b, count[b])
            turns[kind] += 1
            count[b] += 1

    for L in range(DEPTH):
        use("turn", [(L, "norm1", t, h) for t in range(NT) for h in range(2)])
        use("turn", [(L, "xt", t, b) for t in range(NT) for b in range(4)])
        use("turn", [(L, "kct")])
        use("turn", [(L, "mt", t, b) for t in range(NT) for b in range(2)])
        for j, (kind, i, r) in enumerate(JOBS):
            if j == FIRST_SPARSE[i]:
                use("turn", [(L, "pc", i, h) for h in range(2)])
            use("turn", [(L, "p", j)])
        use("turn", [(L, "merge", t, h) for t in range(NT) for h in range(2)])
        use("turn", [(L, "norm2", t, h) for t in range(NT) for h in range(2)])
        use("wide", [(L, "proj", c, t) for c in range(SPLIT_CHUNKS) for t in range(NT)])
        use("proj", [(L, w, t) for t in range(NT) for w in ("uq", "ukv")])
        use("proj", [(L, "c1"), (L, "c1t")] + [(L, "proj", 7, t) for t in range(NT)] + [(L, "c2")])
        use("proj", [(L, "proj", *LATE_GATES[s]) for s in sorted(LATE_GATES)])
        use("proj", [(L, "y", t, h, m) for t in range(NT) for h in range(2) for m in range(3)])
        use("proj", [(L, "out", t, h) for t in range(NT) for h in range(2)])
        use("score", [(L, "z", h) for h in range(4)] + [(L, "S", h) for h in range(4)])
        use("score", [(L, "sc", i) for i in range(NT)] + [(L, "s", j) for j in range(len(JOBS))])
        if L == 0:
            use("outp", [(L, "flip", h) for h in range(8)])
        use("outp", [(L, "sbo", hp) for hp in range(2)] + [(L, "mlao", i, hp) for i in range(NT) for hp in range(2)])
        use("outp", [(L, "nsao", i, r) for i in range(NT) for r in range(4)])
    return plan


def weight_chunks():
    seq, slots = [], []
    for L in range(DEPTH):
        seq += [(L, "in", c) for c in range(SPLIT_CHUNKS)] + [(L, "small"), (L, "w1", 0), (L, "w1", 1)]
        slots += [0, 1, 2, 0, 1, 2, 0] + [1, 2, 3]
        seq += [(L, "in", c) for c in range(SPLIT_CHUNKS, 11)] + [(L, "wo", 0), (L, "wo", 1), (L, "wout", 0), (L, "wout", 1)]
        slots += [0, 1, 2, 3] + [0, 1, 2, 3]
        if L == 0:
            seq += [(L, kind, g) for kind, g in DENSE_CHUNKS]
            slots += [m % RING for m in range(len(DENSE_CHUNKS))]
    assert len(seq) == len(slots)
    return seq, slots




def ffn_chunks(units):
    seq = [("gate", 0), ("up", 0)]
    for u in range(1, units):
        seq += [("gate", u), ("down", u - 1), ("up", u)]
    return seq + [("down", units - 1)]


DENSE_CHUNKS = ffn_chunks(len(DENSE_GROUPS))
EXPERT_CHUNKS = ffn_chunks(EXPERT_UNITS)
DENSE_HALVES = 2 * len(DENSE_CHUNKS)
EXPERT_HALVES = 2 * len(EXPERT_CHUNKS)
PAIRS = N_EXPERTS // 2
SPREAD_BANKS = (6, 7, 4, 5)
PAIR = 2
SPLIT_BUFS = 3
PASSES_OF_RING = PAIR * len(EXPERT_CHUNKS) // MOE_RING
assert PASSES_OF_RING * MOE_RING == PAIR * len(EXPERT_CHUNKS) and DENSE_HALVES % SPLIT_BUFS == 0 and EXPERT_HALVES % SPLIT_BUFS == 0

G_MIX, G_FFN, G_LAYER = 0, DEPTH * KD, 2 * DEPTH * KD
G_Q, G_K, G_LATENT = G_LAYER, G_LAYER + DEPTH, G_LAYER + 4 * DEPTH
GAINS_IN, SMALL_IN = 16 * (4 + 2 * DEPTH), 16 * (6 + 2 * DEPTH)


def trunk(nc, a, out):
    uses = bank_uses()
    chunk_seq, chunk_slots = weight_chunks()
    chunk_no = {key: n for n, key in enumerate(chunk_seq)}
    slot_no = dict(zip(chunk_seq, chunk_slots))

    with ExitStack() as ctx:
        def sb(name, shape, dt=F32):
            return ctx.enter_context(nc.sbuf_tensor(name, shape, dt))

        def sem(name):
            return ctx.enter_context(nc.semaphore(name))

        ps = ctx.enter_context(nc.psum_tensor("ps", [P, 8, 512], F32))

        PROJ0 = RING * SLOT
        BIAS0 = PROJ0 + NT * IN_COLS
        TMP0 = BIAS0 + 8 * 384
        CMP0 = TMP0 + 1536
        MT0 = CMP0 + 768
        PROBST0 = MT0 + 2048
        PCT0 = PROBST0 + 1024
        arena_at = -(-nc.sbuf_base // 32) * 32
        arena = sb("arena", [P, PCT0 + 1024])
        proj = arena[:, PROJ0:BIAS0].rearrange("p (t n) -> p t n", t=NT)
        bias = arena[:, BIAS0:TMP0].rearrange("p (h k) -> p h k", h=8)
        tmp = arena[:, TMP0:CMP0]
        cmp_x = arena[:, CMP0:MT0].rearrange("p (v g n) -> p v g n", v=2, g=3)
        cmp_tokens = arena[:, CMP0:MT0].rearrange("p (v n) -> p v n", v=2)
        mT = arena[:, MT0:PROBST0].rearrange("p (h q) -> p h q", h=8)
        probsT = arena[:, PROBST0:PCT0].rearrange("p (b n) -> p b n", b=2)
        pcT = arena[:, PCT0:].rearrange("p (h q) -> p h q", h=8)

        def rounded(name, shape, at):
            return nc.alloc_sbuf_tensor_at(name, shape, F32R, offset=arena_at + 4 * at)

        w_hi = [rounded(f"w_hi{b}", [P, SLOT // 2], PROJ0 + b * (SLOT // 2)) for b in range(2)]
        w_lo = [rounded(f"w_lo{b}", [P, SLOT // 2], PROJ0 + SLOT + b * (SLOT // 2)) for b in range(2)]
        h_hi = rounded("h_hi", [P, KD, SEQ], PROJ0 + 2 * SLOT)
        h_lo = rounded("h_lo", [P, KD, SEQ], MT0)
        e_hi = rounded("e_hi", [P, KD, P], MT0)
        e_lo = rounded("e_lo", [P, KD, P], MT0 + 1024)
        a_hi = rounded("a_hi", [P, 2, 512], PROBST0)
        a_lo = rounded("a_lo", [P, 2, 512], PCT0)
        slot_at = [n * SLOT for n in range(RING)] + [PROJ0 + 2 * SLOT, PROJ0 + 3 * SLOT]
        slot_order = [slot_no[DEPTH - 1, "wo", k] for k in range(2)] + [RING, RING + 1]
        slot_order += [slot_no[DEPTH - 1, "wout", k] for k in range(2)]
        assert sorted(slot_order) == list(range(MOE_RING))
        assert PROJ0 + 4 * SLOT <= MT0 and PROJ0 + 2 * SLOT + 2048 <= BIAS0
        x = sb("x", [P, NT, D])
        xn = sb("xn", [P, NT, D])
        hT = sb("hT", [P, KD, SEQ])
        xT = sb("xT", [P, 13, SEQ])
        heads_at = -(-nc.sbuf_base // 32) * 32
        heads = sb("heads", [P, NT * 8 * MQ + NT * 4 * HD])
        mqk = heads[:, 0:NT * 8 * MQ].rearrange("p (t h d) -> p t h d", t=NT, h=8)
        mv = heads[:, NT * 8 * MQ:].rearrange("p (t h d) -> p t h d", t=NT, h=4)
        probs = mqk[:, :, :, :].rearrange("p t h d -> p (t h d)").rearrange("p (b n) -> p b n", b=3)
        pcs = cmp_x[:, 0, 0:2, :].rearrange("p g (h n) -> p g h n", h=8)
        yT_at = -(-nc.sbuf_base // 32) * 32
        yT = sb("yT", [P, 8, SEQ])
        w_hi.append(nc.alloc_sbuf_tensor_at("w_hi2", [P, SLOT // 2], F32R, offset=heads_at))
        w_lo.append(nc.alloc_sbuf_tensor_at("w_lo2", [P, SLOT // 2], F32R, offset=yT_at))
        n_hi, n_lo = w_hi[2][:, :].rearrange("p (k q) -> p k q", k=KD), h_lo
        in_hi = [rounded(f"in_hi{b}", [P, SLOT // 2], 3 * SLOT + b * (SLOT // 2)) for b in range(2)]
        in_lo = [w_lo[2], rounded("in_lo1", [P, SLOT // 2], PROBST0)]
        ident = sb("ident", [P, P])
        tri_ge = sb("tri_ge", [P, P])
        ones = sb("ones", [P, P])
        stick_mask = sb("stick_mask", [P, 384])
        causal = sb("causal", [P, SEQ])
        gain_rows = pcT[:, 0, :]
        pos_rows = tmp[0:64, 1024:1024 + P]
        rope_tmp = pcT[:, 0:4, :]
        flip = sb("flip", [P, P])
        gains = sb("gains", [P, 64])
        posT = sb("posT", [P, 4, 16])
        mla_gain = sb("mla_gain", [P, DEPTH, 2, MQ])
        trig = sb("trig", [P, 2, NT, 16])
        bgate = sb("bgate", [BGATE_LO + 12, 512], F32R)
        gate_row = sb("gate_row", [BGATE_LO + 12, 12], F32R)
        bgate_in = proj[0:12, 1, IN_COLS - 512:IN_COLS]
        router = sb("router", [P, KD, N_EXPERTS])
        table = sb("table", [64, 8])
        sums = sb("sums", [P, NT, 20])
        inv_n = sb("inv_n", [P, 20])
        mhalf = sb("mhalf", [P, 20])
        ssum = sb("ssum", [P, NT])
        msum = sb("msum", [P, NT, 8])
        ksum = sb("ksum", [P, 2])
        nmax = sb("nmax", [P, 3, 2])
        prob_sum = sb("prob_sum", [P, 3, 2])
        prec = sb("prob_scale", [P, 3, 2])
        ngate = sb("ngate", [P, NT, 24])
        cmax = sb("cmax", [P, 8])
        csum = sb("csum", [P, 8])
        valid = sb("valid", [P, NT])
        early = yT[:, :, :].rearrange("p a b -> p (a b)")
        ch_raw, ch, ce = (early[:, o:o + 4 * n].rearrange("p (f n) -> p f n", f=4) for o, n in ((0, 48), (192, 30), (312, 30)))
        ckv_c = cmp_x[0:16, 1, 0:2, :].rearrange("p g (f d) -> p (g f) d", f=2)
        c1_rows = early[0:CMP_ROWS, 1024:1536]
        csq = early[0:16, 512:640].rearrange("p (g d) -> p g d", g=2)
        kcT = sb("kcT", [P, 2, 16])
        NS = 2 * N_EXPERTS + 1
        xTf = xT[:, :, :].rearrange("p a b -> p (a b)")
        slots, comb = (xTf[:, o:o + NT * NS].rearrange("p (t e) -> p t e", t=NT) for o in (0, 64))
        route = xTf[:, 128:320].rearrange("p (v t e) -> p v t e", v=12, t=NT)
        top_i = sb("top_i", [P, NT, 8], U32)
        flag = sb("flag", [P, 2])
        flag_i = sb("flag_i", [P, 1], I32)
        now = sb("now", [P, 4])
        ye = xTf[:, 1024:2048]
        pick = xTf[:, 2048:2304].rearrange("p (t s) -> p t s", t=NT)
        put = xTf[:, 2304:2560].rearrange("p (t s) -> p t s", t=NT)
        putT = xTf[:, 2560:2816]
        iota = xTf[:, 2816:2944]
        tri_lt = xTf[:, 2944:3072]
        iota8 = xTf[:, 3072:3080]
        hTf = hT[:, :, :].rearrange("p k q -> p (k q)")
        act_g, act = (hTf[:, o:o + 1024].rearrange("p (b n) -> p b n", b=2) for o in (0, 1024))
        gathered_f = [hTf[:, o:o + 512] for o in (512, 1536)]
        stick = xn[:, :, :].rearrange("p a b -> p (a b)")[:, 0:1536].rearrange("p (h k) -> p h k", h=4)
        stick_tmp = tmp.rearrange("p (h k) -> p h k", h=4)
        rvec = tmp[0:8, 0:512]
        onehot = tmp[0:33, 512:1024]
        bias_dram = nc.dram_tensor("bias_by_distance", (8, 512), F32, kind="Internal").ap()

        bank_full = [sem(f"bank{b}_full") for b in range(8)]
        bank_free = [sem(f"bank{b}_free") for b in range(8)]
        slot_full = [sem(f"slot{s}_full") for s in range(MOE_RING)]
        gains_in = sem("gains_in")
        small_in = sem("small_in")
        bgate_ready = sem("bgate_ready")
        x_in = sem("x_in")
        consts_ready = sem("consts_ready")
        bias_out, bias_in = sem("bias_out"), sem("bias_in")
        v_done, a_done, g_done = sem("vector_done"), sem("scalar_done"), sem("gpsimd_done")
        setup_pe, setup_dve = sem("setup_pe"), sem("setup_dve")
        sq_ready, sums_ready, rstd_ready, xn_ready = sem("sq_ready"), sem("sums_ready"), sem("rstd_ready"), sem("xn_ready")
        head_sq, head_sums, head_rstd, heads_normed = sem("head_sq"), sem("head_sums"), sem("head_rstd"), sem("heads_normed")
        cmp_x_ready = sem("cmp_x_ready")
        mla_in, mla_rope_in, mla_sq, mla_sums, mla_rstd, mla_ready = (
            sem("mla_in"), sem("mla_rope_in"), sem("mla_sq"), sem("mla_sums"), sem("mla_rstd"), sem("mla_ready"))
        ng_exp = sem("ng_exp")
        stick_out = sem("stick_out")
        keys_split = sem("keys_split")
        ch_ready, ch_exp, ch_act = sem("ch_ready"), sem("ch_exp"), sem("ch_act")
        ck_sums, ck_rstd, ck_ready = sem("ck_sums"), sem("ck_rstd"), sem("ck_ready")
        stick_z, stick_ln, stick_sp, stick_t, stick_w = (
            sem("stick_z"), sem("stick_ln"), sem("stick_sp"), sem("stick_t"), sem("stick_w"))
        cmp_s, cmp_e, cmp_p = sem("cmp_s"), sem("cmp_e"), sem("cmp_p")
        max_ready, exp_ready, probs_ready, pv_done = sem("max_ready"), sem("exp_ready"), sem("probs_ready"), sem("pv_done")
        gates_ready, merged, x_mixed = sem("gates_ready"), sem("merged"), sem("x_mixed")
        h_hi_ready, h_lo_ready = sem("h_hi_ready"), sem("h_lo_ready")
        n_hi_ready, n_lo_ready = sem("n_hi_ready"), sem("n_lo_ready")
        in_hi_ready, in_lo_ready, in_used = sem("in_hi_ready"), sem("in_lo_ready"), sem("in_used")
        hi_ready, lo_ready = sem("hi_ready"), sem("lo_ready")
        half_done = sem("half_done")
        silu_done, act_ready = sem("silu_done"), sem("act_ready")
        act_turned, a_hi_ready, a_lo_ready = sem("act_turned"), sem("a_hi_ready"), sem("a_lo_ready")
        x_dense = sem("x_dense")
        route_pe, route_dve, route_exp, routed = sem("route_pe"), sem("route_dve"), sem("route_exp"), sem("routed")
        now_ready, pick_ready = sem("now_ready"), sem("pick_ready")
        gathered, gains_applied, e_hi_ready, e_lo_ready = sem("gathered"), sem("gains_applied"), sem("e_hi_ready"), sem("e_lo_ready")
        put_turned, putT_ready = sem("put_turned"), sem("putT_ready")
        ye_ready, ye_copied, spread, added = sem("ye_ready"), sem("ye_copied"), sem("spread"), sem("added")
        x_final, out_done = sem("x_final"), sem("out_done")

        def bank(key):
            return uses[key][0]

        def bank_taken_over(pe, key):
            b, n = uses[key]
            if n > 0:
                pe.wait_ge(bank_free[b], n)

        def bank_written(eng, key):
            b, n = uses[key]
            eng.wait_ge(bank_full[b], n + 1)

        def bank_read(eng, key):
            b, n = uses[key]
            eng.wait_ge(bank_free[b], n + 1)

        def slot_of(key):
            return slot_no[key]

        landed_value, slot_total = [], [0] * MOE_RING
        for n, key in enumerate(chunk_seq):
            slot_total[slot_no[key]] += 16 * {"small": 4, "wo": 3}.get(key[1], 1)
            landed_value.append(slot_total[slot_no[key]])

        def weights_landed(pe, key):
            pe.wait_ge(slot_full[slot_no[key]], landed_value[chunk_no[key]])

        def expert_slot(n, k, w):
            o = slot_at[slot_order[n % MOE_RING]]
            return arena[:, o:o + k * w].rearrange("p (k w) -> p k w", k=k)

        def expert_half(n, q):
            w = SLOT // 2
            o = slot_at[slot_order[n % MOE_RING]] + w * (q % 2)
            return arena[:, o:o + w], w

        def expert_landed(eng, pair, n):
            s = slot_order[n % MOE_RING]
            eng.wait_ge(slot_full[s], pair * (16 * PASSES_OF_RING) + (slot_total[s] + 16 * (n // MOE_RING + 1)))

        def projection_half_used(eng, L, j):
            if j % 2:
                bank_written(eng, (L, "proj", j // 2, NT - 1))
            else:
                eng.wait_ge(in_used, L * SPLIT_CHUNKS + (j // 2 + 1))

        def projection_half(L, j):
            w = KD // 2 * CHUNKS[j // 2][1]
            o = slot_of((L, "in", j // 2)) * SLOT + w * (j % 2)
            return arena[:, o:o + w], w

        def ffn_half(L, q):
            if L:
                return expert_half(q // 2, q)
            w = SLOT // 2
            o = slot_of((0, *DENSE_CHUNKS[q // 2])) * SLOT
            return arena[:, o + w * (q % 2):o + w * (q % 2) + w], w

        def chunk_shape(kind, w):
            return (w // P, D) if kind == "down" else (KD, w)

        def slot_view(s, k, w):
            return arena[:, s * SLOT:s * SLOT + k * w].rearrange("p (k w) -> p k w", k=k)

        block = ctx.enter_context(nc.Block())

        @block.sync
        def _(sp):
            def rows(ap):
                return ap.rearrange("(k p) n -> p k n", p=P)

            def chunk_free(key):
                L, kind = key[0], key[1]
                if kind == "in" and key[2] < SPLIT_CHUNKS:
                    sp.wait_ge(in_lo_ready, L * IN_HALVES + 2 * key[2] + 2)
                elif kind == "in":
                    bank_written(sp, (L, "proj", key[2], NT - 1))
                elif kind in ("small", "w1"):
                    bank_written(sp, (L, "c2"))
                elif kind == "wo":
                    bank_written(sp, (L, "y", NT - 1, 1, 2))
                elif kind == "wout":
                    bank_written(sp, (L, "out", NT - 1, 1))
                else:
                    sp.wait_ge(lo_ready, 2 * DENSE_CHUNKS.index((kind, key[2])) + 2)

            sp.dma_start(x[:, :, :], a["x"][0].rearrange("(t p) d -> p t d", p=P)).then_inc(x_in, 16)
            for n, key in enumerate(chunk_seq):
                L, kind = key[0], key[1]
                if n == 1:
                    sp.dma_start(table[0:32, :], a["rel_bias_table"]).then_inc(small_in, 16)
                    sp.dma_start(onehot, a["bucket_onehot"]).then_inc(small_in, 16)
                    sp.dma_start(pos_rows, a["nsa_cmp_pos"].rearrange("l k (m j) d -> (l k m) (j d)", j=2)).then_inc(small_in, 16)
                    sp.dma_start(trig[:, :, :, :], a["rope_tables"]).then_inc(small_in, 16)
                    sp.dma_start(bgate_in, a["b_gate"].rearrange("l (c n) -> (l c) n", n=512)).then_inc(small_in, 16)
                    sp.dma_start(router[:, :, :], a["moe_router"][0].rearrange("(k p) e -> p k e", p=P)).then_inc(small_in, 16)
                    for layer in range(DEPTH):
                        sp.dma_start(mla_gain[:, layer, 0, :], a["mla_q_norm"][layer].partition_broadcast(P)).then_inc(small_in, 16)
                        sp.dma_start(mla_gain[:, layer, 1, :], a["mla_k_norm"][layer].partition_broadcast(P)).then_inc(small_in, 16)
                    sp.wait_ge(gains_in, GAINS_IN)
                    sp.wait_ge(small_in, SMALL_IN)
                s = slot_no[key]
                before = [k for k in chunk_seq[:n] if slot_no[k] == s]
                if before:
                    chunk_free(before[-1])
                if kind == "w1" and s == 3:
                    bank_written(sp, (L, "proj", SPLIT_CHUNKS - 1, NT - 1))
                full = slot_full[s]
                if kind == "in":
                    c0, w = CHUNKS[key[2]]
                    parts = [(slot_view(s, KD, w), rows(a["w_in"][L, :, c0:c0 + w]))]
                elif kind == "small":
                    v = slot_view(s, 1, 1536)[:, 0, :]
                    parts = [(v[:, 0:768].rearrange("p (k w) -> p k w", k=2), rows(a["mla_w_uq"][L])),
                             (v[:, 768:1280], a["mla_w_ukv"][L]),
                             (v[:, 1280:1408].rearrange("p (k w) -> p k w", k=2), rows(a["nsa_cmp_w2"][L, 0])),
                             (v[:, 1408:1536].rearrange("p (k w) -> p k w", k=2), rows(a["nsa_cmp_w2"][L, 1]))]
                elif kind == "w1":
                    parts = [(slot_view(s, 16, 256), rows(a["nsa_cmp_w1"][L, key[2]]))]
                elif kind == "wo":
                    v = slot_view(s, 4, D)
                    nsa = a["nsa_w_o"][L].rearrange("(g r d) n -> g d r n", g=2, r=4)
                    plain, pv, q0, qv = ((a["sb_w_o"][L], 0, 0, 2), (a["mla_w_o"][L], 2, 2, 0))[key[2]]
                    parts = [(v[:, pv:pv + 2, :], rows(plain))]
                    parts += [(v[64 * g:64 * g + 64, qv:qv + 2, :], nsa[g, :, q0:q0 + 2, :]) for g in range(2)]
                elif kind == "wout":
                    parts = [(slot_view(s, 4, D), rows(a["w_out"][L, 512 * key[2]:512 * key[2] + 512, :]))]
                elif kind in ("gate", "up"):
                    f, w = DENSE_GROUPS[key[2]]
                    parts = [(slot_view(s, KD, w), rows(a["dense_w_" + kind][0, :, f:f + w]))]
                else:
                    f, w = DENSE_GROUPS[key[2]]
                    parts = [(slot_view(s, w // P, D), rows(a["dense_w_down"][0, f:f + w, :]))]
                for dst, src in parts:
                    sp.dma_start(dst, src).then_inc(full, 16)

            def expert_loads(pair, first_expert, first=False):
                for o in range(PAIR):
                    for m, (kind, u) in enumerate(EXPERT_CHUNKS):
                        n = o * len(EXPERT_CHUNKS) + m
                        if not first or n >= MOE_RING:
                            sp.wait_ge(lo_ready, pair * (PAIR * EXPERT_HALVES) + (DENSE_HALVES + 2 * (n - MOE_RING + 1)))
                        elif n == 0:
                            bank_written(sp, (DEPTH - 1, "y", NT - 1, 1, 2))
                        elif n == 2:
                            sp.wait_ge(merged, 4 * DEPTH)
                        elif n == 4:
                            bank_written(sp, (DEPTH - 1, "out", NT - 1, 1))
                        e = first_expert + o
                        one = slice(e, e + 1) if first else bass.ds(e, 1)
                        if kind == "down":
                            src = a["moe_w_down"][0, one, 512 * u:512 * u + 512, :]
                        else:
                            src = a["moe_w_" + kind][0, one, :, 512 * u:512 * u + 512]
                        sp.dma_start(expert_slot(n, *chunk_shape(kind, 512)),
                                     src.rearrange("e (k p) n -> p (e k) n", p=P)).then_inc(slot_full[slot_order[n % MOE_RING]], 16)

            expert_loads(0, 0, first=True)
            with sp.Fori(1, PAIRS) as pair:
                expert_loads(pair, pair * PAIR)
            sp.wait_ge(routed, 1)
            crowded = sp.value_load(flag_i[0:1, 0:1], min_val=0, max_val=1)
            with sp.If(crowded > 0):
                with sp.Fori(PAIRS, 2 * PAIRS) as pair:
                    expert_loads(pair, pair * PAIR - N_EXPERTS)
            sp.wait_ge(x_final, 1)
            sp.dma_start(out[0].rearrange("(t p) d -> p t d", p=P), x[:, :, :]).then_inc(out_done, 16)
            sp.wait_ge(out_done, 16)

        @block.gpsimd
        def _(pool):
            g = [0]

            def link(ins):
                g[0] += 1
                ins.then_inc(g_done, 1)
                pool.wait_ge(g_done, g[0])

            link(nc.gpsimd.memset(gain_rows, 0.0))
            link(nc.gpsimd.memset(table[32:64, :], NEG))
            link(nc.gpsimd.memset(ident[:, :], 0.0))
            link(nc.gpsimd.affine_select(out=ident[:, :], in_=ident[:, :], compare_op=ALU.not_equal, fill=1.0,
                                         base=0, pattern=[[-1, P]], channel_multiplier=1))
            link(nc.gpsimd.memset(flip[:, :], 0.0))
            link(nc.gpsimd.affine_select(out=flip[:, :], in_=flip[:, :], compare_op=ALU.not_equal, fill=1.0,
                                         base=-(P - 1), pattern=[[1, P]], channel_multiplier=1))
            link(nc.gpsimd.memset(ones[:, :], 1.0))
            link(nc.gpsimd.affine_select(out=tri_ge[:, :], in_=ones[:, :], compare_op=ALU.is_ge, fill=0.0,
                                         base=0, pattern=[[-1, P]], channel_multiplier=1))
            link(nc.gpsimd.memset(stick_mask[:, :], 0.0))
            for c in (0, 256):
                link(nc.gpsimd.affine_select(out=stick_mask[:, c:c + P], in_=stick_mask[:, c:c + P],
                                             compare_op=ALU.is_ge, fill=NEG, base=-1, pattern=[[1, P]],
                                             channel_multiplier=-1))
            link(nc.gpsimd.memset(causal[:, :], 0.0))
            link(nc.gpsimd.affine_select(out=causal[:, :], in_=causal[:, :], compare_op=ALU.is_ge, fill=NEG,
                                         base=P, pattern=[[-1, SEQ]], channel_multiplier=1))
            link(nc.gpsimd.memset(valid[:, :], 1.0))
            link(nc.gpsimd.affine_select(out=valid[:, 0:1], in_=valid[:, 0:1], compare_op=ALU.is_ge, fill=0.0,
                                         base=-31, pattern=[[0, 1]], channel_multiplier=1))
            link(nc.gpsimd.memset(inv_n[:, 0:18], 1.0 / HD))
            link(nc.gpsimd.memset(inv_n[:, 18:19], 1.0 / 256))
            link(nc.gpsimd.memset(inv_n[:, 19:20], 1.0 / 128))
            link(nc.gpsimd.memset(mhalf[:, :], -0.5))
            link(nc.gpsimd.memset(kcT[:, :, :], 0.0))
            nc.gpsimd.memset(cmp_x[:, :, 2, :], 0.0).then_inc(consts_ready, 1)

            def inverse_norm(s, n, done):
                link(nc.gpsimd.tensor_scalar(s, s, 1.0 / n, EPS, ALU.mult, ALU.add))
                w = s.shape[-1]
                nc.gpsimd.tensor_tensor(s, s, mhalf[0:s.shape[0], 0:w], ALU.pow).then_inc(done, 1)

            def residual_norm(N):
                for t in range(NT):
                    pool.wait_ge(sq_ready, NT * N + t + 1)
                    inverse_norm(ssum[:, t:t + 1], D, rstd_ready)

            for L in range(DEPTH):
                residual_norm(2 * L)
                for t in range(NT):
                    pool.wait_ge(head_sums, NT * L + t + 1)
                    link(nc.gpsimd.tensor_tensor(sums[:, t, :], sums[:, t, :], inv_n[:, :], ALU.mult))
                    link(nc.gpsimd.tensor_scalar(sums[:, t, :], sums[:, t, :], 1.0, EPS, ALU.mult, ALU.add))
                    nc.gpsimd.tensor_tensor(sums[:, t, :], sums[:, t, :], mhalf[:, :], ALU.pow).then_inc(head_rstd, 1)
                for t in range(NT):
                    pool.wait_ge(mla_sums, NT * L + t + 1)
                    inverse_norm(msum[:, t, :], MQ, mla_rstd)
                pool.wait_ge(ck_sums, L + 1)
                inverse_norm(ksum[0:N_CMP, :], HD, ck_rstd)
                residual_norm(2 * L + 1)

            bank_read(pool, (DEPTH - 1, "out", NT - 1, 1))
            link(nc.gpsimd.affine_select(out=tri_lt, in_=ones[:, :], compare_op=ALU.is_ge, fill=0.0,
                                         base=-1, pattern=[[1, P]], channel_multiplier=-1))
            link(nc.gpsimd.iota(iota, [[1, P]], base=0, channel_multiplier=0, allow_small_or_imprecise_dtypes=True))
            nc.gpsimd.iota(iota8, [[1, 8]], base=0, channel_multiplier=0,
                           allow_small_or_imprecise_dtypes=True).then_inc(consts_ready, 1)

        @block.scalar
        def _(act_e):
            c = [0]

            def link(ins):
                c[0] += 1
                ins.then_inc(a_done, 1)
                act_e.wait_ge(a_done, c[0])

            act = nc.scalar.activation

            def read_out(key, dst, src):
                bank_written(act_e, key)
                nc.scalar.copy(dst, src).then_inc(bank_free[bank(key)], 1)

            act_e.wait_ge(g_done, 1)
            act_e.dma_start(gain_rows[G_MIX:G_MIX + 16, :], a["mix_norm"].rearrange("l (r c) -> (l r) c", c=P)).then_inc(gains_in, 16)
            act_e.dma_start(gain_rows[G_FFN:G_FFN + 16, :], a["ffn_norm"].rearrange("l (r c) -> (l r) c", c=P)).then_inc(gains_in, 16)
            halves = gain_rows.rearrange("p (a d) -> p a d", a=2)
            act_e.dma_start(halves[G_Q:G_Q + DEPTH], a["nsa_q_norm"].unsqueeze(1).to_broadcast([DEPTH, 2, HD])).then_inc(gains_in, 16)
            act_e.dma_start(halves[G_K:G_K + 3 * DEPTH],
                            a["nsa_k_norm"].rearrange("l k d -> (l k) d").unsqueeze(1).to_broadcast([3 * DEPTH, 2, HD])).then_inc(gains_in, 16)
            for L in range(DEPTH):
                r = G_LATENT + 3 * L
                act_e.dma_start(gain_rows[r:r + 2, :], a["mla_q_a_norm"][L].rearrange("(r c) -> r c", c=P)).then_inc(gains_in, 16)
                act_e.dma_start(gain_rows[r + 2:r + 3, :], a["mla_kv_a_norm"][L:L + 1, :]).then_inc(gains_in, 16)

            def residual_squares(N, tiles=range(NT)):
                for t in tiles:
                    if N == 0:
                        act_e.wait_ge(x_in, 16)
                    elif N % 2:
                        bank_read(act_e, (N // 2, "out", t, 0))
                        bank_read(act_e, (N // 2, "out", t, 1))
                    else:
                        act_e.wait_ge(x_dense, t + 1)
                    act(xn[:, t, :], x[:, t, :], ACT.Square, accum_out=ssum[:, t:t + 1]).then_inc(sq_ready, 1)

            residual_squares(0)
            def bias_to_sbuf():
                act_e.wait_ge(setup_dve, 1)
                act_e.dma_start(bias_dram, rvec).then_inc(bias_out, 16)
                act_e.wait_ge(bias_out, 16)
                toeplitz = bass.AP(bias_dram.tensor, 0, [[1, P], [512, 8], [1, 384]])
                act_e.dma_start(bias, toeplitz).then_inc(bias_in, 16)

            def projection_out(L, c, t):
                c0, w = CHUNKS[c]
                key = (L, "proj", c, t)
                read_out(key, proj[:, t, c0:c0 + w], ps[:, bank(key), 0:w])

            def mixers(L):
                if L > 0:
                    residual_squares(2 * L)

                def projection_rounded(j):
                    weights_landed(act_e, (L, "in", j // 2))
                    if j >= 2:
                        projection_half_used(act_e, L, j - 2)
                    src, w = projection_half(L, j)
                    nc.scalar.copy(in_hi[j % 2][:, 0:w], src).then_inc(in_hi_ready, 1)

                def head_squares(t):
                    for c_ in range(1, N_MIX_CHUNKS):
                        bank_read(act_e, (L, "proj", c_, t))
                    if t == 1:
                        act_e.wait_ge(head_sums, NT * L + 1)
                    act(tmp[:, 0:1152], proj[:, t, NQ:NQ + 1152], ACT.Square).then_inc(head_sq, 1)
                    act(tmp[:, 1152:1536], proj[:, t, CQ:CQ + 384], ACT.Square).then_inc(head_sq, 1)

                def mixer_inputs_0(t):
                    key = (L, "xt", t, 0)
                    read_out(key, xT[:, 0:4, P * t:P * t + P], ps[:, bank(key), :].rearrange("p (j q) -> p j q", j=4))

                for j in range(2):
                    projection_rounded(j)
                for t in range(NT):
                    for h in range(2):
                        bank_read(act_e, (L, "norm1", t, h))
                        v = (slice(None), slice(4 * h, 4 * h + 4), slice(P * t, P * t + P))
                        nc.scalar.copy(n_hi[v], hT[v]).then_inc(n_hi_ready, 1)
                for j in range(2, IN_HALVES):
                    if j % 2:
                        projection_out(L, j // 2 - 1, 0)
                    if j == IN_HALVES - 1:
                        mixer_inputs_0(0)
                    projection_rounded(j)
                    if IN_HALVES - 3 <= j < IN_HALVES - 1:
                        head_squares(j - (IN_HALVES - 3))
                    if L == 0 and j == 4:
                        bias_to_sbuf()
                for t in range(NT):
                    act(ngate[:, t, :], proj[:, t, NG:NG + 24], ACT.Exp, scale=-1.0).then_inc(ng_exp, 1)
                projection_out(L, 6, 0)
                mixer_inputs_0(1)
                for t in range(NT):
                    key = (L, "uq", t)
                    read_out(key, mqk[:, t, 0:4, :], ps[:, bank(key), 0:384].rearrange("p (h d) -> p h d", h=4))
                    key = (L, "ukv", t)
                    both = ps[:, bank(key), :].rearrange("p (h d) -> p h d", h=4)
                    bank_written(act_e, key)
                    nc.scalar.copy(mqk[:, t, 4:8, 0:HD], both[:, :, 0:HD]).then_inc(mla_in, 1)
                    nc.scalar.copy(mv[:, t, :, :], both[:, :, HD:P]).then_inc(bank_free[bank(key)], 1)
                for t in range(NT):
                    act_e.wait_ge(mla_in, NT * L + t + 1)
                    bank_read(act_e, (L, "uq", t))
                    act_e.wait_ge(mla_rope_in, L + 1)
                    act_e.wait_ge(*((head_sums, NT * L + NT) if t == 0 else (mla_sums, NT * L + 1)))
                    act(tmp[:, 0:768], mqk[:, t, :, :].rearrange("p h d -> p (h d)"), ACT.Square).then_inc(mla_sq, 1)
                key = (L, "c1")
                read_out(key, c1_rows, ps[0:CMP_ROWS, bank(key), :])
                key = (L, "c1t")
                read_out(key, ch_raw[:, :, 0:CMP_ROWS], ps[:, bank(key), 0:192].rearrange("p (f n) -> p f n", f=4)[:, :, 0:CMP_ROWS])
                act_e.wait_ge(ch_ready, L + 1)
                act(ce[:, :, :], ch[:, :, :], ACT.Exp, scale=-1.0).then_inc(ch_exp, 1)
                projection_out(L, 7, 0)
                act_e.wait_ge(stick_z, L + 1)
                act_e.wait_ge(mla_sums, NT * L + NT)
                link(act(stick_tmp[:, :, :], stick, ACT.Abs))
                link(act(tmp, tmp, ACT.Exp, scale=-1.0))
                act(tmp, tmp, ACT.Ln, bias=1.0).then_inc(stick_ln, 1)
                for t in range(NT):
                    for b in range(2):
                        key = (L, "mt", t, b)
                        read_out(key, mT[0:MQ, 4 * b:4 * b + 4, P * t:P * t + P],
                                 ps[0:MQ, bank(key), :].rearrange("p (j q) -> p j q", j=4))
                act_e.wait_ge(stick_t, L + 1)
                act(stick, stick, ACT.Exp).then_inc(stick_w, 1)
                for i in range(NT):
                    act_e.wait_ge(cmp_s, NT * L + i + 1)
                    act(pcs[:, i, :, 0:N_CMP], pcs[:, i, :, 0:N_CMP], ACT.Exp).then_inc(cmp_e, 1)
                for hp in range(2):
                    key = (L, "sbo", hp)
                    act_e.wait_ge(stick_out, 2 * L + hp + 1)
                    nc.scalar.copy(yT[:, hp, :], ps[:, bank(key), 0:SEQ]).then_inc(bank_free[bank(key)], 1)
                for s in range(STEPS):
                    if s < len(JOBS):
                        job_exp(L, s)
                    if 0 <= s - LAG_TURN < len(JOBS):
                        job_turned(L, s - LAG_TURN)
                    if 0 <= s - LAG_PV < len(JOBS):
                        job_out(L, s - LAG_PV)
                    if s in LATE_GATES and LATE_GATES[s][1] == 0:
                        projection_out(L, *LATE_GATES[s])
                for t in range(NT):
                    for c_ in range(N_MIX_CHUNKS, len(CHUNKS)):
                        bank_read(act_e, (L, "proj", c_, t))
                    act(proj[:, t, GATES:], proj[:, t, GATES:], ACT.Sigmoid).then_inc(gates_ready, 1)
                for t in range(NT):
                    for h in range(2):
                        key = (L, "merge", t, h)
                        read_out(key, hT[:, 4 * h:4 * h + 4, P * t:P * t + P],
                                 ps[:, bank(key), :].rearrange("p (j q) -> p j q", j=4))
                act_e.wait_ge(merged, 4 * L + 4)
                for q in range(SPLIT_BUFS):
                    if L == 0:
                        weights_landed(act_e, (0, *DENSE_CHUNKS[q // 2]))
                    else:
                        expert_landed(act_e, 0, q // 2)
                    src, w = ffn_half(L, q)
                    nc.scalar.copy(w_hi[q][:, 0:w], src).then_inc(hi_ready, 1)
                for t in range(NT):
                    residual_squares(2 * L + 1, (t,))
                    if L == 0:
                        for h in range(2):
                            split_normed(t, h)

            def job_exp(L, j):
                kind, i, r = JOBS[j]
                nk = P * (i + 1)
                n = len(JOBS) * L + j
                b = n % 3
                act_e.wait_ge(max_ready, n + 1)
                v = probs[:, b, 0:2 * nk].rearrange("p (a k) -> p a k", a=2)
                for h in range(2):
                    act(v[:, h, :], v[:, h, :], ACT.Exp, bias=nmax[:, b, h:h + 1],
                        accum_out=prob_sum[:, b, h:h + 1]).then_inc(exp_ready, 1)

            def job_turned(L, j):
                kind, i, r = JOBS[j]
                n = len(JOBS) * L + j
                if n >= 2:
                    act_e.wait_ge(pv_done, n - 1)
                key = (L, "p", j)
                w = 2 * (i + 1) * P
                read_out(key, probsT[:, n % 2, 0:w], ps[:, bank(key), 0:w])

            def job_out(L, j):
                kind, i, r = JOBS[j]
                if kind == "sel":
                    return
                act_e.wait_ge(pv_done, len(JOBS) * L + j + 1)
                key = (L, "mlao", i, r) if kind == "mla" else (L, "nsao", i, r)
                to = 6 + r if kind == "mla" else 2 + r
                nc.scalar.copy(yT[:, to, P * i:P * i + P], ps[:, bank(key), 0:P]).then_inc(bank_free[bank(key)], 1)

            def split_normed(t, h):
                bank_read(act_e, (0, "norm2", t, h))
                v = (slice(None), slice(4 * h, 4 * h + 4), slice(P * t, P * t + P))
                nc.scalar.copy(h_hi[v], hT[v]).then_inc(h_hi_ready, 1)

            def ffn_rounded_parts(chunks, q0, n0, tiles, widths, landed, slot, gate_bank, turn_bank, extra=None):
                T = len(tiles)

                def turned(u):
                    for t in tiles:
                        n = n0 + (u * T + t)
                        act_e.wait_ge(act_turned, n + 1)
                        w = widths[u]
                        nc.scalar.copy(a_hi[:, t if T > 1 else u % 2, 0:w], ps[:, turn_bank(t), 0:w]).then_inc(a_hi_ready, 1)

                for m, (kind, u) in enumerate(chunks):
                    rows, cols = chunk_shape(kind, widths[u])
                    src = slot(m, rows, cols).rearrange("p k w -> p (k w)")
                    w = rows * cols // 2
                    landed(act_e, m)
                    for half in range(2):
                        q = 2 * m + half
                        if q < SPLIT_BUFS:
                            continue
                        act_e.wait_ge(half_done, q0 + (q + 1 - SPLIT_BUFS))
                        used = q - SPLIT_BUFS
                        before_kind, before_u = chunks[used // 2] if used >= 0 else (None, None)
                        if before_kind == "gate" and used % 2 == 1:
                            for t in tiles:
                                g = widths[before_u]
                                act(act_g[:, t, 0:g], ps[:, gate_bank(t), 0:g], ACT.Silu).then_inc(silu_done, 1)
                        if before_kind == "gate" and used % 2 == 0 and before_u > 0:
                            turned(before_u - 1)
                        nc.scalar.copy(w_hi[q % SPLIT_BUFS][:, 0:w], src[:, w * half:w * half + w]).then_inc(hi_ready, 1)
                        if extra and q == 6:
                            extra()
                turned(len(widths) - 1)

            def dense_slot(m, rows, cols):
                return slot_view(slot_of((0, *DENSE_CHUNKS[m])), rows, cols)

            mixers(0)
            ffn_rounded_parts(DENSE_CHUNKS, 0, 0, range(NT), [w for _, w in DENSE_GROUPS],
                              lambda eng, m: weights_landed(eng, (0, *DENSE_CHUNKS[m])), dense_slot,
                              lambda t: t, lambda t: 2 + t)
            mixers(1)

            act_e.wait_ge(route_dve, 1)
            act(route[:, 2, :, 1:2], route[:, 2, :, 0:1], ACT.Exp).then_inc(route_exp, 1)

            def put_out(it):
                act_e.wait_ge(put_turned, it + 1)
                nc.scalar.copy(putT, ps[:, 1, 0:SEQ]).then_inc(putT_ready, 1)

            def gathered_rounded(it):
                for h in range(2):
                    act_e.wait_ge(gains_applied, it * 2 + (h + 1))
                    nc.scalar.copy(e_hi[:, 4 * h:4 * h + 4, :], gathered_f[h].rearrange("p (j s) -> p j s", j=4)).then_inc(e_hi_ready, 1)

            gathered_rounded(0)
            act_e.sem_inc(ye_ready, 1)

            def next_rounded(pair, o, q):
                n = (o + 1) * len(EXPERT_CHUNKS) + q // 2
                expert_landed(act_e, pair, n)
                act_e.wait_ge(half_done, (pair * PAIR + o + 1) * EXPERT_HALVES + (DENSE_HALVES + q + 1 - SPLIT_BUFS))
                src, w = expert_half(n, q)
                nc.scalar.copy(w_hi[q][:, 0:w], src).then_inc(hi_ready, 1)

            def expert(pair, o, last=False):
                it = pair * PAIR + o
                c0 = o * len(EXPERT_CHUNKS)
                ffn_rounded_parts(EXPERT_CHUNKS, it * EXPERT_HALVES + DENSE_HALVES,
                                  it * EXPERT_UNITS + NT * len(DENSE_GROUPS), (0,), [512] * EXPERT_UNITS,
                                  lambda eng, m: expert_landed(eng, pair, c0 + m),
                                  lambda m, rows, cols: expert_slot(c0 + m, rows, cols), lambda t: 2, lambda t: 0,
                                  extra=lambda: put_out(it))
                gathered_rounded(it + 1)
                if not last:
                    next_rounded(pair, o, 0)
                    next_rounded(pair, o, 1)
                act_e.wait_ge(half_done, (it + 1) * EXPERT_HALVES + DENSE_HALVES)
                act_e.wait_ge(spread, it * 4 + 1)
                nc.scalar.copy(ye[:, 0:512], ps[:, 4, :]).then_inc(ye_ready, 1)
                if not last:
                    next_rounded(pair, o, 2)

            def experts(first_pair):
                with act_e.Fori(first_pair, first_pair + PAIRS - 1) as pair:
                    for o in range(PAIR):
                        expert(pair, o)
                for o in range(PAIR):
                    expert(first_pair + PAIRS - 1, o, last=(o == PAIR - 1))

            experts(0)
            act_e.wait_ge(routed, 1)
            crowded = act_e.value_load(flag_i[0:1, 0:1], min_val=0, max_val=1)
            with act_e.If(crowded > 0):
                for q in range(SPLIT_BUFS):
                    next_rounded(PAIRS - 1, PAIR - 1, q)
                experts(PAIRS)

        @block.vector
        def _(dve):
            c = [0]
            V = nc.vector

            def link(ins):
                c[0] += 1
                ins.then_inc(v_done, 1)
                dve.wait_ge(v_done, c[0])

            def bc(ap, n):
                return ap.unsqueeze(len(ap.shape)).to_broadcast(list(ap.shape) + [n])

            def turned_with_gains(key, dst, col):
                bank_written(dve, key)
                k = dst.shape[1]
                V.tensor_tensor(dst, ps[:, bank(key), 0:k * P].rearrange("p (j q) -> p j q", j=k),
                                bc(gains[:, col:col + k], P), ALU.mult).then_inc(bank_free[bank(key)], 1)

            def residual_scaled(N, t):
                dve.wait_ge(rstd_ready, NT * N + t + 1)
                V.tensor_scalar(xn[:, t, :], x[:, t, :], ssum[:, t:t + 1], None, ALU.mult).then_inc(xn_ready, 1)

            def normed_turned(L, which, t):
                col = (G_MIX if which == "norm1" else G_FFN) + KD * L
                for h in range(2):
                    turned_with_gains((L, which, t, h), hT[:, 4 * h:4 * h + 4, P * t:P * t + P], col + 4 * h)

            def normed_remainder(t):
                for h in range(2):
                    v = (slice(None), slice(4 * h, 4 * h + 4), slice(P * t, P * t + P))
                    dve.wait_ge(h_hi_ready, 2 * t + h + 1)
                    V.tensor_tensor(h_lo[v], hT[v], h_hi[v].bitcast(F32), ALU.subtract).then_inc(h_lo_ready, 1)

            def projection_out(L, c_, t):
                c0, w = CHUNKS[c_]
                key = (L, "proj", c_, t)
                bank_written(dve, key)
                V.tensor_copy(proj[:, t, c0:c0 + w], ps[:, bank(key), 0:w]).then_inc(bank_free[bank(key)], 1)

            def setup_gains():
                dve.wait_ge(setup_pe, 1)
                link(V.tensor_copy(gains[:, :], ps[:, 6, 0:64]))

            def setup_small():
                dve.wait_ge(setup_pe, 2)
                V.tensor_copy(posT[:, :, :].rearrange("p a b -> p (a b)"), ps[:, 6, P:P + 64])
                dve.wait_ge(setup_pe, 3)
                V.tensor_copy(rvec, ps[0:8, 7, :]).then_inc(setup_dve, 1)
                link(V.tensor_scalar(bgate[:, :], ones[0:BGATE_LO + 12, 0:1].to_broadcast([BGATE_LO + 12, 512]), 0.0, None, ALU.mult))
                link(V.tensor_copy(bgate[0:12, :], bgate_in))
                V.tensor_tensor(bgate[BGATE_LO:BGATE_LO + 12, :], bgate_in, bgate[0:12, :].bitcast(F32), ALU.subtract)
                V.tensor_tensor(gate_row[:, :], ident[0:BGATE_LO + 12, 0:12], ident[0:BGATE_LO + 12, BGATE_LO:BGATE_LO + 12],
                                ALU.add).then_inc(bgate_ready, 1)

            def head_sums_of(L, t):
                dve.wait_ge(head_sq, 2 * (NT * L + t) + 2)
                V.tensor_reduce(sums[:, t, 0:18], tmp[:, 0:1152].rearrange("p (h d) -> p h d", d=HD), AX.X, ALU.add)
                V.tensor_reduce(sums[:, t, 18:19], tmp[:, 1152:1408], AX.X, ALU.add)
                V.tensor_reduce(sums[:, t, 19:20], tmp[:, 1408:1536], AX.X, ALU.add).then_inc(head_sums, 1)

            def scale_heads(L, t):
                dve.wait_ge(head_rstd, NT * L + t + 1)
                q = proj[:, t, NQ:NQ + 512].rearrange("p (g r d) -> p g r d", g=2, r=4)
                pairs = xn[:, t, 0:512].rearrange("p (r g d) -> p g r d", r=4, g=2)
                for g in range(2):
                    V.tensor_tensor(pairs[:, g], q[:, g], bc(sums[:, t, 4 * g:4 * g + 4], HD), ALU.mult)
                for c0, n, s0 in ((KS, 2, 12), (KW, 2, 16)):
                    v = proj[:, t, c0:c0 + n * HD].rearrange("p (h d) -> p h d", d=HD)
                    V.tensor_tensor(v, v, bc(sums[:, t, s0:s0 + n], HD), ALU.mult)
                V.tensor_scalar(proj[:, t, CQ:CQ + 256], proj[:, t, CQ:CQ + 256], sums[:, t, 18:19], None, ALU.mult)
                V.tensor_scalar(proj[:, t, CKV:CKV + P], proj[:, t, CKV:CKV + P], sums[:, t, 19:20], None,
                                ALU.mult).then_inc(heads_normed, 1)

            def turned_mixer_inputs(L, t):
                q = slice(P * t, P * t + P)
                key = (L, "xt", t, 1)
                bank_written(dve, key)
                V.tensor_scalar(xT[:, 4:8, q], ps[:, bank(key), :].rearrange("p (j q) -> p j q", j=4),
                                gains[:, G_Q + L:G_Q + L + 1], None, ALU.mult).then_inc(bank_free[bank(key)], 1)
                key = (L, "xt", t, 2)
                bank_written(dve, key)
                b = ps[:, bank(key), :]
                for kv in range(2):
                    for g in range(2):
                        for par in range(2):
                            src = b[64 * g:64 * g + 64, (2 + kv) * P:(3 + kv) * P].rearrange("p (m j) -> p m j", j=2)
                            V.tensor_copy(cmp_x[64 * par:64 * par + 64, kv, g, 64 * t:64 * t + 64], src[:, :, par])
                if t == 0:
                    V.tensor_copy(cmp_x[:, :, 2, 0:16], posT[:, 2 * L:2 * L + 2, :])
                V.tensor_tensor(xT[:, 8:10, q], b[:, 0:2 * P].rearrange("p (j q) -> p j q", j=2),
                                bc(gains[:, G_K + 3 * L + 1:G_K + 3 * L + 3], P), ALU.mult).then_inc(bank_free[bank(key)], 1)
                turned_with_gains((L, "xt", t, 3), xT[:, 10:13, q], G_LATENT + 3 * L)

            def latent_heads(L, t):
                m = mqk[:, t, :, :]
                dve.wait_ge(mla_sq, NT * L + t + 1)
                V.tensor_reduce(msum[:, t, :], tmp[:, 0:768].rearrange("p (h d) -> p h d", d=MQ), AX.X,
                                ALU.add).then_inc(mla_sums, 1)
                dve.wait_ge(mla_rstd, NT * L + t + 1)
                link(V.tensor_tensor(m, m, bc(msum[:, t, :], MQ), ALU.mult))
                for w in range(2):
                    v = m[:, 4 * w:4 * w + 4, :]
                    gain = mla_gain[:, L, w, :].unsqueeze(1).to_broadcast([P, 4, MQ])
                    ins = V.tensor_tensor(v, v, gain, ALU.mult)
                link(ins)
                x1, x2 = m[:, :, 64:80], m[:, :, 80:96]
                cos, sin = (trig[:, f, t, :].unsqueeze(1).to_broadcast([P, 8, 16]) for f in range(2))
                r = rope_tmp.rearrange("p f (h d) -> p f h d", h=8)
                V.tensor_tensor(r[:, 0], x1, cos, ALU.mult)
                V.tensor_tensor(r[:, 1], x2, sin, ALU.mult)
                V.tensor_tensor(r[:, 2], x2, cos, ALU.mult)
                link(V.tensor_tensor(r[:, 3], x1, sin, ALU.mult))
                V.tensor_tensor(x1, r[:, 0], r[:, 1], ALU.subtract)
                V.tensor_tensor(x2, r[:, 2], r[:, 3], ALU.add).then_inc(mla_ready, 1)

            def mixers(L):
                for t in range(NT):
                    residual_scaled(2 * L, t)
                if L == 0:
                    setup_gains()
                for t in range(NT):
                    normed_turned(L, "norm1", t)
                for t in range(NT):
                    for h in range(2):
                        v = (slice(None), slice(4 * h, 4 * h + 4), slice(P * t, P * t + P))
                        dve.wait_ge(n_hi_ready, 4 * L + 2 * t + h + 1)
                        V.tensor_tensor(n_lo[v], hT[v], n_hi[v].bitcast(F32), ALU.subtract).then_inc(n_lo_ready, 1)
                for j in range(IN_HALVES):
                    if j % 2 and j > 1:
                        projection_out(L, j // 2 - 1, 1)
                    if j == IN_HALVES - 1:
                        turned_mixer_inputs(L, 0)
                    src, w = projection_half(L, j)
                    dve.wait_ge(in_hi_ready, L * IN_HALVES + j + 1)
                    V.tensor_tensor(in_lo[j % 2][:, 0:w], src, in_hi[j % 2][:, 0:w].bitcast(F32),
                                    ALU.subtract).then_inc(in_lo_ready, 1)
                    if j == IN_HALVES - 3:
                        head_sums_of(L, 0)
                    if j == IN_HALVES - 2:
                        scale_heads(L, 0)
                        head_sums_of(L, 1)
                    if j == IN_HALVES - 1:
                        scale_heads(L, 1)
                    if L == 0 and j == 2:
                        setup_small()
                dve.wait_ge(ng_exp, NT * L + NT)
                flat = ngate[:, :, :].rearrange("p t n -> p (t n)")
                link(V.tensor_scalar(flat, flat, 1.0, None, ALU.add))
                link(V.reciprocal(flat, flat))
                projection_out(L, 6, 1)
                turned_mixer_inputs(L, 1)
                for t in range(NT):
                    bank_read(dve, (L, "proj", 4, t))
                    ins = V.tensor_copy(mqk[:, t, 4:8, HD:MQ], proj[:, t, KR:KR + 32].unsqueeze(1).to_broadcast([P, 4, 32]))
                ins.then_inc(mla_rope_in, 1)
                for t in range(NT):
                    latent_heads(L, t)
                for t in range(NT):
                    bank_read(dve, (L, "uq", t))
                    bank_read(dve, (L, "ukv", t))
                link(V.tensor_copy(xT[64:P, 10:12, :], xT[64:P, 8:10, :]))
                V.memset(xT[64:P, 8:10, :], 0.0)
                V.memset(xT[0:64, 10:12, :], 0.0).then_inc(keys_split, 1)
                def stick_scores(h):
                    key = (L, "z", h)
                    bank_written(dve, key)
                    V.scalar_tensor_tensor(out=stick[:, h, :], in0=ps[:, bank(key), 0:384], scalar=HD ** -0.5,
                                           in1=stick_mask[:, :], op0=ALU.mult, op1=ALU.add).then_inc(bank_free[bank(key)], 1)
                stick_scores(0)
                stick_scores(1)
                bank_read(dve, (L, "c1t"))
                V.tensor_tensor(ch.rearrange("p f (g n) -> p f g n", g=2),
                                ch_raw[:, :, 0:32].rearrange("p f (g n) -> p f g n", g=2)[:, :, :, 0:N_CMP],
                                ch_raw[:, :, 32:33].unsqueeze(3).to_broadcast([P, 4, 2, N_CMP]),
                                ALU.add).then_inc(ch_ready, 1)
                dve.wait_ge(ch_exp, L + 1)
                link(V.tensor_scalar(ce[:, :, :], ce[:, :, :], 1.0, None, ALU.add))
                link(V.reciprocal(ce[:, :, :], ce[:, :, :]))
                V.tensor_tensor(ch[:, :, :], ch[:, :, :], ce[:, :, :], ALU.mult).then_inc(ch_act, 1)
                stick_scores(2)
                stick_scores(3)
                bank_read(dve, (L, "z", 2))
                bank_read(dve, (L, "z", 3))
                link(V.tensor_copy(cmax[0:1, 0:1], ones[0:1, 0:1]))
                dve.sem_inc(stick_z, 1)
                projection_out(L, 7, 1)
                key = (L, "c2")
                bank_written(dve, key)
                V.tensor_copy(ckv_c[0:N_CMP, :, :], ps[0:N_CMP, bank(key), 0:4 * HD].rearrange("p (f d) -> p f d", f=4)).then_inc(bank_free[bank(key)], 1)
                bank_read(dve, key)
                link(V.tensor_tensor(csq[0:N_CMP, :, :], ckv_c[0:N_CMP, 0:2, :], ckv_c[0:N_CMP, 0:2, :], ALU.mult))
                V.tensor_reduce(ksum[0:N_CMP, :], csq[0:N_CMP, :, :], AX.X, ALU.add).then_inc(ck_sums, 1)
                dve.wait_ge(ck_rstd, L + 1)
                V.tensor_tensor(ckv_c[0:N_CMP, 0:2, :], ckv_c[0:N_CMP, 0:2, :], bc(ksum[0:N_CMP, :], HD),
                                ALU.mult).then_inc(ck_ready, 1)
                key = (L, "kct")
                bank_written(dve, key)
                for g in range(2):
                    r = slice(64 * g, 64 * g + 64)
                    ins = V.tensor_scalar(kcT[r, g, 0:N_CMP], ps[r, bank(key), 0:N_CMP],
                                          gains[r, G_K + 3 * L:G_K + 3 * L + 1], None, ALU.mult)
                ins.then_inc(bank_free[bank(key)], 1)
                dve.wait_ge(stick_ln, L + 1)
                V.scalar_tensor_tensor(out=stick_tmp[:, :, :], in0=stick, scalar=0.0, in1=stick_tmp[:, :, :],
                                       op0=ALU.max, op1=ALU.add).then_inc(stick_sp, 1)
                for h in range(4):
                    key = (L, "S", h)
                    bank_written(dve, key)
                    V.tensor_tensor(stick[:, h, :], stick[:, h, :], ps[:, bank(key), 0:384],
                                    ALU.subtract).then_inc(bank_free[bank(key)], 1)
                bank_read(dve, (L, "S", 2))
                bank_read(dve, (L, "S", 3))
                dve.sem_inc(stick_t, 1)
                if L == 0:
                    for h in range(8):
                        key = (0, "flip", h)
                        bank_written(dve, key)
                        V.tensor_copy(bias[:, h, :], ps[:, bank(key), 0:384]).then_inc(bank_free[bank(key)], 1)
                    for h in (6, 7):
                        bank_read(dve, (0, "flip", h))
                for i in range(NT):
                    key = (L, "sc", i)
                    bank_written(dve, key)
                    s = pcs[:, i, :, 0:N_CMP]
                    k0 = 31 + P * (1 - i)
                    V.scalar_tensor_tensor(out=s, in0=ps[:, bank(key), 0:P].rearrange("p (h n) -> p h n", h=8)[:, :, 0:N_CMP],
                                           scalar=HD ** -0.5, in1=bias[:, :, k0:k0 + 16 * (N_CMP - 1) + 1:16],
                                           op0=ALU.mult, op1=ALU.add).then_inc(bank_free[bank(key)], 1)
                    bank_read(dve, key)
                    link(V.tensor_reduce(cmax[:, :], s, AX.X, ALU.max))
                    V.tensor_tensor(s, s, bc(cmax[:, :], N_CMP), ALU.subtract).then_inc(cmp_s, 1)
                    dve.wait_ge(cmp_e, NT * L + i + 1)
                    link(V.tensor_reduce(csum[:, :], s, AX.X, ALU.add))
                    link(V.reciprocal(csum[:, :], csum[:, :]))
                    link(V.scalar_tensor_tensor(out=csum[:, :], in0=csum[:, :], scalar=valid[:, i:i + 1],
                                                in1=ngate[:, i, 0:24:3], op0=ALU.mult, op1=ALU.mult))
                    V.tensor_tensor(s, s, bc(csum[:, :], N_CMP), ALU.mult).then_inc(cmp_p, 1)
                for s in range(STEPS):
                    if s < len(JOBS):
                        job_scores(L, s)
                    if 0 <= s - 1 < len(JOBS):
                        job_scale(L, s - 1)
                    for i in range(NT):
                        if s - LAG_TURN == FIRST_SPARSE[i]:
                            compressed_turned(L, i)
                    if s in LATE_GATES and LATE_GATES[s][1] == 1:
                        projection_out(L, *LATE_GATES[s])
                for t in range(NT):
                    dve.wait_ge(gates_ready, NT * L + t + 1)
                    for h in range(2):
                        to = xn[:, t, 512 * h:512 * h + 512]
                        for m in range(3):
                            key = (L, "y", t, h, m)
                            gate = proj[:, t, GATES + D * m + 512 * h:GATES + D * m + 512 * h + 512]
                            dst = to if m == 0 else tmp[:, 512 * (m - 1):512 * m]
                            bank_written(dve, key)
                            V.tensor_tensor(dst, ps[:, bank(key), :], gate, ALU.mult).then_inc(bank_free[bank(key)], 1)
                            bank_read(dve, key)
                            if m == 1:
                                link(V.tensor_tensor(to, to, dst, ALU.add))
                            if m == 2:
                                V.tensor_tensor(to, to, dst, ALU.add).then_inc(merged, 1)
                                dve.wait_ge(merged, 4 * L + 2 * t + h + 1)
                def ffn_remainder(q):
                    src, w = ffn_half(L, q)
                    dve.wait_ge(hi_ready, L * DENSE_HALVES + q + 1)
                    V.tensor_tensor(w_lo[q][:, 0:w], src, w_hi[q][:, 0:w].bitcast(F32), ALU.subtract).then_inc(lo_ready, 1)

                for t in range(NT):
                    for h in range(2):
                        key = (L, "out", t, h)
                        bank_written(dve, key)
                        V.tensor_tensor(x[:, t, 512 * h:512 * h + 512], x[:, t, 512 * h:512 * h + 512],
                                        ps[:, bank(key), :], ALU.add).then_inc(bank_free[bank(key)], 1)
                        if (t, h) == (0, 1):
                            residual_scaled(2 * L + 1, 0)
                        if (t, h) == (1, 0):
                            normed_turned(L, "norm2", 0)
                            if L == 0:
                                normed_remainder(0)
                        if 2 * t + h < SPLIT_BUFS:
                            ffn_remainder(2 * t + h)
                residual_scaled(2 * L + 1, 1)
                normed_turned(L, "norm2", 1)
                if L == 0:
                    normed_remainder(1)

            def job_scores(L, j):
                kind, i, r = JOBS[j]
                nk = P * (i + 1)
                n = len(JOBS) * L + j
                b = n % 3
                if j >= 3:
                    bank_written(dve, (L, "p", j - 3))
                v = probs[:, b, 0:2 * nk].rearrange("p (a k) -> p a k", a=2)
                k0 = P * (1 - i)
                if kind == "mla":
                    add = causal[:, k0:SEQ].unsqueeze(1).to_broadcast([P, 2, nk])
                    scale = MQ ** -0.5
                else:
                    add = bias[:, r:8:4, k0:SEQ]
                    scale = HD ** -0.5
                key = (L, "s", j)
                bank_written(dve, key)
                V.scalar_tensor_tensor(out=v, in0=ps[:, bank(key), 0:2 * nk].rearrange("p (a k) -> p a k", a=2),
                                       scalar=scale, in1=add, op0=ALU.mult, op1=ALU.add).then_inc(bank_free[bank(key)], 1)
                bank_read(dve, key)
                V.tensor_reduce(nmax[:, b, :], v, AX.X, ALU.max, negate=True).then_inc(max_ready, 1)

            def job_scale(L, j):
                kind, i, r = JOBS[j]
                nk = P * (i + 1)
                n = len(JOBS) * L + j
                b = n % 3
                dve.wait_ge(exp_ready, 2 * n + 2)
                link(V.reciprocal(prec[:, b, :], prob_sum[:, b, :]))
                if kind != "mla":
                    g = 3 * r + (1 if kind == "sel" else 2)
                    link(V.tensor_tensor(prec[:, b, :], prec[:, b, :], ngate[:, i, g:g + 13:12], ALU.mult))
                v = probs[:, b, 0:2 * nk].rearrange("p (a k) -> p a k", a=2)
                V.tensor_tensor(v, v, bc(prec[:, b, :], nk), ALU.mult).then_inc(probs_ready, 1)

            def compressed_turned(L, i):
                for h in range(2):
                    key = (L, "pc", i, h)
                    if i > 0 and h == 0:
                        dve.wait_ge(pv_done, len(JOBS) * L + FIRST_SPARSE[i])
                    bank_written(dve, key)
                    V.tensor_copy(pcT[0:N_CMP, 4 * h:4 * h + 4, :],
                                  ps[0:N_CMP, bank(key), :].rearrange("p (h q) -> p h q", h=4)).then_inc(bank_free[bank(key)], 1)

            def ffn_remainders(chunks, q0, n0, tiles, widths, slot, up_bank, turn_bank, extra=None):
                T = len(tiles)

                def turned(u):
                    for t in tiles:
                        n = n0 + (u * T + t)
                        w, b = widths[u], t if T > 1 else u % 2
                        dve.wait_ge(a_hi_ready, n + 1)
                        V.tensor_tensor(a_lo[:, b, 0:w], ps[:, turn_bank(t), 0:w], a_hi[:, b, 0:w].bitcast(F32),
                                        ALU.subtract).then_inc(a_lo_ready, 1)

                def hidden(u, q):
                    dve.wait_ge(half_done, q0 + (q + 1))
                    for t in tiles:
                        g = widths[u]
                        dve.wait_ge(silu_done, n0 + (u * T + t + 1))
                        V.tensor_tensor(act[:, t, 0:g], act_g[:, t, 0:g], ps[:, up_bank(t), 0:g],
                                        ALU.mult).then_inc(act_ready, 1)

                for m, (kind, u) in enumerate(chunks):
                    rows, cols = chunk_shape(kind, widths[u])
                    src = slot(m, rows, cols).rearrange("p k w -> p (k w)")
                    w = rows * cols // 2
                    for half in range(2):
                        q = 2 * m + half
                        if q < SPLIT_BUFS:
                            continue
                        used = q - SPLIT_BUFS
                        before_kind, before_u = chunks[used // 2] if used >= 0 else (None, None)
                        if before_kind == "up" and used % 2 == 1:
                            hidden(before_u, used)
                        if before_kind == "gate" and used % 2 == 0 and before_u > 0:
                            turned(before_u - 1)
                        dve.wait_ge(hi_ready, q0 + (q + 1))
                        V.tensor_tensor(w_lo[q % SPLIT_BUFS][:, 0:w], src[:, w * half:w * half + w],
                                        w_hi[q % SPLIT_BUFS][:, 0:w].bitcast(F32), ALU.subtract).then_inc(lo_ready, 1)
                        if extra and q == 12:
                            extra()
                hidden(len(widths) - 1, 2 * len(chunks) - SPLIT_BUFS)
                turned(len(widths) - 1)

            mixers(0)
            dve.wait_ge(h_lo_ready, 4)
            ffn_remainders(DENSE_CHUNKS, 0, 0, range(NT), [w for _, w in DENSE_GROUPS],
                           lambda m, rows, cols: slot_view(slot_of((0, *DENSE_CHUNKS[m])), rows, cols),
                           lambda t: 2 + t, lambda t: 2 + t)
            dve.wait_ge(half_done, DENSE_HALVES)
            for t in range(NT):
                for h in range(2):
                    v = x[:, t, 512 * h:512 * h + 512]
                    ins = V.tensor_tensor(v, v, ps[:, 4 + 2 * t + h, :], ALU.add)
                ins.then_inc(x_dense, 1)
            mixers(1)

            dve.wait_ge(route_pe, 1)
            dve.wait_ge(consts_ready, 2)
            logits, top, w_top, oh0, oh1, sel = (route[:, n] for n in range(6))
            slot1 = route[:, 6]
            link(V.tensor_copy(logits, ps[:, 5, 0:16].rearrange("p (t e) -> p t e", t=NT)))
            for t in range(NT):
                link(V.max(top[:, t, :], logits[:, t, :]))
                link(V.max_index(top_i[:, t, :], top[:, t, :], logits[:, t, :]))
            top_f = route[:, 7]
            link(V.tensor_copy(top_f, top_i[:, :, :]))
            V.tensor_tensor(w_top[:, :, 0:1], top[:, :, 1:2], top[:, :, 0:1], ALU.subtract).then_inc(route_dve, 1)
            dve.wait_ge(route_exp, 1)
            link(V.tensor_scalar(w_top[:, :, 2:3], w_top[:, :, 1:2], 1.0, None, ALU.add))
            link(V.reciprocal(w_top[:, :, 3:4], w_top[:, :, 2:3]))
            link(V.tensor_tensor(w_top[:, :, 4:5], w_top[:, :, 1:2], w_top[:, :, 3:4], ALU.mult))
            for t in range(NT):
                V.tensor_scalar(oh0[:, t, :], iota8, top_f[:, t, 0:1], None, ALU.is_equal)
                link(V.tensor_scalar(oh1[:, t, :], iota8, top_f[:, t, 1:2], None, ALU.is_equal))
                link(V.tensor_scalar(comb[:, t, 0:8], oh1[:, t, :], w_top[:, t, 4:5], None, ALU.mult))
                link(V.scalar_tensor_tensor(out=comb[:, t, 0:8], in0=oh0[:, t, :], scalar=w_top[:, t, 3:4],
                                            in1=comb[:, t, 0:8], op0=ALU.mult, op1=ALU.add))
            V.tensor_copy(comb[:, :, 8:16], comb[:, :, 0:8])
            V.memset(comb[:, :, 16:17], 0.0)
            V.tensor_tensor(sel, oh0, oh1, ALU.add).then_inc(route_dve, 1)
            dve.wait_ge(route_pe, 2)
            link(V.scalar_tensor_tensor(out=slot1, in0=ps[:, 1, 0:16].rearrange("p (t e) -> p t e", t=NT), scalar=1.0,
                                        in1=sel, op0=ALU.add, op1=ALU.mult))
            link(V.tensor_scalar(slots[:, :, 0:8], slot1, -1.0, None, ALU.add))
            V.tensor_scalar(slots[:, :, 8:16], slot1, -1.0 - P, None, ALU.add)
            V.memset(slots[:, :, 16:17], -1.0)

            def pick_tokens(it, first=False):
                if not first:
                    dve.wait_ge(gathered, it * 2)
                    dve.wait_ge(put_turned, it)
                V.tensor_copy(now[:, 0:2], slots[:, :, bass.ds(it, 1)].rearrange("p t o -> p (t o)"))
                V.tensor_copy(now[:, 2:4], comb[:, :, bass.ds(it, 1)].rearrange("p t o -> p (t o)")).then_inc(now_ready, 1)
                dve.wait_ge(now_ready, it + 1)
                for t in range(NT):
                    V.tensor_scalar(pick[:, t, :], iota, now[:, t:t + 1], None, ALU.is_equal)
                    ins = V.tensor_scalar(put[:, t, :], iota, now[:, t:t + 1], now[:, 2 + t:3 + t], ALU.is_equal, ALU.mult)
                ins.then_inc(pick_ready, 1)

            ffn_gain = G_FFN + KD * (DEPTH - 1)

            def gathered_out(it):
                for h in range(2):
                    dve.wait_ge(gathered, it * 2 + (h + 1))
                    V.tensor_tensor(gathered_f[h].rearrange("p (j s) -> p j s", j=4),
                                    ps[:, 6 + h, :].rearrange("p (j s) -> p j s", j=4),
                                    bc(gains[:, ffn_gain + 4 * h:ffn_gain + 4 * h + 4], P), ALU.mult).then_inc(gains_applied, 1)
                for h in range(2):
                    dve.wait_ge(e_hi_ready, it * 2 + (h + 1))
                    V.tensor_tensor(e_lo[:, 4 * h:4 * h + 4, :], gathered_f[h].rearrange("p (j s) -> p j s", j=4),
                                    e_hi[:, 4 * h:4 * h + 4, :].bitcast(F32), ALU.subtract).then_inc(e_lo_ready, 1)

            pick_tokens(0, True)
            link(V.tensor_reduce(flag[:, 0:1], ps[:, 1, 16:24], AX.X, ALU.max))
            link(V.tensor_scalar(flag[:, 1:2], flag[:, 0:1], P + 0.5, None, ALU.is_gt))
            V.tensor_copy(flag_i[:, :], flag[:, 1:2]).then_inc(routed, 1)
            gathered_out(0)
            dve.sem_inc(added, 1)

            def add_spread(it):
                for k in range(4):
                    t, h = k // 2, k % 2
                    dve.wait_ge(spread, it * 4 + (k + 2))
                    dve.wait_ge(added, it * 4 + (k + 1))
                    v = x[:, t, 512 * h:512 * h + 512]
                    V.tensor_tensor(v, v, ps[:, SPREAD_BANKS[k], :], ALU.add).then_inc(added, 1)

            def next_remainder(pair, o, q):
                dve.wait_ge(hi_ready, (pair * PAIR + o + 1) * EXPERT_HALVES + (DENSE_HALVES + q + 1))
                src, w = expert_half((o + 1) * len(EXPERT_CHUNKS) + q // 2, q)
                V.tensor_tensor(w_lo[q][:, 0:w], src, w_hi[q][:, 0:w].bitcast(F32), ALU.subtract).then_inc(lo_ready, 1)

            def expert(pair, o, last=False):
                it = pair * PAIR + o
                c0 = o * len(EXPERT_CHUNKS)
                ffn_remainders(EXPERT_CHUNKS, it * EXPERT_HALVES + DENSE_HALVES,
                               it * EXPERT_UNITS + NT * len(DENSE_GROUPS), (0,), [512] * EXPERT_UNITS,
                               lambda m, rows, cols: expert_slot(c0 + m, rows, cols), lambda t: 3, lambda t: 0,
                               extra=lambda: pick_tokens(it + 1))
                gathered_out(it + 1)
                if not last:
                    next_remainder(pair, o, 0)
                dve.wait_ge(half_done, (it + 1) * EXPERT_HALVES + DENSE_HALVES)
                dve.wait_ge(spread, it * 4 + 1)
                V.tensor_copy(ye[:, 512:1024], ps[:, 5, :]).then_inc(ye_copied, 1)
                if not last:
                    next_remainder(pair, o, 1)
                    next_remainder(pair, o, 2)
                add_spread(it)

            def experts(first_pair):
                with dve.Fori(first_pair, first_pair + PAIRS - 1) as pair:
                    for o in range(PAIR):
                        expert(pair, o)
                for o in range(PAIR):
                    expert(first_pair + PAIRS - 1, o, last=(o == PAIR - 1))

            experts(0)
            dve.wait_ge(routed, 1)
            crowded = dve.value_load(flag_i[0:1, 0:1], min_val=0, max_val=1)
            with dve.If(crowded > 0):
                for q in range(SPLIT_BUFS):
                    next_remainder(PAIRS - 1, PAIR - 1, q)
                experts(PAIRS)
            V.tensor_copy(now[:, 0:1], flag[:, 0:1]).then_inc(x_final, 1)

        @block.tensor
        def _(pe):
            mm, turn = nc.tensor.matmul, nc.tensor.transpose

            def done(ins, key):
                ins.then_inc(bank_full[bank(key)], 1)

            pe.wait_ge(consts_ready, 1)
            pe.wait_ge(gains_in, GAINS_IN)
            turn(ps[:, 6, 0:P], gain_rows, ident[:, :]).then_inc(setup_pe, 1)

            def setup_small():
                pe.wait_ge(small_in, SMALL_IN)
                turn(ps[:, 6, P:P + 64], pos_rows, ident[0:64, 0:64]).then_inc(setup_pe, 1)
                mm(ps[0:8, 7, :], table[0:33, 0:8], onehot, start=True, stop=True).then_inc(setup_pe, 1)

            def turn_residual(key, t, h):
                bank_taken_over(pe, key)
                for j in range(4):
                    ins = turn(ps[:, bank(key), P * j:P * j + P], xn[:, t, P * (4 * h + j):P * (4 * h + j + 1)], ident[:, :])
                done(ins, key)

            def turned_norm(L, which, tiles=range(NT)):
                N = 2 * L + (which == "norm2")
                for t in tiles:
                    pe.wait_ge(xn_ready, NT * N + t + 1)
                    for h in range(2):
                        turn_residual((L, which, t, h), t, h)

            def project(L, c, t, ks=range(KD)):
                c0, w = CHUNKS[c]
                key = (L, "proj", c, t)
                if ks[0] == 0:
                    bank_taken_over(pe, key)
                    weights_landed(pe, (L, "in", c))
                wv = slot_view(slot_of((L, "in", c)), KD, w)
                b = ps[:, bank(key), 0:w]
                for k in ks:
                    mm(b, hT[:, k, P * t:P * t + P], wv[:, k, :], start=(k == 0), stop=False)
                if ks[-1] == KD - 1:
                    done(add_gate_bias(L, c, b), key)

            def add_gate_bias(L, c, b):
                row = 6 * L + c - N_MIX_CHUNKS
                return mm(b, gate_row[:, row:row + 1].to_broadcast([BGATE_LO + 12, P]), bgate[:, :], start=False, stop=True)

            def project_split(L, c):
                w = CHUNKS[c][1]
                rows = KD // 2
                keys = [(L, "proj", c, t) for t in range(NT)]
                gate = c >= N_MIX_CHUNKS
                if c == N_MIX_CHUNKS:
                    pe.wait_ge(bgate_ready, 1)
                for half in range(2):
                    j = 2 * c + half
                    wh, wl = (v[j % 2][:, 0:rows * w].rearrange("p (k w) -> p k w", k=rows) for v in (in_hi, in_lo))
                    pe.wait_ge(in_hi_ready, L * IN_HALVES + j + 1)
                    for t in range(NT):
                        if half == 0:
                            bank_taken_over(pe, keys[t])
                        if c == 0:
                            pe.wait_ge(n_lo_ready, 4 * L + 2 * t + half + 1)
                        for k in range(rows):
                            for n, part in enumerate((n_hi, n_lo)):
                                mm(ps[:, bank(keys[t]), 0:w], part[:, rows * half + k, P * t:P * t + P], wh[:, k, :],
                                   start=(half == 0 and k == 0 and n == 0), stop=False)
                    pe.wait_ge(in_lo_ready, L * IN_HALVES + j + 1)
                    for t in range(NT):
                        b = ps[:, bank(keys[t]), 0:w]
                        for k in range(rows):
                            last = half == 1 and k == rows - 1 and not gate
                            ins = mm(b, n_hi[:, rows * half + k, P * t:P * t + P], wl[:, k, :], start=False, stop=last)
                        if half == 1:
                            done(add_gate_bias(L, c, b) if gate else ins, keys[t])
                    if half == 0:
                        ins.then_inc(in_used, 1)

            def turn_mixer_inputs(L, t):
                pe.wait_ge(heads_normed, NT * L + t + 1)
                p = proj[:, t, :]
                pairs = [xn[:, t, P * r:P * r + P] for r in range(4)]
                sources = [[p[:, c0:c0 + P] for c0 in (SBQ, SBQ + P, SBK, SBK + P)], pairs,
                           [p[:, c0:c0 + P] for c0 in (KS, KW, KC, VC)],
                           [p[:, c0:c0 + P] for c0 in (CQ, CQ + P, CKV)]]
                for b, group in enumerate(sources):
                    key = (L, "xt", t, b)
                    bank_taken_over(pe, key)
                    for j, src in enumerate(group):
                        ins = turn(ps[:, bank(key), P * j:P * j + P], src, ident[:, :])
                    done(ins, key)

            def latent_up(L, t):
                small = slot_view(slot_of((L, "small")), 1, 1536)[:, 0, :]
                bank_read(pe, (L, "xt", t, 3))
                weights_landed(pe, (L, "small"))
                key = (L, "uq", t)
                bank_taken_over(pe, key)
                for k in range(2):
                    ins = mm(ps[:, bank(key), 0:384], xT[:, 10 + k, P * t:P * t + P], small[:, 384 * k:384 * k + 384],
                             start=(k == 0), stop=(k == 1))
                done(ins, key)
                key = (L, "ukv", t)
                bank_taken_over(pe, key)
                done(mm(ps[:, bank(key), :], xT[:, 12, P * t:P * t + P], small[:, 768:1280], start=True, stop=True), key)

            def compress_hidden(L):
                key = (L, "c1")
                bank_taken_over(pe, key)
                for t in range(NT):
                    bank_read(pe, (L, "xt", t, 2))
                for kv in range(2):
                    weights_landed(pe, (L, "w1", kv))
                    w1 = slot_view(slot_of((L, "w1", kv)), 16, 256)
                    for c in range(16):
                        ins = mm(ps[0:CMP_ROWS, bank(key), 256 * kv:256 * kv + 256], cmp_tokens[:, kv, c:c + 8 * (CMP_ROWS - 1) + 1:8],
                                 w1[:, c, :], start=(c == 0), stop=(c == 15))
                done(ins, key)

            def compress_turn(L):
                bank_read(pe, (L, "c1"))
                key = (L, "c1t")
                bank_taken_over(pe, key)
                for f in range(4):
                    ins = turn(ps[:, bank(key), 48 * f:48 * f + CMP_ROWS], c1_rows[:, P * f:P * f + P],
                               ident[0:CMP_ROWS, 0:CMP_ROWS])
                done(ins, key)

            def compress_out(L):
                key = (L, "c2")
                small = slot_view(slot_of((L, "small")), 1, 1536)[:, 0, :]
                bank_taken_over(pe, key)
                pe.wait_ge(ch_act, L + 1)
                for kv in range(2):
                    for g in range(2):
                        o = (2 * kv + g) * HD
                        for hc in range(2):
                            w = 1280 + P * kv + HD * hc
                            ins = mm(ps[0:N_CMP, bank(key), o:o + HD], ch[:, 2 * kv + hc, N_CMP * g:N_CMP * g + N_CMP],
                                     small[:, w:w + HD], start=(hc == 0), stop=(hc == 1))
                done(ins, key)

            def job_scores(L, j):
                kind, i, r = JOBS[j]
                nk = P * (i + 1)
                key = (L, "s", j)
                bank_taken_over(pe, key)
                for h in range(2):
                    o = ps[:, bank(key), h * nk:h * nk + nk]
                    if kind == "mla":
                        ins = mm(o, mT[0:MQ, 2 * r + h, P * i:P * i + P], mT[0:MQ, 4 + 2 * r + h, 0:nk], start=True, stop=True)
                    else:
                        row = (8 if kind == "sel" else 9) + 2 * h
                        ins = mm(o, xT[:, 4 + r, P * i:P * i + P], xT[:, row, 0:nk], start=True, stop=True)
                done(ins, key)

            def job_turn(L, j):
                kind, i, r = JOBS[j]
                nk = P * (i + 1)
                n = len(JOBS) * L + j
                key = (L, "p", j)
                bank_taken_over(pe, key)
                pe.wait_ge(probs_ready, n + 1)
                for c in range(2 * (i + 1)):
                    ins = turn(ps[:, bank(key), P * c:P * c + P], probs[:, n % 3, P * c:P * c + P], ident[:, :])
                done(ins, key)

            def compressed_turn(L, i):
                pe.wait_ge(cmp_p, NT * L + i + 1)
                for half in range(2):
                    key = (L, "pc", i, half)
                    bank_taken_over(pe, key)
                    for h in range(4):
                        ins = turn(ps[0:N_CMP, bank(key), P * h:P * h + P], pcs[:, i, 4 * half + h, 0:N_CMP], ident[:, :])
                    done(ins, key)

            def job_value(L, j):
                kind, i, r = JOBS[j]
                n = len(JOBS) * L + j
                key = (L, "mlao", i, r) if kind == "mla" else (L, "nsao", i, r)
                if kind != "win":
                    bank_taken_over(pe, key)
                bank_read(pe, (L, "p", j))
                if kind == "win" and r == 0:
                    for h in range(2):
                        bank_read(pe, (L, "pc", i, h))
                for h in range(2):
                    o = ps[64 * h:64 * h + 64, bank(key), 0:P]
                    for kc in range(i + 1):
                        if kind == "mla":
                            v = mv[:, kc, 2 * r + h, :]
                        else:
                            v0 = (VS if kind == "sel" else VW) + HD * h
                            v = proj[:, kc, v0:v0 + HD]
                        c = h * (i + 1) + kc
                        ins = mm(o, v, probsT[:, n % 2, P * c:P * c + P], start=(kind != "win" and kc == 0),
                                 stop=(kind == "mla" and kc == i))
                    if kind == "win":
                        ins = mm(o, ckv_c[0:N_CMP, 2 + h, :], pcT[0:N_CMP, 4 * h + r, :], start=False, stop=True)
                ins.then_inc(pv_done, 1)

            def route_logits(t):
                for h in range(2):
                    bank_read(pe, (DEPTH - 1, "norm2", t, h))
                for k in range(KD):
                    ins = mm(ps[:, 5, 8 * t:8 * t + 8], hT[:, k, P * t:P * t + P], router[:, k, :],
                             start=(k == 0), stop=(k == KD - 1))
                return ins

            def mixers(L):
                turned_norm(L, "norm1")
                for c in range(SPLIT_CHUNKS - 1):
                    project_split(L, c)
                    if L == 0 and c == 0:
                        setup_small()
                turn_mixer_inputs(L, 0)
                project_split(L, SPLIT_CHUNKS - 1)
                turn_mixer_inputs(L, 1)
                for t in range(NT):
                    latent_up(L, t)
                compress_hidden(L)
                for t in range(NT):
                    bank_read(pe, (L, "xt", t, 0))
                for h in range(4):
                    if h == 2:
                        compress_turn(L)
                    key = (L, "z", h)
                    bank_taken_over(pe, key)
                    r = slice(64 * (h % 2), 64 * (h % 2) + 64)
                    mm(ps[:, bank(key), 0:SEQ], xT[r, 2 + h // 2, 0:P], xT[r, h // 2, :], start=True, stop=True)
                    done(mm(ps[:, bank(key), SEQ:SEQ + P], xT[r, 2 + h // 2, P:SEQ], xT[r, h // 2, P:SEQ],
                            start=True, stop=True), key)
                for t in range(NT):
                    project(L, 7, t)
                compress_out(L)
                key = (L, "kct")
                bank_taken_over(pe, key)
                pe.wait_ge(ck_ready, L + 1)
                done(turn(ps[:, bank(key), 0:N_CMP], ckv_c[0:N_CMP, 0:2, :].rearrange("p g d -> p (g d)"),
                          ident[0:N_CMP, 0:N_CMP]), key)
                for t in range(NT):
                    pe.wait_ge(mla_ready, NT * L + t + 1)
                    for b in range(2):
                        key = (L, "mt", t, b)
                        bank_taken_over(pe, key)
                        for j in range(4):
                            ins = turn(ps[0:MQ, bank(key), P * j:P * j + P], mqk[:, t, 4 * b + j, :], ident[:, :])
                        done(ins, key)
                pe.wait_ge(stick_sp, L + 1)
                for h in range(4):
                    key = (L, "S", h)
                    bank_taken_over(pe, key)
                    b = ps[:, bank(key), :]
                    mm(b[:, 0:SEQ], tri_ge[:, :], stick_tmp[:, h, 0:SEQ], start=True, stop=False)
                    mm(b[:, P:SEQ], ones[:, :], stick_tmp[:, h, SEQ:SEQ + P], start=False, stop=True)
                    done(mm(b[:, SEQ:SEQ + P], tri_ge[:, :], stick_tmp[:, h, SEQ:SEQ + P], start=True, stop=True), key)
                if L == 0:
                    pe.wait_ge(bias_in, 16)
                    for h in range(8):
                        key = (0, "flip", h)
                        bank_taken_over(pe, key)
                        done(mm(ps[:, bank(key), 0:384], flip[:, :], bias[:, h, :], start=True, stop=True), key)
                bank_read(pe, (L, "kct"))
                pe.wait_ge(keys_split, L + 1)
                for i in range(NT):
                    key = (L, "sc", i)
                    bank_taken_over(pe, key)
                    for h in range(8):
                        g, r = h // 4, h % 4
                        ins = mm(ps[:, bank(key), 16 * h:16 * h + N_CMP], xT[:, 4 + r, P * i:P * i + P],
                                 kcT[:, g, 0:N_CMP], start=True, stop=True)
                    done(ins, key)
                pe.wait_ge(stick_w, L + 1)
                for hp in range(2):
                    key = (L, "sbo", hp)
                    bank_taken_over(pe, key)
                    for a_ in range(2):
                        h = 2 * hp + a_
                        o = ps[64 * a_:64 * a_ + 64, bank(key), :]
                        v0 = SBV + HD * h
                        mm(o[:, 0:SEQ], proj[:, 0, v0:v0 + HD], stick[:, h, 0:SEQ], start=True, stop=False)
                        ins = mm(o[:, P:SEQ], proj[:, 1, v0:v0 + HD], stick[:, h, SEQ:SEQ + P], start=False, stop=True)
                    ins.then_inc(stick_out, 1)
                for t in range(NT):
                    for b in range(2):
                        bank_read(pe, (L, "mt", t, b))
                for s in range(STEPS):
                    late = LATE_PRODUCTS[s]
                    if s < len(JOBS):
                        job_scores(L, s)
                    for unit, k in late[:1]:
                        project(L, *unit, (k,))
                    if 0 <= s - LAG_PV < len(JOBS):
                        job_value(L, s - LAG_PV)
                    for unit, k in late[1:]:
                        project(L, *unit, (k,))
                    j = s - LAG_TURN
                    if 0 <= j < len(JOBS):
                        for i in range(NT):
                            if j == FIRST_SPARSE[i]:
                                compressed_turn(L, i)
                        job_turn(L, j)
                for r in (2, 3):
                    bank_read(pe, (L, "nsao", NT - 1, r))
                for k in range(2):
                    weights_landed(pe, (L, "wo", k))
                wo = [slot_view(slot_of((L, "wo", k)), 4, D) for k in range(2)]
                for t in range(NT):
                    for h in range(2):
                        for m, ks in enumerate(((0, 1), (2, 3, 4, 5), (6, 7))):
                            key = (L, "y", t, h, m)
                            bank_taken_over(pe, key)
                            for k in ks:
                                ins = mm(ps[:, bank(key), :], yT[:, k, P * t:P * t + P],
                                         wo[k // 4][:, k % 4, 512 * h:512 * h + 512], start=(k == ks[0]), stop=(k == ks[-1]))
                            done(ins, key)
                for t in range(NT):
                    for h in range(2):
                        pe.wait_ge(merged, 4 * L + 2 * t + h + 1)
                        turn_residual((L, "merge", t, h), t, h)
                for k in range(2):
                    weights_landed(pe, (L, "wout", k))
                wout = [slot_view(slot_of((L, "wout", k)), 4, D) for k in range(2)]
                for t in range(NT):
                    for h in range(2):
                        bank_read(pe, (L, "merge", t, h))
                    for h in range(2):
                        key = (L, "out", t, h)
                        bank_taken_over(pe, key)
                        for k in range(KD):
                            ins = mm(ps[:, bank(key), :], hT[:, k, P * t:P * t + P],
                                     wout[k // 4][:, k % 4, 512 * h:512 * h + 512], start=(k == 0), stop=(k == KD - 1))
                        done(ins, key)
                        if (t, h) == (1, 0):
                            turned_norm(L, "norm2", (0,))
                if L == DEPTH - 1:
                    route_logits(0)
                turned_norm(L, "norm2", (1,))

            def ffn(chunks, q0, n0, tiles, widths, hi, lo, gate_bank, up_bank, turn_bank, y_bank, before_last=None,
                    before_last_down=None, y_free=None, extra=None):
                T = len(tiles)

                def products(q, kind, u, half):
                    rows, cols = chunk_shape(kind, widths[u])
                    rows //= 2
                    wh, wl = (v[q % SPLIT_BUFS][:, 0:rows * cols].rearrange("p (k w) -> p k w", k=rows) for v in (w_hi, w_lo))
                    first = half == 0 and (kind != "down" or u == 0)
                    last = half == 1 and (kind != "down" or u == len(widths) - 1)

                    def sweep(weights, which, opening, closing):
                        for t in tiles:
                            for k in range(rows):
                                kk = half * rows + k
                                for n, part in enumerate(which):
                                    if kind == "down":
                                        b = t if T > 1 else u % 2
                                        lhs = (a_hi, a_lo)[part][:, b, P * kk:P * kk + P]
                                    else:
                                        lhs = (hi, lo)[part](kk, t)
                                    for h in range(2 if kind == "down" else 1):
                                        if kind == "down":
                                            out_, rhs = ps[:, y_bank(t) + h, :], weights[:, k, 512 * h:512 * h + 512]
                                        else:
                                            out_ = ps[:, (gate_bank if kind == "gate" else up_bank)(t), 0:cols]
                                            rhs = weights[:, k, :]
                                        ins = mm(out_, lhs, rhs, start=(opening and k == 0 and n == 0),
                                                 stop=(closing and k == rows - 1 and n == len(which) - 1))
                        return ins

                    pe.wait_ge(hi_ready, q0 + (q + 1))
                    sweep(wh, (0, 1), first, False)
                    pe.wait_ge(lo_ready, q0 + (q + 1))
                    sweep(wl, (0,), False, last).then_inc(half_done, 1)

                def turn_hidden(u):
                    for t in tiles:
                        pe.wait_ge(act_ready, n0 + (u * T + t + 1))
                        for j in range(widths[u] // P):
                            ins = turn(ps[:, turn_bank(t), P * j:P * j + P], act[:, t, P * j:P * j + P], ident[:, :])
                        ins.then_inc(act_turned, 1)

                for m, (kind, u) in enumerate(chunks):
                    if kind == "gate" and u > 0:
                        pe.wait_ge(silu_done, n0 + u * T)
                    if kind == "up" and u > 0:
                        pe.wait_ge(a_lo_ready, n0 + u * T)
                    if kind == "down":
                        if u == len(widths) - 1:
                            if before_last:
                                before_last()
                            turn_hidden(u)
                            if before_last_down:
                                before_last_down()
                        pe.wait_ge(a_lo_ready, n0 + (u + 1) * T)
                        if u == 0 and y_free:
                            y_free()
                    for half in range(2):
                        products(2 * m + half, kind, u, half)
                        if kind == "gate" and half == 0 and u > 0:
                            turn_hidden(u - 1)
                        if extra and m == 1 and half == 1:
                            extra()

            mixers(0)

            pe.wait_ge(h_hi_ready, 4)
            pe.wait_ge(h_lo_ready, 4)
            ffn(DENSE_CHUNKS, 0, 0, range(NT), [w for _, w in DENSE_GROUPS],
                lambda k, t: h_hi[:, k, P * t:P * t + P], lambda k, t: h_lo[:, k, P * t:P * t + P],
                lambda t: t, lambda t: 2 + t, lambda t: 2 + t, lambda t: 4 + 2 * t)
            mixers(1)

            route_logits(1).then_inc(route_pe, 1)
            pe.wait_ge(route_dve, 2)
            pe.wait_ge(consts_ready, 2)
            sel = route[:, 5]
            mm(ps[:, 1, 0:8], tri_lt, sel[:, 0, :], start=True, stop=True)
            mm(ps[:, 1, 8:16], ones[:, :], sel[:, 0, :], start=True, stop=False)
            mm(ps[:, 1, 8:16], tri_lt, sel[:, 1, :], start=False, stop=True)
            mm(ps[:, 1, 16:24], ones[:, :], sel[:, 0, :], start=True, stop=False)
            mm(ps[:, 1, 16:24], ones[:, :], sel[:, 1, :], start=False, stop=True).then_inc(route_pe, 1)

            def gather(it, h, first=False):
                if h == 0:
                    pe.wait_ge(pick_ready, it + 1)
                if not first:
                    pe.wait_ge(added, it * 4 - 3)
                for j in range(4):
                    k = 4 * h + j
                    for t in range(NT):
                        ins = mm(ps[:, 6 + h, P * j:P * j + P], xn[:, t, P * k:P * k + P], pick[:, t, :],
                                 start=(t == 0), stop=(t == NT - 1))
                ins.then_inc(gathered, 1)

            def turn_put(it):
                for t in range(NT):
                    ins = turn(ps[:, 1, P * t:P * t + P], put[:, t, :], ident[:, :])
                ins.then_inc(put_turned, 1)

            gather(0, 0, True)
            gather(0, 1, True)
            pe.wait_ge(routed, 1)
            pe.sem_inc(spread, 1)

            def expert(pair, o):
                it = pair * PAIR + o
                pe.wait_ge(e_lo_ready, it * 2 + 2)
                ffn(EXPERT_CHUNKS, it * EXPERT_HALVES + DENSE_HALVES, it * EXPERT_UNITS + NT * len(DENSE_GROUPS),
                    (0,), [512] * EXPERT_UNITS, lambda k, t: e_hi[:, k, :], lambda k, t: e_lo[:, k, :],
                    lambda t: 2, lambda t: 3, lambda t: 0, lambda t: 4,
                    before_last=lambda: gather(it + 1, 0), before_last_down=lambda: gather(it + 1, 1),
                    extra=lambda: turn_put(it), y_free=lambda: pe.wait_ge(added, it * 4 + 1))
                pe.wait_ge(ye_ready, it + 2)
                pe.wait_ge(ye_copied, it + 1)
                pe.wait_ge(putT_ready, it + 1)
                for k in range(4):
                    t, h = k // 2, k % 2
                    if k < 2:
                        pe.wait_ge(gains_applied, it * 2 + (3 + k))
                    mm(ps[:, SPREAD_BANKS[k], :], putT[:, P * t:P * t + P], ye[:, 512 * h:512 * h + 512],
                       start=True, stop=True).then_inc(spread, 1)

            with pe.Fori(0, PAIRS) as pair:
                for o in range(PAIR):
                    expert(pair, o)
            crowded = pe.value_load(flag_i[0:1, 0:1], min_val=0, max_val=1)
            with pe.If(crowded > 0):
                with pe.Fori(PAIRS, 2 * PAIRS) as pair:
                    for o in range(PAIR):
                        expert(pair, o)


_INS = ['x', 'rel_bias_table', 'mix_norm', 'w_in', 'b_gate', 'sb_w_o', 'nsa_q_norm', 'nsa_k_norm', 'nsa_cmp_pos',
        'nsa_cmp_w1', 'nsa_cmp_w2', 'nsa_w_o', 'mla_q_a_norm', 'mla_kv_a_norm', 'mla_w_uq', 'mla_w_ukv', 'mla_q_norm',
        'mla_k_norm', 'mla_w_o', 'w_out', 'ffn_norm', 'dense_w_gate', 'dense_w_up', 'dense_w_down', 'moe_router',
        'moe_w_gate', 'moe_w_up', 'moe_w_down']


def shape_constants():
    import math
    import numpy as np
    rel = np.arange(SEQ)
    n = np.maximum(rel, 1).astype(np.float32)
    large = 16 + (np.log(n / np.float32(16)) / np.float32(math.log(1024 / 16)) * np.float32(16)).astype(np.int32)
    bucket = np.where(rel < 16, rel, np.minimum(large, 31))
    onehot = np.zeros((33, 512), np.float32)
    for j in range(512):
        d = SEQ - 1 - j
        onehot[bucket[d] if d >= 0 else 32, j] = 1.0
    inv = np.float32(10000.0) ** (-np.arange(16, dtype=np.float32) / np.float32(16))
    ang = np.arange(SEQ, dtype=np.float32)[:, None] * inv[None, :]
    trig = np.stack([np.cos(ang), np.sin(ang)]).astype(np.float32)
    return onehot, np.ascontiguousarray(trig.reshape(2, NT, P, 16).transpose(2, 0, 1, 3))


def kernel(**inputs):
    import numpy as _np
    import concourse.bacc as _bacc
    from concourse import mybir as _mybir
    from concourse.bass_utils import run_bass_kernel_spmd as _run

    nc = _bacc.Bacc("TRN2", target_bir_lowering=False, num_devices=1)
    arrays, args = {}, {}
    onehot, trig = shape_constants()
    for name, arr in [(n, inputs[n]) for n in _INS] + [("bucket_onehot", onehot), ("rope_tables", trig)]:
        v = _np.ascontiguousarray(arr)
        arrays[f"in_{name}_dram"] = v
        args[name] = nc.dram_tensor(f"in_{name}_dram", v.shape, _mybir.dt.from_np(v.dtype), kind="ExternalInput").ap()
    out = nc.dram_tensor("out_0_dram", (1, SEQ, D), _mybir.dt.float32, kind="ExternalOutput").ap()
    trunk(nc, args, out)
    r = _run(nc, [arrays], core_ids=[0])
    return r.results[0]["out_0_dram"]
```
